# Optimizing a Trainium2 kernel written in Bass

```python
import math
import jax, jax.numpy as jnp
from jax import lax
import numpy as np

D_MODEL = 1024
BATCH = 1
SEQ = 1024
DEPTH = 2

D_MIX = D_MODEL
EPS = 1e-5
ATTN_HEADS = 4
ATTN_QK_DIM = 64
ATTN_V_DIM = 2 * ATTN_QK_DIM
ATTN_WIDTH = ATTN_HEADS * ATTN_V_DIM
Q_BLOCK = 128
ROPE_THETA = 500000.0
ROT_DIM = ATTN_QK_DIM // 4
SC_WIDTH = 256
SC_CONV = 3
SSD_HEADS = 4
SSD_HEAD_DIM = 64
SSD_WIDTH = SSD_HEADS * SSD_HEAD_DIM
SSD_GROUPS = 2
SSD_STATE = 128
SSD_HEADS_PER_GROUP = SSD_HEADS // SSD_GROUPS
SSD_CONV = 3
SSD_CHUNK = 128
SSD_XBC = SSD_WIDTH + 2 * SSD_GROUPS * SSD_STATE
D_FF = 2816
FFN_CONV = 3

Q_COLS = ATTN_HEADS * 2 * ATTN_QK_DIM
K_COLS = Q_COLS
V_COLS = ATTN_WIDTH
_SEG = [Q_COLS, K_COLS, V_COLS, SC_WIDTH, SC_WIDTH, SC_WIDTH, SSD_WIDTH, SSD_XBC, SSD_HEADS, SSD_HEADS]
SPLITS = [int(v) for v in np.cumsum(_SEG)[:-1]]
IN_COLS = int(sum(_SEG))

kernel_name = "hymba_style_bidir_diffattn_shortconv_ssd"

F32 = jnp.float32

def rms_norm(x, g):
    xf = x.astype(F32)
    y = xf * lax.rsqrt(jnp.mean(xf * xf, axis=-1, keepdims=True) + EPS)
    return (y * g.astype(F32)).astype(x.dtype)

def conv_centered(t, w, bias=None):
    K = w.shape[0]
    pad = K // 2
    S = t.shape[1]
    tp = jnp.pad(t, ((0, 0), (pad, pad), (0, 0)))
    out = tp[:, 0:S] * w[0]
    for k in range(1, K):
        out = out + tp[:, k:k + S] * w[k]
    if bias is not None:
        out = out + bias
    return out

def partial_rotary(t, cos, sin):
    half = ROT_DIM // 2
    c = cos[:, :, None, None, :].astype(t.dtype)
    s = sin[:, :, None, None, :].astype(t.dtype)
    t1 = t[..., :half]
    t2 = t[..., half:ROT_DIM]
    return jnp.concatenate([t1 * c - t2 * s, t2 * c + t1 * s, t[..., ROT_DIM:]], axis=-1)

def diff_attention(q, k, v, lam, lam_init, subln_g):
    b, S, h, _, d = q.shape
    nq = S // Q_BLOCK
    scale = d ** -0.5
    qb = q.reshape(b, nq, Q_BLOCK, h, 2, d).transpose(1, 0, 2, 3, 4, 5)

    def block(qi):
        s = jnp.einsum('bqhcd,bkhcd->bhcqk', qi, k).astype(F32) * scale
        p = jax.nn.softmax(s, axis=-1)
        w = p[:, :, 0] - lam * p[:, :, 1]
        return jnp.einsum('bhqk,bkhe->bqhe', w.astype(v.dtype), v)

    o = lax.map(block, qb)
    o = o.transpose(1, 0, 2, 3, 4).reshape(b, S, h, ATTN_V_DIM)
    o = rms_norm(o, subln_g) * (1.0 - lam_init)
    return o.reshape(b, S, h * ATTN_V_DIM)

def ssd_scan(x, dt, A, Bm, Cm):
    b, S, h, p = x.shape
    n = Bm.shape[-1]
    c = S // SSD_CHUNK
    L = SSD_CHUNK
    xd = (x * dt[..., None]).reshape(b, c, L, h, p)
    a = (dt * A).reshape(b, c, L, h).transpose(0, 3, 1, 2)
    Bc = Bm.reshape(b, c, L, h, n)
    Cc = Cm.reshape(b, c, L, h, n)
    a_cs = jnp.cumsum(a, axis=-1)
    mask = jnp.tril(jnp.ones((L, L), dtype=bool))
    seg = a_cs[..., :, None] - a_cs[..., None, :]
    Lmat = jnp.where(mask, jnp.exp(jnp.where(mask, seg, 0.0)), 0.0)
    scores = jnp.einsum('bclhn,bcshn->bhcls', Cc, Bc) * Lmat
    y_diag = jnp.einsum('bhcls,bcshp->bclhp', scores, xd)
    decay_states = jnp.exp(a_cs[..., -1:] - a_cs)
    states = jnp.einsum('bclhn,bhcl,bclhp->bchpn', Bc, decay_states, xd)
    chunk_decay = jnp.exp(a_cs[..., -1])

    def step(hstate, inp):
        st, dec = inp
        return hstate * dec[..., None, None] + st, hstate

    h0 = jnp.zeros((b, h, p, n), dtype=states.dtype)
    _, prev = lax.scan(step, h0, (states.transpose(1, 0, 2, 3, 4), chunk_decay.transpose(2, 0, 1)))
    prev = prev.transpose(1, 0, 2, 3, 4)
    y_off = jnp.einsum('bclhn,bchpn,bhcl->bclhp', Cc, prev, jnp.exp(a_cs))
    return (y_diag + y_off).reshape(b, S, h, p)

def ssd_mixer(xbc, z, dt_f, dt_b, conv_w, conv_b, dt_bias, a_log, d_skip, norm_g):
    b, S, _ = xbc.shape
    xbc = jax.nn.silu(conv_centered(xbc, conv_w, conv_b))
    xs, Bm, Cm = jnp.split(xbc, [SSD_WIDTH, SSD_WIDTH + SSD_GROUPS * SSD_STATE], axis=-1)
    xs = xs.reshape(b, S, SSD_HEADS, SSD_HEAD_DIM).astype(F32)
    Bm = jnp.repeat(Bm.reshape(b, S, SSD_GROUPS, SSD_STATE), SSD_HEADS_PER_GROUP, axis=2).astype(F32)
    Cm = jnp.repeat(Cm.reshape(b, S, SSD_GROUPS, SSD_STATE), SSD_HEADS_PER_GROUP, axis=2).astype(F32)
    A = -jnp.exp(a_log.astype(F32))
    dtb = dt_bias.astype(F32)
    dtf = jax.nn.softplus(dt_f.astype(F32) + dtb[0])
    dtr = jax.nn.softplus(dt_b.astype(F32) + dtb[1])
    flip = lambda t: jnp.flip(t, axis=1)
    y_fwd = ssd_scan(xs, dtf, A[0], Bm, Cm)
    y_bwd = flip(ssd_scan(flip(xs), flip(dtr), A[1], flip(Bm), flip(Cm)))
    y = y_fwd + y_bwd + d_skip.astype(F32)[:, None] * xs
    y = y.reshape(b, S, SSD_WIDTH) * jax.nn.silu(z.astype(F32))
    gs = SSD_WIDTH // SSD_GROUPS
    y = rms_norm(y.reshape(b, S, SSD_GROUPS, gs), norm_g.reshape(SSD_GROUPS, gs))
    return y.reshape(b, S, SSD_WIDTH).astype(z.dtype)

def setup_inputs(seed: int = 0) -> dict:
    key = jax.random.key(seed)
    ks = jax.random.split(key, 24)
    nrm = lambda k, shape, s: jax.random.normal(k, shape, dtype=F32) * s
    x = jax.random.normal(ks[0], (BATCH, SEQ, D_MODEL), dtype=F32)
    offs = jax.random.randint(ks[1], (BATCH, 1), 0, 1024, dtype=jnp.int32)
    positions = (jnp.arange(SEQ, dtype=jnp.int32)[None, :] + offs).astype(jnp.int32)
    dt0 = jnp.exp(jax.random.uniform(ks[10], (DEPTH, 2, SSD_HEADS), minval=math.log(1e-3), maxval=math.log(1e-1)))
    return {
        "x": x,
        "positions": positions,
        "norm_mix_g": 1.0 + nrm(ks[2], (DEPTH, D_MODEL), 0.02),
        "w_in": nrm(ks[3], (DEPTH, D_MODEL, IN_COLS), D_MODEL ** -0.5),
        "lam_q1": nrm(ks[4], (DEPTH, ATTN_QK_DIM), 0.1),
        "lam_k1": nrm(ks[5], (DEPTH, ATTN_QK_DIM), 0.1),
        "lam_q2": nrm(ks[6], (DEPTH, ATTN_QK_DIM), 0.1),
        "lam_k2": nrm(ks[7], (DEPTH, ATTN_QK_DIM), 0.1),
        "subln_g": 1.0 + nrm(ks[8], (DEPTH, ATTN_V_DIM), 0.02),
        "sc_conv_w": nrm(ks[9], (DEPTH, SC_CONV, SC_WIDTH), SC_CONV ** -0.5),
        "ssd_conv_w": nrm(ks[11], (DEPTH, SSD_CONV, SSD_XBC), SSD_CONV ** -0.5),
        "ssd_conv_b": nrm(ks[12], (DEPTH, SSD_XBC), 0.02),
        "ssd_dt_bias": dt0 + jnp.log(-jnp.expm1(-dt0)),
        "ssd_a_log": jnp.log(jax.random.uniform(ks[13], (DEPTH, 2, SSD_HEADS), minval=1.0, maxval=16.0)),
        "ssd_d": 1.0 + nrm(ks[14], (DEPTH, SSD_HEADS), 0.02),
        "ssd_norm_g": 1.0 + nrm(ks[15], (DEPTH, SSD_WIDTH), 0.02),
        "w_out": nrm(ks[16], (DEPTH, D_MIX, D_MODEL), D_MIX ** -0.5),
        "norm_ffn_g": 1.0 + nrm(ks[17], (DEPTH, D_MODEL), 0.02),
        "w_up": nrm(ks[18], (DEPTH, D_MODEL, 2 * D_FF), D_MODEL ** -0.5),
        "ffn_conv_w": nrm(ks[19], (DEPTH, FFN_CONV, 2 * D_FF), FFN_CONV ** -0.5),
        "ffn_conv_b": nrm(ks[20], (DEPTH, 2 * D_FF), 0.02),
        "w_down": nrm(ks[21], (DEPTH, D_FF, D_MODEL), D_FF ** -0.5),
        "final_norm_g": 1.0 + nrm(ks[22], (D_MODEL,), 0.02),
    }

def reference(x, positions, norm_mix_g, w_in, lam_q1, lam_k1, lam_q2, lam_k2, subln_g, sc_conv_w,
              ssd_conv_w, ssd_conv_b, ssd_dt_bias, ssd_a_log, ssd_d, ssd_norm_g, w_out,
              norm_ffn_g, w_up, ffn_conv_w, ffn_conv_b, w_down, final_norm_g):
    b, S, _ = x.shape
    inv_freq = ROPE_THETA ** (-jnp.arange(0, ROT_DIM, 2, dtype=F32) / ROT_DIM)
    ang = positions.astype(F32)[..., None] * inv_freq
    cos, sin = jnp.cos(ang), jnp.sin(ang)

    for l in range(DEPTH):
        lam_init = 0.8 - 0.6 * math.exp(-0.3 * l)
        h = rms_norm(x, norm_mix_g[l])
        proj = h @ w_in[l]
        q, k, v, sc_b, sc_c, sc_h, z, xbc, dt_f, dt_b = jnp.split(proj, SPLITS, axis=-1)

        q = partial_rotary(q.reshape(b, S, ATTN_HEADS, 2, ATTN_QK_DIM), cos, sin)
        k = partial_rotary(k.reshape(b, S, ATTN_HEADS, 2, ATTN_QK_DIM), cos, sin)
        v = v.reshape(b, S, ATTN_HEADS, ATTN_V_DIM)
        lam = (jnp.exp(jnp.sum(lam_q1[l].astype(F32) * lam_k1[l].astype(F32)))
               - jnp.exp(jnp.sum(lam_q2[l].astype(F32) * lam_k2[l].astype(F32))) + lam_init)
        y_attn = diff_attention(q, k, v, lam, lam_init, subln_g[l])

        y_conv = sc_b * conv_centered(sc_c * sc_h, sc_conv_w[l])

        y_ssd = ssd_mixer(xbc, z, dt_f, dt_b, ssd_conv_w[l], ssd_conv_b[l], ssd_dt_bias[l],
                          ssd_a_log[l], ssd_d[l], ssd_norm_g[l])

        y = jnp.concatenate([y_attn, y_conv.astype(y_attn.dtype), y_ssd.astype(y_attn.dtype)], axis=-1)
        x = x + (y @ w_out[l]).astype(x.dtype)

        h = rms_norm(x, norm_ffn_g[l])
        u = conv_centered(h @ w_up[l], ffn_conv_w[l], ffn_conv_b[l])
        g, u = jnp.split(u, 2, axis=-1)
        x = x + ((jax.nn.silu(g) * u) @ w_down[l]).astype(x.dtype)

    return rms_norm(x, final_norm_g)


_drawn_inputs = setup_inputs


def setup_inputs(seed=0):
    import zlib

    import numpy as np

    out = dict(_drawn_inputs(seed))
    spreads = {}
    factors = {'subln_g': 4.402,
     'ssd_conv_b': 3.117,
     'ssd_d': 7.633,
     'ssd_norm_g': 4.72,
     'norm_ffn_g': 3.275,
     'ffn_conv_b': 3.188,
     'final_norm_g': 2.827}
    for name, (base, spread) in spreads.items():
        noise = np.random.default_rng([zlib.crc32(name.encode()), seed]).standard_normal(out[name].shape)
        drawn = base * np.exp(spread * noise) if base else spread * noise
        out[name] = __import__('jax').numpy.asarray(drawn.astype(out[name].dtype))
    for name, factor in factors.items():
        out[name] = (out[name] * factor).astype(out[name].dtype)
    return out
```

```python
import math
from contextlib import ExitStack

import numpy as np

import concourse.bass as bass
from concourse import mybir

F32 = mybir.dt.float32
F32R = mybir.dt.float32r
I32 = mybir.dt.int32
ALU = mybir.AluOpType
ACT = mybir.ActivationFunctionType
AX_X = mybir.AxisListType.X

P = 128
HALF = 512
EPS = 1e-5
ROPE_THETA = 500000.0
RING = 6
RAW = 3
LOOKAHEAD = 4
TWO_PI_PARTS = (6.28125, 1.93500518798828125e-3, 3.01991598196e-7)
PI_BELOW = 3.1415925
ROUND = 12582912.0


def build(nc, x, positions, norm_mix_g, w_in, lam_q1, lam_k1, lam_q2, lam_k2, subln_g, sc_conv_w,
          ssd_conv_w, ssd_conv_b, ssd_dt_bias, ssd_a_log, ssd_d, ssd_norm_g, w_out,
          norm_ffn_g, w_up, ffn_conv_w, ffn_conv_b, w_down, final_norm_g, out):
    _, S, D = x.shape
    L = w_in.shape[0]
    KT = D // P
    TB = S // P
    DQK = lam_q1.shape[1]
    DV = subln_g.shape[1]
    HEADS = 4
    ROT = DQK // 4
    R2 = ROT // 2
    HC = 2 * HEADS
    SCW = sc_conv_w.shape[2]
    SCT = SCW // P
    SSDW = ssd_norm_g.shape[1]
    XT = SSDW // P
    XBCT = ssd_conv_w.shape[2] // P
    NH = ssd_d.shape[1]
    FF = w_down.shape[1]
    FT = FF // P
    CH = 2
    NCH = FT // CH
    assert (S, D, DQK, DV, KT, TB, SCT, XT, XBCT, NH) == (1024, 1024, 64, 128, 8, 8, 2, 2, 6, 4)
    assert FT % CH == 0

    COL_Q, COL_K, COL_V, COL_SC = 0, HC * DQK, 2 * HC * DQK, 2 * HC * DQK + HEADS * DV
    COL_Z = COL_SC + 3 * SCW
    COL_XBC = COL_Z + SSDW
    COL_DT = COL_XBC + XBCT * P
    F_TILES = ([("xbc", t, COL_XBC + t * P) for t in range(XBCT)] + [("z", t, COL_Z + t * P) for t in range(XT)]
               + [(kind, t, COL_SC + n * SCW + t * P) for t in range(SCT) for kind, n in (("c", 1), ("h", 2), ("b", 0))])
    GROUPS = [("v", COL_V), ("q", COL_Q), ("k", COL_K)]
    P_DT = 0
    P_F = 4
    P_G = P_F + 2 * len(F_TILES)
    P_OUT = P_G + KT * len(GROUPS)
    P_UP0 = P_OUT + 2 * KT
    UPN = 4 * CH
    DNN = 2 * CH
    P_BODY = P_UP0 + UPN
    P_DN = P_BODY + (NCH - 1) * (UPN + DNN)
    PANELS = P_DN + DNN
    assert PANELS % RING == 0 and PANELS % RAW == 0 and (UPN + DNN) % RING == 0

    C_FW = [k * 2 * FT for k in range(3)]
    C_FB = 6 * FT
    C_G1 = 8 * FT
    C_G2 = C_G1 + KT
    C_XW = C_G2 + KT
    C_XB = C_XW + 3 * XBCT
    C_SW = C_XB + XBCT
    C_NG = C_SW + 3 * SCT
    C_SUB = C_NG + XT
    C_LAM = C_SUB + 1
    C_A = C_LAM + 1
    C_DTB = C_A + 2 * NH
    C_D = C_DTB + 2 * NH
    NPRM = C_D + XT
    INV_FREQ = [float(np.float32(ROPE_THETA) ** np.float32(-2.0 * j / ROT)) for j in range(R2)]
    LAM_INIT = [0.8 - 0.6 * math.exp(-0.3 * l) for l in range(L)]

    with ExitStack() as ctx:
        def sb(name, shape, dt=F32):
            return ctx.enter_context(nc.sbuf_tensor(name, shape, dt))

        def sem(name):
            return ctx.enter_context(nc.semaphore(name))

        xT = sb("xT", [P, KT, S])
        base_h = (nc.sbuf_base + 63) // 64 * 64
        slab_h = sb("slab_h", [P, base_h - nc.sbuf_base + 2 * KT * S * 4], mybir.dt.uint8)
        raw = [sb(f"raw{i}", [P, HALF]) for i in range(RAW)]
        whi = [sb(f"whi{i}", [P, HALF], F32R) for i in range(RING)]
        wlo = [sb(f"wlo{i}", [P, HALF], F32R) for i in range(RING)]
        ident = sb("ident", [P, P])
        identr = sb("identr", [P, P], F32R)
        ones = sb("ones", [P, P])
        upto = sb("upto", [P, P])
        downto = sb("downto", [P, P])
        capf = sb("capf", [P, P])
        capb = sb("capb", [P, P])
        prm = sb("prm", [P, L, NPRM])
        pc = sb("pc", [P, NPRM])
        cosT = sb("cosT", [P, TB, R2])
        sinT = sb("sinT", [P, TB, R2])
        small = sb("small", [P, 64])
        minus_half = sb("minus_half", [P, 32])
        rstd = sb("rstd", [P, 32])
        nmax = sb("nmax", [P, 2, 2])
        lsum = sb("lsum", [P, 2, 2])
        rlsum = sb("rlsum", [P, 2, 2])
        mix = sb("mix", [P, 2])
        ssq = sb("ssq", [P, HEADS * TB])

        base_a = (nc.sbuf_base + 63) // 64 * 64
        KB = 1024

        def region(base, limit):
            def at(name, offset, shape, dt=F32):
                n = 4
                for s in shape[1:]:
                    n *= s
                assert offset + n <= limit, name
                return nc.alloc_sbuf_tensor_at(name, shape, dt, offset=base + offset)
            return at

        h_at = region(base_h, 2 * KT * S * 4)
        a_at = region(base_a, 74 * KB)
        slab_a = sb("slab_a", [P, base_a - nc.sbuf_base + 74 * KB], mybir.dt.uint8)

        ahi = h_at("ahi", 0, [P, KT, S], F32R)
        alo = h_at("alo", 32 * KB, [P, KT, S], F32R)
        xin = h_at("xin", 0, [P, TB, D])
        kst = h_at("kst", 32 * KB, [P, HC, S], F32R)
        E = h_at("E", 0, [P, 2, 2, S])
        WT = [h_at(f"WT{i}", (20 + 4 * i) * KB, [P, TB, P]) for i in range(2)]
        q_tok = a_at("q_tok", 0, [P, TB, HEADS * DV])
        v_tok = a_at("v_tok", 16 * KB, [P, TB, HEADS * DV])
        o_tok = q_tok
        yc = a_at("yc", 48 * KB, [P, SCT, S])
        ys = a_at("ys", 56 * KB, [P, XT, S])
        ksp = [a_at(f"ksp{i}", (64 + 4 * i) * KB, [P, HC, 2, DQK], F32R) for i in range(2)]
        k_tok = a_at("k_tok", 32 * KB, [P, TB, HC * DQK])
        qsp = [a_at(f"qsp{i}", (32 + 2 * i) * KB, [P, 2, 2, 2, DQK], F32R) for i in range(2)]
        qT = [a_at(f"qT{i}", (36 + 2 * i) * KB, [P, 2, 2, P], F32R) for i in range(2)]
        W = [a_at(f"W{i}", (40 + 4 * i) * KB, [P, S]) for i in range(2)]
        yn = h_at("yn", 0, [P, HEADS, TB, P])
        xbc = a_at("xbc", 0, [P, XBCT, S])
        st = a_at("st", 24 * KB, [P, TB, XT, 2, P])
        cv = [a_at(f"cv{i}", (40 + 4 * i) * KB, [P, S]) for i in range(2)]
        seg = a_at("seg", 40 * KB, [P, 2, NH, P])
        erow = a_at("erow", 44 * KB, [P, 2, NH, P])
        xb_tok = [a_at(f"xb_tok{i}", (64 + 2 * i) * KB, [P, 4 * P]) for i in range(2)]
        xw = [a_at(f"xw{i}", (68 + 2 * i) * KB, [P, 2, NH, DQK]) for i in range(2)]
        dtT = a_at("dtT", 24 * KB, [8, S])
        rot = a_at("rot", 72 * KB, [P, 4, HC, R2])
        osq = a_at("osq", 64 * KB, [P, P])
        DW = TB * 2 * NH
        dtb_ = [a_at(f"dt{i}", 72 * KB + i * 4 * DW, [P, TB, 2 * NH]) for i in range(8)]
        DT_EXP, DT, DT_W, DT_DEC, DT_A, DT_CUM = (dtb_[i] for i in (2, 7, 0, 1, 4, 5))
        sqs = a_at("sqs", 40 * KB, [P, XT, S])
        acc = a_at("acc", 64 * KB, [P, S])
        sq = a_at("sq", 68 * KB, [P, S])
        ht = [a_at(f"ht{i}", (52 + 8 * i) * KB, [P, S]) for i in range(2)]
        mhi = a_at("mhi", 0, [P, CH, S], F32R)
        mlo = a_at("mlo", 8 * KB, [P, CH, S], F32R)
        tg = [a_at(f"tg{i}", (32 + 4 * i) * KB, [P, S]) for i in range(2)]
        tu = [a_at(f"tu{i}", (40 + 4 * i) * KB, [P, S]) for i in range(2)]
        stage = [[a_at(f"stage{l}{i}", (3 * l + i) * 512, [P, P]) for i in range(3)] for l in range(L)]
        lamv = a_at("lamv", 4 * KB, [P, 4, L, DQK])
        lamp = a_at("lamp", 8 * KB, [P, 2, L, DQK])
        lams = a_at("lams", 10 * KB, [P, 2, L])
        pos_i = a_at("pos_i", 11 * KB, [TB, P], I32)
        pos_f = a_at("pos_f", 11 * KB + 512, [TB, P])
        pos_c = a_at("pos_c", 12 * KB, [P, TB])
        ang = [a_at(f"ang{i}", 13 * KB + 256 * i, [P, TB, R2]) for i in range(3)]
        fg_row = a_at("fg_row", 16 * KB, [P, D])
        o_row = [a_at(f"o_row{i}", (20 + 4 * i) * KB, [P, D]) for i in range(2)]

        ps = ctx.enter_context(nc.psum_tensor("ps", [P, 8, HALF], F32))

        def pair(u):
            k = u % 4
            return ps[:, 2 * k:2 * k + 2, :].rearrange("p b n -> p (b n)")

        def pair(k):
            return ps[:, 2 * k:2 * k + 2, :].rearrange("p b n -> p (b n)")

        def half(k, h):
            return ps[:, 2 * k + h, :]

        class Count:

            def __init__(self, name, n, credit=0):
                self.sem, self.n, self.credit = ctx.enter_context(nc.semaphore(name)), n, credit

            def until(self, l, k):
                return l * self.n + k + self.credit

        s_raw = [sem(f"raw_loaded{i}") for i in range(RAW)]
        s_split = Count("panels_split", PANELS, RAW)
        s_hi = Count("panels_hi", PANELS)
        s_panel = Count("panels_used", PANELS, RING)

        s_setup = sem("setup_loaded")
        s_xin = sem("x_loaded")
        s_fg = sem("final_gain_loaded")
        s_const = sem("constants_made")
        s_pset = sem("setup_pe")
        s_aset = sem("setup_act")
        s_dset = sem("setup_dve")
        s_xt0 = sem("x_feature_major_pe")
        s_xt1 = sem("x_feature_major_stored")
        s_fin = sem("final_transposed")
        s_row = sem("final_row_ready")
        s_dlink = sem("setup_dve_steps")
        s_out = [sem(f"rows_stored{i}") for i in range(2)]

        s_sq = Count("squares_written", 2 * KT)
        s_acc = Count("squares_added", 2 * KT)
        s_nsum = Count("square_sums_ready", 2)
        s_ms = Count("mean_squares_ready", 2)
        s_rs = Count("rstd_ready", 2)
        s_dg = Count("rstd_diagonals_ready", 2)
        s_nb = Count("rstd_broadcast_ready", 2)
        s_ht = Count("normed_ready", 2 * KT)
        s_hh = Count("normed_hi_ready", 2 * KT)
        s_hl = Count("normed_lo_ready", 2 * KT)
        s_pc = Count("layer_parameters_ready", 1)

        s_c1 = Count("conv_centre_done", XBCT)
        s_c2 = Count("conv_left_done", XBCT)
        s_c3 = Count("conv_done", XBCT)
        s_xs = Count("xbc_ready", XBCT)
        s_z = Count("z_gate_ready", XT)
        s_sa = Count("short_conv_c_stored", SCT)
        s_sc = Count("short_conv_steps", 5 * SCT)
        s_dtp = Count("dt_feature_major_stored", 1)
        s_dtt = Count("dt_transposed", 1)

        STEP_A = 17
        DV_STEPS = STEP_A + 3
        s_dv = Count("dt_steps", DV_STEPS)
        s_da = Count("dt_exps", 3)
        s_cum = Count("cumulated", 1)
        s_t1 = Count("chunk_transposed", TB)
        s_tok = Count("chunk_position_major", TB)
        s_xw = Count("weighted_x_ready", TB)
        s_stp = Count("states_made", TB)
        s_st = Count("states_stored", TB)
        s_chain = Count("states_chained", 2 * (TB - 2))
        s_rows = Count("decay_rows_made", TB)
        s_gx = Count("gram_made", TB)
        s_seg = Count("segments_ready", TB)
        s_es = Count("segments_exped", TB)
        s_er = Count("rows_exped", TB)
        s_xt = Count("x_position_major", TB)
        s_cs = Count("scaled_c_ready", TB)
        s_mf = Count("decay_forward_done", TB)
        s_mb = Count("decay_both_done", TB)
        s_m = Count("ssd_matrix_ready", TB)
        s_y = Count("ssd_product_ready", TB)
        s_yd = Count("ssd_skip_added", TB)
        s_yz = Count("ssd_gated", TB)
        s_ysq = Count("ssd_squares_ready", 1)
        s_ysum = Count("ssd_square_sums_ready", 1)
        s_yms = Count("ssd_mean_squares_ready", 1)
        s_yrs = Count("ssd_rstd_ready", 1)
        s_ydg = Count("ssd_diagonals_ready", 1)
        s_ynb = Count("ssd_rstd_broadcast_ready", 1)
        s_yn = Count("ssd_output_ready", 1)

        s_g = Count("group_bank_ready", (TB - 1) * len(GROUPS))
        s_ge = Count("group_rows_stored", TB * len(GROUPS))
        s_ra = Count("rotary_products", 2 * TB)
        s_rb = Count("rotary_written", 2 * TB)
        s_kh = Count("k_hi_ready", TB)
        s_kl = Count("k_lo_ready", TB)
        s_kt = Count("k_transposed", TB)
        s_ks = Count("k_stack_ready", TB)

        ITS = HEADS * TB
        s_qh = Count("q_hi_split", ITS)
        s_ql = Count("q_lo_split", ITS)
        s_qt = Count("q_transposed", ITS, 2)
        s_qs = Count("q_stack_ready", ITS, 1)
        s_s = Count("scores_ready", 2 * ITS, 4)
        s_mx = Count("maxima_ready", 2 * ITS)
        s_e = Count("exps_ready", 2 * ITS, 2)
        s_rl = Count("sum_reciprocals_ready", ITS)
        s_cc = Count("mix_factor_ready", ITS)
        s_w = Count("weights_mixed", ITS, 2)
        s_wt = Count("weights_transposed", ITS, 2)
        s_we = Count("weights_key_major", ITS, 1)
        s_o = Count("head_product_ready", ITS, 2)
        s_oe = Count("head_output_stored", ITS, 1)
        s_os = Count("head_squares_summed", ITS, 1)
        s_oms = Count("head_mean_squares_ready", 1)
        s_ors = Count("head_rstd_ready", 1)
        s_on = Count("heads_normed", HEADS)
        s_ot = Count("heads_transposed", HEADS)
        s_yh = Count("outputs_hi_ready", KT)
        s_yl = Count("outputs_lo_ready", KT)

        s_res = Count("residual_added", KT)
        s_m1 = Count("mlp_centre_done", 2 * FT)
        s_m2 = Count("mlp_left_done", 2 * FT)
        s_m3 = Count("mlp_conv_done", 2 * FT)
        s_sg = Count("mlp_gate_ready", FT)
        s_mm = Count("mlp_product_ready", FT)
        s_mh = Count("mlp_hi_ready", FT)
        s_ml = Count("mlp_lo_ready", FT)
        s_dr = Count("down_tile_ready", NCH * (KT - 2))
        s_dn = Count("down_tile_added", NCH * KT, KT)

        STEP = UPN + DNN

        def hi_of(act, l, p, i=None, width=HALF):
            at = p if i is None else p + i * STEP
            loads = p // RAW + 1 if i is None else p // RAW + 1 + i * (STEP // RAW)
            act.wait_ge(s_raw[p % RAW], (l * (PANELS // RAW) + loads) * 16)
            act.wait_ge(s_panel.sem, s_panel.until(l, at - RING + 1))
            nc.scalar.activation(whi[p % RING][:, 0:width], raw[p % RAW][:, 0:width], ACT.Copy).then_inc(s_hi.sem, 1)

        def lo_of(dve, l, p, i=None, width=HALF):
            at = p if i is None else p + i * STEP
            dve.wait_ge(s_hi.sem, s_hi.until(l, at + 1))
            nc.vector.tensor_tensor(wlo[p % RING][:, 0:width], raw[p % RAW][:, 0:width],
                                    whi[p % RING][:, 0:width].bitcast(F32), ALU.subtract).then_inc(s_split.sem, 1)

        def ahead(part_of, eng, l, p, i=None):
            q = p + LOOKAHEAD
            if q < PANELS:
                part_of(eng, l, q, i)
            else:
                part_of(eng, l + 1, q - PANELS, None, width=16)

        def psum_down(n):
            return (n + 2) % 4

        block = ctx.enter_context(nc.Block())

        @block.sync
        def _(sp):
            n_setup = 0

            def setup(dst, src):
                sp.dma_start(dst, src).then_inc(s_setup, 16)

            sp.dma_start(xin[:, :, :], x[0].rearrange("(t p) d -> p t d", p=P)).then_inc(s_xin, 16)
            for l in range(L):
                a, b, c = stage[l]
                taps = [ffn_conv_w[l, k].rearrange("(t p) -> t p", p=P) for k in range(3)]
                setup(a[0:2 * FT, :], taps[0])
                setup(a[2 * FT:4 * FT, :], taps[1])
                setup(b[0:2 * FT, :], taps[2])
                setup(b[2 * FT:4 * FT, :], ffn_conv_b[l].rearrange("(t p) -> t p", p=P))
                r = 0
                for src in (norm_mix_g[l], norm_ffn_g[l], ssd_conv_w[l].rearrange("k c -> (k c)"), ssd_conv_b[l],
                            sc_conv_w[l].rearrange("k c -> (k c)"), ssd_norm_g[l], subln_g[l]):
                    rows = src.rearrange("(t p) -> t p", p=P)
                    setup(c[r:r + rows.shape[0], :], rows)
                    r += rows.shape[0]
                assert r == C_LAM - C_G1
                for n, v in enumerate((lam_q1, lam_k1, lam_q2, lam_k2)):
                    setup(lamv[:, n, l, :], v[l].partition_broadcast(P))
                setup(prm[:, l, C_A:C_A + 2 * NH], ssd_a_log[l].rearrange("d h -> (d h)").partition_broadcast(P))
                setup(prm[:, l, C_DTB:C_DTB + 2 * NH], ssd_dt_bias[l].rearrange("d h -> (d h)").partition_broadcast(P))
                for h in range(NH):
                    g, hf = h // 2, h % 2
                    setup(prm[64 * hf:64 * hf + 64, l, C_D + g:C_D + g + 1], ssd_d[l, h:h + 1].partition_broadcast(64))
            setup(pos_i[:, :], positions[0].rearrange("(t p) -> t p", p=P))

            w_in_t = w_in.rearrange("l (k p) n -> l p k n", p=P)
            w_out_t = w_out.rearrange("l (k p) n -> l p k n", p=P)
            w_up_t = w_up.rearrange("l (k p) n -> l p k n", p=P)

            def load(l, dst, src, p, i=None, also=False):
                sp.wait_ge(s_split.sem, s_split.until(l, (p if i is None else p + i * STEP) - RAW + 1 + also))
                sp.dma_start(dst, src).then_inc(s_raw[p % RAW], 16)

            def one(ap, l):
                return ap[bass.ds(l, 1)].rearrange("l p k n -> (l p) k n")

            def dt_slot(p):
                return raw[p % RAW][:, 0:16].rearrange("p (k n) -> p k n", n=8)

            def tiles_slot(p):
                return raw[p % RAW][:, :].rearrange("p (k c) -> p k c", c=P)

            def load_up(l, q, p, chunk, i=None):
                cols = bass.ds(chunk * (CH * P) + (q // 4) * P + ((q % 4) // 2) * FF, P)
                load(l, tiles_slot(p), one(w_up_t[:, :, 4 * (q % 2):4 * (q % 2) + 4, cols], l), p, i)

            def load_dn(l, q, p, chunk, i=None):
                src = w_down[bass.ds(l, 1), bass.ds(chunk * (CH * P) + (q % CH) * P, P),
                             (q // CH) * HALF:(q // CH + 1) * HALF].rearrange("l p n -> (l p) n")
                load(l, raw[p % RAW][:, :], src, p, i)

            with nc.sync.Fori(0, L) as l:
                for p in range(P_F):
                    load(l, dt_slot(p), one(w_in_t[:, :, 2 * p:2 * p + 2, COL_DT:COL_DT + 8], l), p)
                for n, (_, _, col) in enumerate(F_TILES):
                    for h in range(2):
                        p = P_F + 2 * n + h
                        load(l, tiles_slot(p), one(w_in_t[:, :, 4 * h:4 * h + 4, col:col + P], l), p)
                for n, (_, col) in enumerate(GROUPS):
                    for k in range(KT):
                        p = P_G + KT * n + k
                        dst = raw[p % RAW][:, :].rearrange("p (k n) -> p k n", k=1)
                        src = one(w_in_t[:, :, k:k + 1, col:col + HALF], l)
                        if col == k == 0:
                            sp.dma_start(dst, src).then_inc(s_raw[p % RAW], 16)
                            continue
                        load(l, dst, src, p, also=GROUPS[(n + 1) % len(GROUPS)][1] == 0 and k == KT - 1)
                for n in range(KT):
                    for h in range(2):
                        p = P_OUT + 2 * n + h
                        load(l, tiles_slot(p), one(w_out_t[:, :, 4 * h:4 * h + 4, n * P:(n + 1) * P], l), p)
                for q in range(UPN):
                    load_up(l, q, P_UP0 + q, 0)
                with nc.sync.Fori(0, NCH - 1) as i:
                    for q in range(UPN):
                        load_up(l, q, P_BODY + q, i + 1, i)
                    for q in range(DNN):
                        load_dn(l, q, P_BODY + UPN + q, i, i)
                for q in range(DNN):
                    load_dn(l, q, P_DN + q, NCH - 1)
            for p in range(LOOKAHEAD):
                sp.wait_ge(s_split.sem, s_split.until(L, p - RAW + 1))
                sp.dma_start(dt_slot(p), w_in_t[0, :, 2 * p:2 * p + 2, COL_DT:COL_DT + 8]).then_inc(s_raw[p % RAW], 16)
            sp.dma_start(fg_row[:, :], final_norm_g.partition_broadcast(P)).then_inc(s_fg, 16)
            for b in range(TB):
                sp.wait_ge(s_row, b + 1)
                sp.dma_start(out[0, b * P:(b + 1) * P, :], o_row[b % 2][:, :]).then_inc(s_out[b % 2], 16)
            for i in range(2):
                sp.wait_ge(s_out[i], 16 * (TB // 2))

        N_SETUP = 16 * (L * (4 + 7 + 4 + 2 + NH) + 1)

        @block.gpsimd
        def _(pool):
            g = nc.gpsimd
            g.memset(ident[:, :], 0.0).then_inc(s_const, 1)
            g.memset(ones[:, :], 1.0).then_inc(s_const, 1)
            g.memset(capf[:, :], 0.0).then_inc(s_const, 1)
            g.memset(capb[:, :], 0.0).then_inc(s_const, 1)
            g.memset(minus_half[:, :], -0.5).then_inc(s_const, 1)
            pool.wait_ge(s_const, 5)
            g.affine_select(out=ident[:, :], in_=ident[:, :], compare_op=ALU.not_equal, fill=1.0, base=0,
                            pattern=[[-1, P]], channel_multiplier=1).then_inc(s_const, 1)
            for dst, src, fill, sign in ((upto, ones, 0.0, 1), (downto, ones, 0.0, -1),
                                         (capf, capf, -1e30, 1), (capb, capb, -1e30, -1)):
                g.affine_select(out=dst[:, :], in_=src[:, :], compare_op=ALU.is_ge, fill=fill, base=0,
                                pattern=[[sign, P]], channel_multiplier=-sign).then_inc(s_const, 1)

            def power(c_in, c_out, l, k, n):
                pool.wait_ge(c_in.sem, c_in.until(l, k))
                g.tensor_tensor(rstd[:, 0:n], small[:, 0:n], minus_half[:, 0:n], ALU.pow).then_inc(c_out.sem, 1)

            def rotary(l, n, rows, b):
                v = rows[:, b, :].rearrange("p (h d) -> p h d", d=DQK)
                t1, t2 = v[:, :, 0:R2], v[:, :, R2:ROT]
                c = cosT[:, b:b + 1, :].broadcast_to([P, HC, R2])
                s = sinT[:, b:b + 1, :].broadcast_to([P, HC, R2])
                if n or b:
                    pool.wait_ge(s_rb.sem, s_rb.until(l, TB * n + b))
                pool.wait_ge(s_ge.sem, s_ge.until(l, TB * (n + 1) + b + 1))
                g.tensor_tensor(rot[:, 0, :, :], t1, c, ALU.mult)
                g.tensor_tensor(rot[:, 1, :, :], t2, s, ALU.mult)
                g.tensor_tensor(rot[:, 2, :, :], t2, c, ALU.mult)
                g.tensor_tensor(rot[:, 3, :, :], t1, s, ALU.mult).then_inc(s_ra.sem, 1)
                pool.wait_ge(s_ra.sem, s_ra.until(l, TB * n + b + 1))
                g.tensor_tensor(t1, rot[:, 0, :, :], rot[:, 1, :, :], ALU.subtract)
                g.tensor_tensor(t2, rot[:, 2, :, :], rot[:, 3, :, :], ALU.add).then_inc(s_rb.sem, 1)

            pool.wait_ge(s_aset, 3)
            with nc.gpsimd.Fori(0, L) as l:
                power(s_ms, s_rs, l, 1, TB)
                power(s_yms, s_yrs, l, 1, XT * TB)
                for n, rows in enumerate((q_tok, k_tok)):
                    for b in range(TB):
                        rotary(l, n, rows, b)
                with nc.gpsimd.Fori(0, HEADS) as hd:
                    for j in range(TB):
                        src = q_tok[:, j, bass.ds(hd * DV, DV)].rearrange("p (c d) -> p c d", d=DQK)
                        pool.wait_ge(s_qh.sem, s_qh.until(l, hd * TB + j + 1))
                        g.tensor_tensor(qsp[j % 2][:, :, 1, :, :], src.unsqueeze(2).broadcast_to([P, 2, 2, DQK]),
                                        qsp[j % 2][:, :, 0, :, :].bitcast(F32), ALU.subtract).then_inc(s_ql.sem, 1)
                power(s_oms, s_ors, l, 1, ITS)
                power(s_ms, s_rs, l, 2, TB)
            power(s_ms, s_rs, L, 1, TB)

        @block.scalar
        def _(act):
            a = nc.scalar

            def square_tile(l, k):
                if isinstance(k, int) and k % KT >= 2:
                    act.wait_ge(s_acc.sem, s_acc.until(l, k - 1))
                a.activation((sq, ht[0])[k % 2][:, :], xT[:, k % KT, :], ACT.Square).then_inc(s_sq.sem, 1)

            def normed_hi(l, n):
                for k in range(KT):
                    act.wait_ge(s_ht.sem, s_ht.until(l, n * KT + k + 1))
                    a.activation(ahi[:, k, :], ht[k % 2][:, :], ACT.Copy).then_inc(s_hh.sem, 1)

            def col(c):
                return pc[:, c:c + 1]

            act.sem_inc(s_qs.sem, s_qs.credit)
            act.sem_inc(s_e.sem, s_e.credit)
            act.sem_inc(s_we.sem, s_we.credit)
            act.sem_inc(s_oe.sem, s_oe.credit)
            act.sem_inc(s_os.sem, s_os.credit)
            act.wait_ge(s_setup, N_SETUP)
            for l in range(L):
                a_log = prm[:, l, C_A:C_A + 2 * NH]
                last = a.activation(a_log, a_log, ACT.Exp)
            last.then_inc(s_aset, 1)
            act.wait_ge(s_dset, 1)
            a.activation(lams[:, :, :], lams[:, :, :], ACT.Exp).then_inc(s_aset, 1)
            act.wait_ge(s_dset, 3)
            a.activation(sinT[:, :, :], ang[0][:, :, :], ACT.Sin)
            a.activation(cosT[:, :, :], ang[1][:, :, :], ACT.Sin).then_inc(s_aset, 1)
            for k in range(KT):
                act.wait_ge(s_xt0, k + 1)
                a.activation(xT[:, k, :], pair(k % 4), ACT.Copy).then_inc(s_xt1, 1)
                act.wait_ge(s_xt1, k + 1)
                square_tile(0, k)
            for p in range(LOOKAHEAD):
                hi_of(act, 0, p, width=16)

            with nc.scalar.Fori(0, L) as l:
                normed_hi(l, 0)
                for p in range(P_F):
                    ahead(hi_of, act, l, p)
                act.wait_ge(s_panel.sem, s_panel.until(l, P_F))
                a.activation(dtT[:, :], pair(2)[0:8, :], ACT.Copy).then_inc(s_dtp.sem, 1)

                def silu_xbc(t):
                    act.wait_ge(s_c3.sem, s_c3.until(l, t + 1))
                    a.activation(xbc[:, t, :], cv[t % 2][:, :], ACT.Silu).then_inc(s_xs.sem, 1)

                for n, (kind, t, _) in enumerate(F_TILES):
                    p = P_F + 2 * n
                    ahead(hi_of, act, l, p)
                    ahead(hi_of, act, l, p + 1)
                    act.wait_ge(s_panel.sem, s_panel.until(l, p + 2))
                    if kind == "xbc":
                        if t >= 2:
                            act.wait_ge(s_xs.sem, s_xs.until(l, t - 1))
                        a.activation(cv[t % 2][:, :], pair(n % 4), ACT.Identity, bias=col(C_XB + t),
                                     scale=col(C_XW + XBCT + t)).then_inc(s_c1.sem, 1)
                        if t:
                            silu_xbc(t - 1)
                    elif kind == "z":
                        if t == 0:
                            silu_xbc(XBCT - 1)
                        a.activation(ys[:, t, :], pair(n % 4), ACT.Silu).then_inc(s_z.sem, 1)
                    elif kind == "c":
                        if t:
                            act.wait_ge(s_sc.sem, s_sc.until(l, 5 * t))
                        else:
                            act.wait_ge(s_xs.sem, s_xs.until(l, XBCT))
                        a.activation(cv[0][:, :], pair(n % 4), ACT.Copy).then_inc(s_sa.sem, 1)

                act.wait_ge(s_dv.sem, s_dv.until(l, 3))
                a.activation(DT_EXP[:, :, :], DT_EXP[:, :, :], ACT.Exp, scale=-1.0).then_inc(s_da.sem, 1)
                act.wait_ge(s_dv.sem, s_dv.until(l, DV_STEPS - 1))
                a.activation(DT_W[:, :, :], DT_W[:, :, :], ACT.Exp).then_inc(s_da.sem, 1)
                a.activation(DT_DEC[:, :, :], ps[:, 0, 64:64 + DW].rearrange("p (t h) -> p t h", h=2 * NH),
                             ACT.Exp).then_inc(s_da.sem, 1)

                def store_states(c):
                    act.wait_ge(s_stp.sem, s_stp.until(l, c + 1))
                    a.activation(st[:, c, :, :, :].rearrange("p g d n -> p (g d n)"), ps[:, 4 + c % 2, :],
                                 ACT.Copy).then_inc(s_st.sem, 1)

                for c in range(TB):
                    act.wait_ge(s_t1.sem, s_t1.until(l, c + 1))
                    if c >= 2:
                        act.wait_ge(s_stp.sem, s_stp.until(l, c - 1))
                        act.wait_ge(s_xw.sem, s_xw.until(l, c - 1))
                    a.activation(xb_tok[c % 2][:, :], ps[:, 2 + c % 2, :], ACT.Copy).then_inc(s_tok.sem, 1)
                    if c:
                        store_states(c - 1)
                store_states(TB - 1)
                for c in range(TB):
                    if c:
                        act.wait_ge(s_y.sem, s_y.until(l, c))
                    act.wait_ge(s_gx.sem, s_gx.until(l, c + 1))
                    act.wait_ge(s_rows.sem, s_rows.until(l, c + 1))
                    a.activation(xb_tok[c % 2][:, 0:SSDW], ps[:, 4 + c % 2, SSDW:2 * SSDW],
                                 ACT.Copy).then_inc(s_xt.sem, 1)
                    a.activation(erow[:, :, :, :].rearrange("p d h l -> p (d h l)"), pair(c % 2),
                                 ACT.Exp).then_inc(s_er.sem, 1)
                    act.wait_ge(s_seg.sem, s_seg.until(l, c + 1))
                    a.activation(seg[:, :, :, :], seg[:, :, :, :], ACT.Exp).then_inc(s_es.sem, 1)
                act.wait_ge(s_yz.sem, s_yz.until(l, TB))
                a.activation(sqs[:, :, :], ys[:, :, :], ACT.Square).then_inc(s_ysq.sem, 1)

                for n, (kind, _) in enumerate(GROUPS):
                    for k in range(KT):
                        ahead(hi_of, act, l, P_G + KT * n + k)
                    for b in range(TB):
                        if b < TB - 1:
                            act.wait_ge(s_g.sem, s_g.until(l, (TB - 1) * n + b + 1))
                        else:
                            act.wait_ge(s_panel.sem, s_panel.until(l, P_G + KT * (n + 1)))
                        dst = {"v": v_tok, "q": q_tok, "k": k_tok}[kind]
                        a.activation(dst[:, b, :], ps[:, b, :], ACT.Copy,
                                     scale=DQK ** -0.5 if kind == "q" else 1.0).then_inc(s_ge.sem, 1)

                def store_stack(b):
                    act.wait_ge(s_kt.sem, s_kt.until(l, b + 1))
                    a.activation(kst[:, :, b * P:(b + 1) * P], pair(b % 4).rearrange("p (h n) -> p h n", n=P),
                                 ACT.Copy).then_inc(s_ks.sem, 1)

                for b in range(TB + 1):
                    if b < TB:
                        act.wait_ge(s_rb.sem, s_rb.until(l, TB + b + 1))
                        if b >= 2:
                            act.wait_ge(s_kt.sem, s_kt.until(l, b - 1))
                        a.activation(ksp[b % 2][:, :, 0, :], k_tok[:, b, :].rearrange("p (h d) -> p h d", d=DQK),
                                     ACT.Copy).then_inc(s_kh.sem, 1)
                    if b:
                        store_stack(b - 1)

                with nc.scalar.Fori(0, HEADS) as hd:
                    it0 = hd * TB

                    def q_stack(j):
                        act.wait_ge(s_qt.sem, s_qt.until(l, it0 + j + 1))
                        act.wait_ge(s_s.sem, s_s.until(l, 2 * (it0 + j) - 2))
                        a.activation(qT[j % 2][:, :, :, :].rearrange("p c s q -> p (c s q)"), ps[:, 6, :],
                                     ACT.Copy).then_inc(s_qs.sem, 1)

                    def exps(j):
                        act.wait_ge(s_w.sem, s_w.until(l, it0 + j - 1))
                        for c in range(2):
                            act.wait_ge(s_mx.sem, s_mx.until(l, 2 * (it0 + j) + c + 1))
                            a.activation(E[:, j % 2, c, :], pair(c), ACT.Exp, bias=nmax[:, j % 2, c:c + 1],
                                         accum_out=lsum[:, j % 2, c:c + 1]).then_inc(s_e.sem, 1)

                    q_stack(0)
                    exps(0)
                    q_stack(1)
                    for j in range(TB):
                        if j + 2 < TB:
                            q_stack(j + 2)
                        if j + 1 < TB:
                            exps(j + 1)
                        act.wait_ge(s_wt.sem, s_wt.until(l, it0 + j + 1))
                        act.wait_ge(s_o.sem, s_o.until(l, it0 + j - 1))
                        a.activation(WT[j % 2][:, :, :].rearrange("p b q -> p (b q)"), pair(2),
                                     ACT.Copy).then_inc(s_we.sem, 1)
                        act.wait_ge(s_o.sem, s_o.until(l, it0 + j + 1))
                        act.wait_ge(s_rl.sem, s_rl.until(l, it0 + j + 1))
                        r0 = rlsum[:, j % 2, 0:1]
                        a.activation(o_tok[:, j, bass.ds(hd * DV, DV)], ps[:, 7, 0:DV], ACT.Copy,
                                     scale=r0).then_inc(s_oe.sem, 1)
                        a.activation(osq[:, :], ps[:, 7, 0:DV], ACT.Square, scale=r0,
                                     accum_out=ssq[:, bass.ds(it0 + j, 1)]).then_inc(s_os.sem, 1)

                for t, src in enumerate((yc[:, 0, :], yc[:, 1, :], ys[:, 0, :], ys[:, 1, :])):
                    if t == 0:
                        act.wait_ge(s_on.sem, s_on.until(l, 1))
                    a.activation(ahi[:, HEADS + t, :], src, ACT.Copy).then_inc(s_yh.sem, 1)
                for h in range(HEADS):
                    act.wait_ge(s_ot.sem, s_ot.until(l, h + 1))
                    if h == 0:
                        act.wait_ge(s_ot.sem, s_ot.until(l, HEADS))
                    a.activation(ahi[:, h, :], pair(h), ACT.Identity, bias=0.0, scale=col(C_SUB)).then_inc(s_yh.sem, 1)

                for n in range(KT):
                    ahead(hi_of, act, l, P_OUT + 2 * n)
                    ahead(hi_of, act, l, P_OUT + 2 * n + 1)
                    act.wait_ge(s_res.sem, s_res.until(l, n + 1))
                    square_tile(l, KT + n)

                normed_hi(l, 1)

                def centre(n, tile, j, up):
                    c = up * FT + j
                    if isinstance(c, int):
                        b, w = col(C_FB + c), col(C_FW[1] + c)
                    else:
                        b, w = pc[:, bass.ds(C_FB + c, 1)], pc[:, bass.ds(C_FW[1] + c, 1)]
                    a.activation(tile[:, :], pair((n + 2) % 4), ACT.Identity, bias=b, scale=w).then_inc(s_m1.sem, 1)

                def gate(k, j):
                    act.wait_ge(s_m3.sem, s_m3.until(l, 2 * k + 2))
                    a.activation(tg[j][:, :], tg[j][:, :], ACT.Silu).then_inc(s_sg.sem, 1)

                def product_hi(k, slot, j):
                    act.wait_ge(s_mm.sem, s_mm.until(l, k + 1))
                    a.activation(mhi[:, slot, :], tg[j][:, :], ACT.Copy).then_inc(s_mh.sem, 1)

                def up_chunk(chunk, p0, i=None):
                    for n in range(2 * CH):
                        j, up = n // 2, n % 2
                        ahead(hi_of, act, l, p0 + 2 * n, i)
                        ahead(hi_of, act, l, p0 + 2 * n + 1, i)
                        at = p0 + 2 * n + 2 if i is None else p0 + 2 * n + 2 + i * STEP
                        act.wait_ge(s_panel.sem, s_panel.until(l, at))
                        if i is not None and up == 0:
                            act.wait_ge(s_ml.sem, s_ml.until(l, (chunk - 1) * CH + j + 1))
                        centre(n, (tg, tu)[up][j], chunk * CH + j, up)
                        if n == 2:
                            gate(chunk * CH, 0)

                def products(chunk, slot):
                    gate(chunk * CH + 1, 1)
                    product_hi(chunk * CH, slot, 0)
                    product_hi(chunk * CH + 1, slot + 1, 1)

                up_chunk(0, P_UP0)
                products(0, 0)
                with nc.scalar.Fori(0, NCH - 1) as i:
                    up_chunk(i + 1, P_BODY, i)
                    for q in range(DNN):
                        ahead(hi_of, act, l, P_BODY + UPN + q, i)
                        if q == 0:
                            gate((i + 1) * CH + 1, 1)
                    act.wait_ge(s_panel.sem, s_panel.until(l, P_BODY + UPN + DNN + i * STEP))
                    product_hi((i + 1) * CH, 0, 0)
                    product_hi((i + 1) * CH + 1, 1, 1)
                for q in range(DNN):
                    ahead(hi_of, act, l, P_DN + q)
                for n in range(KT):
                    act.wait_ge(s_dn.sem, s_dn.until(l, (NCH - 1) * KT + n + 1))
                    square_tile(l + 1, n)

        @block.vector
        def _(dve):
            v = nc.vector
            links = [0]

            def link(ins, value=None):
                links[0] += 1
                ins.then_inc(s_dlink, 1)
                dve.wait_ge(s_dlink, links[0])

            def col(c):
                return pc[:, c:c + 1]

            def add_squares(l, k):
                src = (sq, ht[0])[k % 2]
                dve.wait_ge(s_sq.sem, s_sq.until(l, k + 1))
                if k % KT == 0:
                    v.tensor_copy(acc[:, :], src[:, :]).then_inc(s_acc.sem, 1)
                else:
                    dve.wait_ge(s_acc.sem, s_acc.until(l, k))
                    v.tensor_tensor(acc[:, :], acc[:, :], src[:, :], ALU.add).then_inc(s_acc.sem, 1)

            def mean_squares(l, n):
                dve.wait_ge(s_nsum.sem, s_nsum.until(l, n + 1))
                v.tensor_scalar(small[:, 0:TB], ps[:, 0, 0:TB], 1.0 / D, EPS, ALU.mult, ALU.add).then_inc(s_ms.sem, 1)

            def diagonals(l, n, c_rs, c_dg, dst, count):
                dve.wait_ge(c_rs.sem, c_rs.until(l, n + 1))
                for b in range(count):
                    last = v.tensor_scalar(dst(b), ident[:, :], rstd[:, b:b + 1], None, ALU.mult)
                last.then_inc(c_dg.sem, 1)

            def norm(l, n, gain):
                mean_squares(l, n)
                diagonals(l, n, s_rs, s_dg, lambda b: sq[:, b * P:(b + 1) * P], TB)
                dve.wait_ge(s_nb.sem, s_nb.until(l, n + 1))

                def lo(k):
                    dve.wait_ge(s_hh.sem, s_hh.until(l, n * KT + k + 1))
                    v.tensor_tensor(alo[:, k, :], ht[k % 2][:, :], ahi[:, k, :].bitcast(F32),
                                    ALU.subtract).then_inc(s_hl.sem, 1)

                for k in range(KT):
                    if k >= 2:
                        dve.wait_ge(s_hl.sem, s_hl.until(l, n * KT + k - 1))
                    v.scalar_tensor_tensor(out=ht[k % 2][:, :], in0=xT[:, k, :], scalar=col(gain + k), in1=pair(1),
                                           op0=ALU.mult, op1=ALU.mult).then_inc(s_ht.sem, 1)
                    if k:
                        lo(k - 1)
                lo(KT - 1)

            def taps(l, dst, src, w0, w2, c_mid, c_end, k):
                v.scalar_tensor_tensor(out=dst[:, 1:S], in0=src[:, 0:S - 1], scalar=w0, in1=dst[:, 1:S],
                                       op0=ALU.mult, op1=ALU.add).then_inc(c_mid.sem, 1)
                dve.wait_ge(c_mid.sem, c_mid.until(l, k))
                v.scalar_tensor_tensor(out=dst[:, 0:S - 1], in0=src[:, 1:S], scalar=w2, in1=dst[:, 0:S - 1],
                                       op0=ALU.mult, op1=ALU.add).then_inc(c_end.sem, 1)

            dve.sem_inc(s_split.sem, s_split.credit)
            dve.sem_inc(s_w.sem, s_w.credit)
            dve.sem_inc(s_dn.sem, s_dn.credit)
            dve.wait_ge(s_const, 10)
            link(v.tensor_copy(identr[:, :], ident[:, :]))
            dve.wait_ge(s_setup, N_SETUP)
            link(v.tensor_copy(pos_f[:, :], pos_i[:, :]))
            v.tensor_tensor(lamp[:, :, :, :], lamv[:, 0:4:2, :, :], lamv[:, 1:4:2, :, :], ALU.mult).then_inc(s_dlink, 1)
            links[0] += 1
            dve.wait_ge(s_dlink, links[0])
            v.tensor_reduce(lams[:, :, :], lamp[:, :, :, :], AX_X, ALU.add).then_inc(s_dset, 1)
            dve.wait_ge(s_pset, 2 * 3 + 1)
            for l in range(L):
                at = 0
                for i, n in enumerate((4 * FT, 4 * FT, C_LAM - C_G1)):
                    link(v.tensor_copy(prm[:, l, at:at + n], ps[:, 3 * l + i, 0:n]))
                    at += n
                sub = prm[:, l, C_SUB:C_SUB + 1]
                link(v.tensor_scalar(sub, sub, 1.0 - LAM_INIT[l], None, ALU.mult))
            dve.wait_ge(s_aset, 1)
            for l in range(L):
                a_row = prm[:, l, C_A:C_A + 2 * NH]
                link(v.tensor_scalar(a_row, a_row, -1.0, None, ALU.mult))
            dve.wait_ge(s_aset, 2)
            for l in range(L):
                m = prm[:, l, C_LAM:C_LAM + 1]
                link(v.tensor_tensor(m, lams[:, 1, l:l + 1], lams[:, 0, l:l + 1], ALU.subtract))
                link(v.tensor_scalar(m, m, -LAM_INIT[l], None, ALU.add))
            link(v.tensor_copy(pos_c[:, :], ps[:, 6, 0:TB]))
            for j in range(R2):
                link(v.tensor_scalar(ang[0][:, :, j], pos_c[:, :], INV_FREQ[j], None, ALU.mult))
            link(v.tensor_scalar(ang[1][:, :, :], ang[0][:, :, :], 1.0 / (2 * math.pi), ROUND, ALU.mult, ALU.add))
            link(v.tensor_scalar(ang[1][:, :, :], ang[1][:, :, :], -ROUND, None, ALU.add))
            for part in TWO_PI_PARTS:
                link(v.scalar_tensor_tensor(out=ang[0][:, :, :], in0=ang[1][:, :, :], scalar=-part,
                                            in1=ang[0][:, :, :], op0=ALU.mult, op1=ALU.add))
            link(v.tensor_scalar(ang[0][:, :, :], ang[0][:, :, :], PI_BELOW, -PI_BELOW, ALU.min, ALU.max))
            link(v.scalar_tensor_tensor(out=ang[2][:, :, :], in0=ang[0][:, :, :], scalar=-1.0, in1=ang[0][:, :, :],
                                        op0=ALU.mult, op1=ALU.max))
            v.tensor_scalar(ang[1][:, :, :], ang[2][:, :, :], -1.0, math.pi / 2, ALU.mult,
                            ALU.add).then_inc(s_dset, 2)
            for k in range(KT):
                add_squares(0, k)
            for p in range(LOOKAHEAD):
                lo_of(dve, 0, p, width=16)

            with nc.vector.Fori(0, L) as l:
                v.tensor_copy(pc[:, :], prm[:, bass.ds(l, 1), :].rearrange("p a n -> p (a n)")).then_inc(s_pc.sem, 1)
                dve.wait_ge(s_pc.sem, s_pc.until(l, 1))
                norm(l, 0, C_G1)
                for p in range(P_F):
                    ahead(lo_of, dve, l, p)

                def dstep(ins):
                    steps[0] += 1
                    ins.then_inc(s_dv.sem, 1)
                    dve.wait_ge(s_dv.sem, s_dv.until(l, steps[0]))

                steps = [0]

                def by_block(c):
                    return pc[:, c:c + 2 * NH].unsqueeze(1).broadcast_to([P, TB, 2 * NH])

                for n, (kind, t, _) in enumerate(F_TILES):
                    p = P_F + 2 * n
                    ahead(lo_of, dve, l, p)
                    ahead(lo_of, dve, l, p + 1)
                    if kind == "xbc":
                        dve.wait_ge(s_c1.sem, s_c1.until(l, t + 1))
                        taps(l, cv[t % 2], pair(n % 4), col(C_XW + t), col(C_XW + 2 * XBCT + t), s_c2, s_c3, t + 1)
                    elif kind == "h":
                        dve.wait_ge(s_sa.sem, s_sa.until(l, t + 1))
                        dve.wait_ge(s_panel.sem, s_panel.until(l, p + 2))
                        v.tensor_tensor(cv[1][:, :], pair(n % 4), cv[0][:, :], ALU.mult).then_inc(s_sc.sem, 1)
                        dve.wait_ge(s_sc.sem, s_sc.until(l, 5 * t + 1))
                        v.tensor_scalar(cv[0][:, :], cv[1][:, :], col(C_SW + SCT + t), None,
                                        ALU.mult).then_inc(s_sc.sem, 1)
                        for w, (dst, src) in ((t, (slice(1, S), slice(0, S - 1))),
                                              (2 * SCT + t, (slice(0, S - 1), slice(1, S)))):
                            k = 5 * t + (2 if w == t else 3)
                            dve.wait_ge(s_sc.sem, s_sc.until(l, k))
                            v.scalar_tensor_tensor(out=cv[0][:, dst], in0=cv[1][:, src], scalar=col(C_SW + w),
                                                   in1=cv[0][:, dst], op0=ALU.mult, op1=ALU.add).then_inc(s_sc.sem, 1)
                    elif kind == "b":
                        dve.wait_ge(s_panel.sem, s_panel.until(l, p + 2))
                        dve.wait_ge(s_sc.sem, s_sc.until(l, 5 * t + 4))
                        v.tensor_tensor(yc[:, t, :], pair(n % 4), cv[0][:, :], ALU.mult).then_inc(s_sc.sem, 1)
                    if n == 0:
                        dve.wait_ge(s_dtt.sem, s_dtt.until(l, 1))
                        dstep(v.tensor_tensor(dtb_[0][:, :, :], ps[:, 6, 0:DW].rearrange("p (t h) -> p t h", h=2 * NH),
                                              by_block(C_DTB), ALU.add))

                d = [t[:, :, :] for t in dtb_]
                dstep(v.tensor_scalar(d[1], d[0], 0.0, None, ALU.max))
                dstep(v.scalar_tensor_tensor(out=d[2], in0=d[0], scalar=-1.0, in1=d[0], op0=ALU.mult, op1=ALU.max))
                dve.wait_ge(s_da.sem, s_da.until(l, 1))
                dstep(v.tensor_scalar(d[3], d[2], 2.0, None, ALU.add))
                dstep(v.reciprocal(d[4], d[3]))
                dstep(v.tensor_tensor(d[5], d[2], d[4], ALU.mult))
                dstep(v.tensor_tensor(d[6], d[5], d[5], ALU.mult))
                dstep(v.tensor_scalar(d[3], d[6], 1.0 / 15, None, ALU.mult))
                for n in (13, 11, 9, 7, 5, 3):
                    dstep(v.scalar_tensor_tensor(out=d[3], in0=d[3], scalar=1.0 / n, in1=d[6], op0=ALU.add,
                                                 op1=ALU.mult))
                dstep(v.scalar_tensor_tensor(out=d[4], in0=d[3], scalar=1.0, in1=d[5], op0=ALU.add, op1=ALU.mult))
                dstep(v.scalar_tensor_tensor(out=d[7], in0=d[4], scalar=2.0, in1=d[1], op0=ALU.mult, op1=ALU.add))
                dstep(v.tensor_tensor(DT_A[:, :, :], d[7], by_block(C_A), ALU.mult))
                assert steps[0] == STEP_A
                dve.wait_ge(s_cum.sem, s_cum.until(l, 1))
                q4 = DW // 2
                v.tensor_copy(DT_CUM[:, :, 0:NH], ps[:, 0, 0:q4].rearrange("p (t h) -> p t h", h=NH))
                dstep(v.tensor_copy(DT_CUM[:, :, NH:2 * NH], ps[:, 0, q4:DW].rearrange("p (t h) -> p t h", h=NH)))
                total = ps[:, 0, DW:2 * DW].rearrange("p (t h) -> p t h", h=2 * NH)
                dstep(v.tensor_tensor(DT_W[:, :, :], total, DT_CUM[:, :, :], ALU.subtract))
                dve.wait_ge(s_da.sem, s_da.until(l, 2))
                dstep(v.tensor_tensor(DT_W[:, :, :], DT_W[:, :, :], d[7], ALU.mult))
                assert steps[0] == DV_STEPS

                for c in range(TB):
                    dve.wait_ge(s_tok.sem, s_tok.until(l, c + 1))
                    if c >= 2:
                        dve.wait_ge(s_stp.sem, s_stp.until(l, c - 1))
                    x4 = xb_tok[c % 2][:, 0:SSDW].rearrange("p (h d) -> p h d", h=NH)
                    for dr in range(2):
                        w4 = DT_W[:, c, dr * NH:(dr + 1) * NH].unsqueeze(2).broadcast_to([P, NH, DQK])
                        last = v.tensor_tensor(xw[c % 2][:, dr, :, :], x4, w4, ALU.mult)
                    last.then_inc(s_xw.sem, 1)
                dve.wait_ge(s_st.sem, s_st.until(l, TB))
                dve.wait_ge(s_da.sem, s_da.until(l, 3))
                for n in range(1, TB - 1):
                    for dr in range(2):
                        c, prev = (n, n - 1) if dr == 0 else (TB - 1 - n, TB - n)
                        if n > 1:
                            dve.wait_ge(s_chain.sem, s_chain.until(l, 2 * (n - 1) - 1 + dr))
                        for h in range(NH):
                            g, hf = h // 2, h % 2
                            cols = slice(hf * DQK, (hf + 1) * DQK)
                            last = v.scalar_tensor_tensor(
                                out=st[:, c, g, dr, cols], in0=st[:, prev, g, dr, cols],
                                scalar=DT_DEC[:, c, dr * NH + h:dr * NH + h + 1], in1=st[:, c, g, dr, cols],
                                op0=ALU.mult, op1=ALU.add)
                        last.then_inc(s_chain.sem, 1)

                def skip_and_gate(c):
                    cols = slice(c * P, (c + 1) * P)
                    dve.wait_ge(s_y.sem, s_y.until(l, c + 1))
                    for g in range(XT):
                        last = v.scalar_tensor_tensor(out=xbc[:, g, cols], in0=xbc[:, g, cols], scalar=col(C_D + g),
                                                      in1=ps[:, 6 + c % 2, g * P:(g + 1) * P],
                                                      op0=ALU.mult, op1=ALU.add)
                    last.then_inc(s_yd.sem, 1)
                    dve.wait_ge(s_yd.sem, s_yd.until(l, c + 1))
                    v.tensor_tensor(ys[:, :, cols], xbc[:, 0:XT, cols], ys[:, :, cols], ALU.mult).then_inc(s_yz.sem, 1)

                dve.wait_ge(s_z.sem, s_z.until(l, XT))
                for c in range(TB):
                    dve.wait_ge(s_er.sem, s_er.until(l, c + 1))
                    if c:
                        dve.wait_ge(s_y.sem, s_y.until(l, c))
                    rows = pair(c % 2).rearrange("p (d h l) -> p d h l", d=2, h=NH)
                    for dr, cap in ((0, capf), (1, capb)):
                        for h in range(NH):
                            last = v.scalar_tensor_tensor(out=seg[:, dr, h, :], in0=rows[:, dr, h, :],
                                                          scalar=DT_CUM[:, c, dr * NH + h:dr * NH + h + 1],
                                                          in1=cap[:, :], op0=ALU.subtract, op1=ALU.min)
                    last.then_inc(s_seg.sem, 1)
                    for g in range(XT):
                        cT = xbc[:, 4 + g:5 + g, c * P:(c + 1) * P].unsqueeze(1).broadcast_to([P, 2, 2, P])
                        e4 = erow[:, :, 2 * g:2 * g + 2, :]
                        last = v.tensor_tensor(e4, e4, cT, ALU.mult)
                    last.then_inc(s_cs.sem, 1)
                    dve.wait_ge(s_es.sem, s_es.until(l, c + 1))
                    for h in range(NH):
                        last = v.tensor_scalar(seg[:, 0, h, :], seg[:, 0, h, :], DT[:, c, h:h + 1], None, ALU.mult)
                    last.then_inc(s_mf.sem, 1)
                    dve.wait_ge(s_mf.sem, s_mf.until(l, c + 1))
                    for h in range(NH):
                        last = v.scalar_tensor_tensor(out=seg[:, 0, h, :], in0=seg[:, 1, h, :],
                                                      scalar=DT[:, c, NH + h:NH + h + 1], in1=seg[:, 0, h, :],
                                                      op0=ALU.mult, op1=ALU.add)
                    last.then_inc(s_mb.sem, 1)
                    dve.wait_ge(s_mb.sem, s_mb.until(l, c + 1))
                    dve.wait_ge(s_xt.sem, s_xt.until(l, c + 1))
                    for g in range(XT):
                        gram = ps[:, 4 + c % 2, g * P:(g + 1) * P].unsqueeze(1).broadcast_to([P, 2, P])
                        m = seg[:, 0, 2 * g:2 * g + 2, :]
                        last = v.tensor_tensor(m, gram, m, ALU.mult)
                    last.then_inc(s_m.sem, 1)
                    if c:
                        skip_and_gate(c - 1)
                skip_and_gate(TB - 1)

                dve.wait_ge(s_ysum.sem, s_ysum.until(l, 1))
                v.tensor_scalar(small[:, 0:XT * TB], ps[:, 0, 0:XT * TB], 1.0 / P, EPS, ALU.mult,
                                ALU.add).then_inc(s_yms.sem, 1)
                diagonals(l, 0, s_yrs, s_ydg, lambda b: sqs[:, b // TB, (b % TB) * P:(b % TB + 1) * P], XT * TB)
                dve.wait_ge(s_ynb.sem, s_ynb.until(l, 1))
                for g in range(XT):
                    last = v.scalar_tensor_tensor(out=ys[:, g, :], in0=ys[:, g, :], scalar=col(C_NG + g),
                                                  in1=pair(1 + g), op0=ALU.mult, op1=ALU.mult)
                last.then_inc(s_yn.sem, 1)

                for p in range(P_G, P_OUT):
                    ahead(lo_of, dve, l, p)
                for b in range(TB):
                    dve.wait_ge(s_kh.sem, s_kh.until(l, b + 1))
                    rows = k_tok[:, b, :].rearrange("p (h d) -> p h d", d=DQK)
                    v.tensor_tensor(ksp[b % 2][:, :, 1, :], rows, ksp[b % 2][:, :, 0, :].bitcast(F32),
                                    ALU.subtract).then_inc(s_kl.sem, 1)

                with nc.vector.Fori(0, HEADS) as hd:
                    it0 = hd * TB

                    def q_hi(j):
                        dve.wait_ge(s_qt.sem, s_qt.until(l, it0 + j - 1))
                        src = q_tok[:, j, bass.ds(hd * DV, DV)].rearrange("p (c d) -> p c d", d=DQK)
                        v.tensor_copy(qsp[j % 2][:, :, 0, :, :], src.unsqueeze(2).broadcast_to([P, 2, 2, DQK])
                                      ).then_inc(s_qh.sem, 1)

                    def maxima(j):
                        for c in range(2):
                            dve.wait_ge(s_s.sem, s_s.until(l, 2 * (it0 + j) + c + 1))
                            v.tensor_reduce(nmax[:, j % 2, c:c + 1], pair(c), AX_X, ALU.max,
                                            negate=True).then_inc(s_mx.sem, 1)

                    q_hi(0)
                    q_hi(1)
                    maxima(0)
                    for j in range(TB):
                        if j + 2 < TB:
                            q_hi(j + 2)
                        if j + 1 < TB:
                            maxima(j + 1)
                        dve.wait_ge(s_e.sem, s_e.until(l, 2 * (it0 + j) + 2))
                        v.reciprocal(rlsum[:, j % 2, :], lsum[:, j % 2, :]).then_inc(s_rl.sem, 1)
                        dve.wait_ge(s_rl.sem, s_rl.until(l, it0 + j + 1))
                        v.scalar_tensor_tensor(out=mix[:, j % 2:j % 2 + 1], in0=lsum[:, j % 2, 0:1],
                                               scalar=rlsum[:, j % 2, 1:2], in1=col(C_LAM), op0=ALU.mult,
                                               op1=ALU.mult).then_inc(s_cc.sem, 1)
                        dve.wait_ge(s_cc.sem, s_cc.until(l, it0 + j + 1))
                        dve.wait_ge(s_wt.sem, s_wt.until(l, it0 + j - 1))
                        v.scalar_tensor_tensor(out=W[j % 2][:, :], in0=E[:, j % 2, 1, :],
                                               scalar=mix[:, j % 2:j % 2 + 1], in1=E[:, j % 2, 0, :],
                                               op0=ALU.mult, op1=ALU.add).then_inc(s_w.sem, 1)

                dve.wait_ge(s_os.sem, s_os.until(l, ITS))
                v.tensor_scalar(small[:, 0:ITS], ssq[:, :], 1.0 / DV, EPS, ALU.mult, ALU.add).then_inc(s_oms.sem, 1)
                dve.wait_ge(s_ors.sem, s_ors.until(l, 1))
                for h in range(HEADS):
                    for b in range(TB):
                        last = v.tensor_scalar(yn[:, h, b, :], o_tok[:, b, h * DV:(h + 1) * DV],
                                               rstd[:, h * TB + b:h * TB + b + 1], None, ALU.mult)
                    last.then_inc(s_on.sem, 1)
                for t, src in enumerate((yc[:, 0, :], yc[:, 1, :], ys[:, 0, :], ys[:, 1, :])):
                    dve.wait_ge(s_yh.sem, s_yh.until(l, t + 1))
                    v.tensor_tensor(alo[:, HEADS + t, :], src, ahi[:, HEADS + t, :].bitcast(F32),
                                    ALU.subtract).then_inc(s_yl.sem, 1)
                for h in range(HEADS):
                    dve.wait_ge(s_yh.sem, s_yh.until(l, HEADS + h + 1))
                    v.scalar_tensor_tensor(out=alo[:, h, :], in0=pair(h), scalar=col(C_SUB),
                                           in1=ahi[:, h, :].bitcast(F32), op0=ALU.mult,
                                           op1=ALU.subtract).then_inc(s_yl.sem, 1)

                for n in range(KT):
                    ahead(lo_of, dve, l, P_OUT + 2 * n)
                    ahead(lo_of, dve, l, P_OUT + 2 * n + 1)
                    dve.wait_ge(s_panel.sem, s_panel.until(l, P_OUT + 2 * n + 2))
                    v.tensor_tensor(xT[:, n, :], pair(n % 4), xT[:, n, :], ALU.add).then_inc(s_res.sem, 1)
                    if n:
                        add_squares(l, KT + n - 1)
                add_squares(l, 2 * KT - 1)

                norm(l, 1, C_G2)

                def conv(n, j, up, k):
                    c = up * FT + j
                    w0, w2 = ((col(C_FW[0] + c), col(C_FW[2] + c)) if isinstance(c, int) else
                              (pc[:, bass.ds(C_FW[0] + c, 1)], pc[:, bass.ds(C_FW[2] + c, 1)]))
                    dve.wait_ge(s_m1.sem, s_m1.until(l, k))
                    taps(l, (tg, tu)[up][n // 2], pair((n + 2) % 4), w0, w2, s_m2, s_m3, k)

                def up_chunk(chunk, p0, i=None):
                    for n in range(2 * CH):
                        ahead(lo_of, dve, l, p0 + 2 * n, i)
                        ahead(lo_of, dve, l, p0 + 2 * n + 1, i)
                        conv(n, chunk * CH + n // 2, n % 2, 2 * CH * chunk + n + 1)

                def product(k, j):
                    dve.wait_ge(s_sg.sem, s_sg.until(l, k + 1))
                    v.tensor_tensor(tg[j][:, :], tg[j][:, :], tu[j][:, :], ALU.mult).then_inc(s_mm.sem, 1)

                def product_lo(k, j):
                    dve.wait_ge(s_mh.sem, s_mh.until(l, k + 1))
                    v.tensor_tensor(mlo[:, j, :], tg[j][:, :], mhi[:, j, :].bitcast(F32),
                                    ALU.subtract).then_inc(s_ml.sem, 1)

                def add_down(chunk, n, p, i=None):
                    if n % 4 == 3:
                        dve.wait_ge(s_panel.sem, s_panel.until(l, p + 1 if i is None else p + 1 + i * STEP))
                    else:
                        dve.wait_ge(s_dr.sem, s_dr.until(l, chunk * (KT - 2) + (n // 4) * 3 + n % 4 + 1))
                    v.tensor_tensor(xT[:, n, :], pair(psum_down(n)), xT[:, n, :], ALU.add).then_inc(s_dn.sem, 1)

                up_chunk(0, P_UP0)
                product(0, 0)
                product(1, 1)
                product_lo(0, 0)
                product_lo(1, 1)
                with nc.vector.Fori(0, NCH - 1) as i:
                    up_chunk(i + 1, P_BODY, i)
                    product((i + 1) * CH, 0)
                    for h in range(2):
                        for q in range(CH):
                            ahead(lo_of, dve, l, P_BODY + UPN + h * CH + q, i)
                        for n in range(4 * h, 4 * h + 4):
                            add_down(i, n, P_BODY + UPN + h * CH + CH - 1, i)
                        if h == 0:
                            product((i + 1) * CH + 1, 1)
                    product_lo((i + 1) * CH, 0)
                    product_lo((i + 1) * CH + 1, 1)
                for h in range(2):
                    for q in range(CH):
                        ahead(lo_of, dve, l, P_DN + h * CH + q)
                    for n in range(4 * h, 4 * h + 4):
                        add_down(NCH - 1, n, P_DN + h * CH + CH - 1)
                        if n:
                            add_squares(l + 1, n - 1)
                add_squares(l + 1, KT - 1)

            mean_squares(L, 0)
            dve.wait_ge(s_rs.sem, s_rs.until(L, 1))
            dve.wait_ge(s_fg, 16)
            for b in range(TB):
                dve.wait_ge(s_fin, b + 1)
                if b >= 2:
                    dve.wait_ge(s_out[b % 2], 16 * (b // 2))
                v.scalar_tensor_tensor(out=o_row[b % 2][:, :], in0=pair(b % 4), scalar=rstd[:, b:b + 1],
                                       in1=fg_row[:, :], op0=ALU.mult, op1=ALU.mult).then_inc(s_row, 1)

        @block.tensor
        def _(pe):
            t = nc.tensor

            def k_tile(outs, w_hi, w_lo, xhi, xlo, first, last):
                for h in range(2):
                    t.matmul(outs[h], w_hi, xhi[:, h * HALF:(h + 1) * HALF], start=first, stop=False)
                for h in range(2):
                    t.matmul(outs[h], w_hi, xlo[:, h * HALF:(h + 1) * HALF], start=False, stop=False)
                for h in range(2):
                    mm = t.matmul(outs[h], w_lo, xhi[:, h * HALF:(h + 1) * HALF], start=False, stop=last)
                return mm

            def halves(k, rows=P):
                return [ps[0:rows, 2 * k + h, :] for h in range(2)]

            def feature_tile(l, p, k, i=None, ready=None):
                for h in range(2):
                    at = p + h if i is None else p + h + i * STEP
                    pe.wait_ge(s_split.sem, s_split.until(l, at + 1))
                    n = (p + h) % RING
                    for j in range(4):
                        kt = 4 * h + j
                        if ready is not None:
                            pe.wait_ge(ready[0].sem, ready[0].until(l, ready[1] + kt + 1))
                        mm = k_tile(halves(k), whi[n][:, j * P:(j + 1) * P], wlo[n][:, j * P:(j + 1) * P],
                                    ahi[:, kt, :], alo[:, kt, :], kt == 0, kt == KT - 1)
                    mm.then_inc(s_panel.sem, 1)

            def square_sums(l, n):
                pe.wait_ge(s_acc.sem, s_acc.until(l, n * KT + KT))
                for b in range(TB):
                    mm = t.matmul(ps[:, 0, b:b + 1], acc[:, b * P:(b + 1) * P], ones[:, 0:1], start=True, stop=True)
                mm.then_inc(s_nsum.sem, 1)

            def norm(l, n):
                square_sums(l, n)
                pe.wait_ge(s_dg.sem, s_dg.until(l, n + 1))
                for b in range(TB):
                    mm = t.matmul(pair(1)[:, b * P:(b + 1) * P], ones[:, :], sq[:, b * P:(b + 1) * P],
                                  start=True, stop=True)
                mm.then_inc(s_nb.sem, 1)

            pe.sem_inc(s_panel.sem, s_panel.credit)
            pe.sem_inc(s_qt.sem, s_qt.credit)
            pe.sem_inc(s_s.sem, s_s.credit)
            pe.sem_inc(s_wt.sem, s_wt.credit)
            pe.sem_inc(s_o.sem, s_o.credit)
            pe.wait_ge(s_const, 10)
            pe.wait_ge(s_setup, N_SETUP)
            for l in range(L):
                for i, n in enumerate((4 * FT, 4 * FT, C_LAM - C_G1)):
                    t.transpose(ps[:, 3 * l + i, 0:n], stage[l][i][0:n, :], ident[0:n, 0:n]).then_inc(s_pset, 1)
            pe.wait_ge(s_dlink, 2)
            t.transpose(ps[:, 6, 0:TB], pos_f[:, :], ident[0:TB, 0:TB]).then_inc(s_pset, 1)
            pe.wait_ge(s_dset, 3)
            pe.wait_ge(s_xin, 16)
            for k in range(KT):
                if k >= 4:
                    pe.wait_ge(s_xt1, k - 3)
                for b in range(TB):
                    mm = t.transpose(pair(k % 4)[:, b * P:(b + 1) * P], xin[:, b, k * P:(k + 1) * P], ident[:, :])
                mm.then_inc(s_xt0, 1)

            with nc.tensor.Fori(0, L) as l:
                norm(l, 0)

                for p in range(P_F):
                    pe.wait_ge(s_split.sem, s_split.until(l, p + 1))
                    for j in range(2):
                        kt = 2 * p + j
                        pe.wait_ge(s_hl.sem, s_hl.until(l, kt + 1))
                        mm = k_tile(halves(2, 8), whi[p % RING][:, 8 * j:8 * j + 8], wlo[p % RING][:, 8 * j:8 * j + 8],
                                    ahi[:, kt, :], alo[:, kt, :], kt == 0, kt == KT - 1)
                    mm.then_inc(s_panel.sem, 1)

                left = []
                for n, (kind, i, _) in enumerate(F_TILES):
                    if n == 2:
                        pe.wait_ge(s_dtp.sem, s_dtp.until(l, 1))
                    elif n == 3:
                        pe.wait_ge(s_dv.sem, s_dv.until(l, 1))
                    elif n >= 4:
                        pe.wait_ge(left[n - 4][0].sem, left[n - 4][0].until(l, left[n - 4][1]))
                    left.append({"xbc": (s_c3, i + 1), "z": (s_z, i + 1), "c": (s_sa, i + 1),
                                 "h": (s_sc, 5 * i + 1), "b": (s_sc, 5 * i + 5)}[kind])
                    feature_tile(l, P_F + 2 * n, n % 4)
                    if n == 0:
                        pe.wait_ge(s_dtp.sem, s_dtp.until(l, 1))
                        for b in range(TB):
                            mm = t.matmul(ps[:, 6, b * 8:b * 8 + 8], dtT[:, b * P:(b + 1) * P], ident[0:8, 0:8],
                                          start=True, stop=True)
                        mm.then_inc(s_dtt.sem, 1)

                pe.wait_ge(s_dv.sem, s_dv.until(l, STEP_A))
                q4 = DW // 2
                a8 = DT_A
                t.matmul(ps[:, 0, 0:q4], upto[:, :], a8[:, :, 0:NH], start=True, stop=True)
                t.matmul(ps[:, 0, q4:DW], downto[:, :], a8[:, :, NH:2 * NH], start=True, stop=True)
                t.matmul(ps[:, 0, DW:2 * DW], ones[:, :], a8[:, :, :], start=True, stop=True).then_inc(s_cum.sem, 1)

                pe.wait_ge(s_xs.sem, s_xs.until(l, XBCT))

                def chunk_tokens(c):
                    if c >= 2:
                        pe.wait_ge(s_tok.sem, s_tok.until(l, c - 1))
                    for n in range(4):
                        mm = t.transpose(ps[:, 2 + c % 2, n * P:(n + 1) * P], xbc[:, n, c * P:(c + 1) * P], ident[:, :])
                    mm.then_inc(s_t1.sem, 1)

                chunk_tokens(0)
                for c in range(TB):
                    if c + 1 < TB:
                        chunk_tokens(c + 1)
                    pe.wait_ge(s_xw.sem, s_xw.until(l, c + 1))
                    if c >= 2:
                        pe.wait_ge(s_st.sem, s_st.until(l, c - 1))
                    for g in range(XT):
                        mm = t.matmul(ps[:, 4 + c % 2, 2 * g * P:2 * (g + 1) * P],
                                      xb_tok[c % 2][:, SSDW + g * P:SSDW + (g + 1) * P],
                                      xw[c % 2][:, :, 2 * g:2 * g + 2, :], start=True, stop=True)
                    mm.then_inc(s_stp.sem, 1)

                def decay_rows(c):
                    if c == 0:
                        pe.wait_ge(s_da.sem, s_da.until(l, 3))
                    if c == 1:
                        pe.wait_ge(s_tok.sem, s_tok.until(l, TB))
                    if c >= 2:
                        pe.wait_ge(s_seg.sem, s_seg.until(l, c - 1))
                        pe.wait_ge(s_er.sem, s_er.until(l, c - 1))
                    rows = pair(c % 2)
                    for n in range(2 * NH):
                        mm = t.matmul(rows[:, n * P:(n + 1) * P], a8[:, c, n:n + 1].broadcast_to([P, P]),
                                      (upto if n < NH else downto)[:, :], start=True, stop=True)
                    mm.then_inc(s_rows.sem, 1)

                def gram(c):
                    cols = slice(c * P, (c + 1) * P)
                    if c < 2:
                        pe.wait_ge(s_st.sem, s_st.until(l, TB))
                    else:
                        pe.wait_ge(s_xt.sem, s_xt.until(l, c - 1))
                        pe.wait_ge(s_m.sem, s_m.until(l, c - 1))
                    for g in range(XT):
                        t.matmul(ps[:, 4 + c % 2, g * P:(g + 1) * P], xbc[:, 2 + g, cols], xbc[:, 4 + g, cols],
                                 start=True, stop=True)
                    for g in range(XT):
                        mm = t.transpose(ps[:, 4 + c % 2, (2 + g) * P:(3 + g) * P], xbc[:, g, cols], ident[:, :])
                    mm.then_inc(s_gx.sem, 1)

                decay_rows(0)
                gram(0)
                for c in range(TB):
                    if c + 1 < TB:
                        decay_rows(c + 1)
                        gram(c + 1)
                    pe.wait_ge(s_m.sem, s_m.until(l, c + 1))
                    pe.wait_ge(s_xt.sem, s_xt.until(l, c + 1))
                    pe.wait_ge(s_cs.sem, s_cs.until(l, c + 1))
                    if c == 0:
                        pe.wait_ge(s_chain.sem, s_chain.until(l, 2 * (TB - 2)))
                    if c >= 2:
                        pe.wait_ge(s_yd.sem, s_yd.until(l, c - 1))
                    for h in range(NH):
                        g, hf = h // 2, h % 2
                        o = ps[64 * hf:64 * hf + 64, 6 + c % 2, g * P:(g + 1) * P]
                        cols = slice(hf * DQK, (hf + 1) * DQK)
                        parts = [(xb_tok[c % 2][:, h * DQK:(h + 1) * DQK], seg[:, 0, h, :])]
                        if c > 0:
                            parts.append((st[:, c - 1, g, 0, cols], erow[:, 0, h, :]))
                        if c < TB - 1:
                            parts.append((st[:, c + 1, g, 1, cols], erow[:, 1, h, :]))
                        for n, (w, m) in enumerate(parts):
                            mm = t.matmul(o, w, m, start=n == 0, stop=n == len(parts) - 1)
                    mm.then_inc(s_y.sem, 1)
                pe.wait_ge(s_ysq.sem, s_ysq.until(l, 1))
                for n in range(XT * TB):
                    mm = t.matmul(ps[:, 0, n:n + 1], sqs[:, n // TB, (n % TB) * P:(n % TB + 1) * P], ones[:, 0:1],
                                  start=True, stop=True)
                mm.then_inc(s_ysum.sem, 1)
                pe.wait_ge(s_ydg.sem, s_ydg.until(l, 1))
                for n in range(XT * TB):
                    cols = slice((n % TB) * P, (n % TB + 1) * P)
                    mm = t.matmul(pair(1 + n // TB)[:, cols], ones[:, :], sqs[:, n // TB, cols], start=True, stop=True)
                mm.then_inc(s_ynb.sem, 1)

                for n in range(len(GROUPS)):
                    for k in range(KT):
                        p = P_G + KT * n + k
                        pe.wait_ge(s_split.sem, s_split.until(l, p + 1))
                        if n == 0 and k == 0:
                            pe.wait_ge(s_yn.sem, s_yn.until(l, 1))
                        for b in range(TB):
                            if n and k == 0:
                                pe.wait_ge(s_ge.sem, s_ge.until(l, TB * (n - 1) + b + 1))
                            xh, xl = ahi[:, k, b * P:(b + 1) * P], alo[:, k, b * P:(b + 1) * P]
                            w_h, w_l = whi[p % RING][:, :], wlo[p % RING][:, :]
                            t.matmul(ps[:, b, :], xh, w_h, start=k == 0, stop=False)
                            t.matmul(ps[:, b, :], xh, w_l, start=False, stop=False)
                            mm = t.matmul(ps[:, b, :], xl, w_h, start=False, stop=k == KT - 1)
                            if k == KT - 1 and b < TB - 1:
                                mm.then_inc(s_g.sem, 1)
                        mm.then_inc(s_panel.sem, 1)
                for b in range(TB):
                    pe.wait_ge(s_kl.sem, s_kl.until(l, b + 1))
                    if b < 4:
                        pe.wait_ge(s_ge.sem, s_ge.until(l, TB * 2 + 2 * b + 2))
                    else:
                        pe.wait_ge(s_ks.sem, s_ks.until(l, b - 3))
                    for h in range(HC):
                        mm = t.transpose(pair(b % 4)[:, h * P:(h + 1) * P].bitcast(F32R),
                                         ksp[b % 2][:, h, :, :].rearrange("p a d -> p (a d)"), identr[:, :])
                    mm.then_inc(s_kt.sem, 1)

                with nc.tensor.Fori(0, HEADS) as hd:
                    it0 = hd * TB

                    def q_turn(j):
                        if j == 0:
                            pe.wait_ge(s_ks.sem, s_ks.until(l, TB))
                        pe.wait_ge(s_ql.sem, s_ql.until(l, it0 + j + 1))
                        pe.wait_ge(s_qs.sem, s_qs.until(l, it0 + j))
                        for n in range(4):
                            mm = t.transpose(ps[:, 6, n * P:(n + 1) * P].bitcast(F32R),
                                             qsp[j % 2][:, n // 2, n % 2, :, :].rearrange("p a d -> p (a d)"),
                                             identr[:, :])
                        mm.then_inc(s_qt.sem, 1)

                    def scores(j):
                        pe.wait_ge(s_qs.sem, s_qs.until(l, it0 + j + 1))
                        for c in range(2):
                            pe.wait_ge(s_e.sem, s_e.until(l, 2 * (it0 + j) - 1 + c))
                            for part in range(2):
                                for h in range(2):
                                    mm = t.matmul(half(c, h), qT[j % 2][:, c, part, :],
                                                  kst[:, bass.ds(hd * 2 + c, 1), h * HALF:(h + 1) * HALF]
                                                  .rearrange("p a n -> p (a n)"), start=part == 0, stop=part == 1)
                            mm.then_inc(s_s.sem, 1)

                    q_turn(0)
                    q_turn(1)
                    scores(0)
                    for j in range(TB):
                        if j + 2 < TB:
                            q_turn(j + 2)
                        if j + 1 < TB:
                            scores(j + 1)
                        pe.wait_ge(s_w.sem, s_w.until(l, it0 + j + 1))
                        pe.wait_ge(s_we.sem, s_we.until(l, it0 + j))
                        for b in range(TB):
                            mm = t.transpose(pair(2)[:, b * P:(b + 1) * P], W[j % 2][:, b * P:(b + 1) * P], ident[:, :])
                        mm.then_inc(s_wt.sem, 1)
                        pe.wait_ge(s_we.sem, s_we.until(l, it0 + j + 1))
                        pe.wait_ge(s_os.sem, s_os.until(l, it0 + j))
                        for b in range(TB):
                            mm = t.matmul(ps[:, 7, 0:DV], WT[j % 2][:, b, :], v_tok[:, b, bass.ds(hd * DV, DV)],
                                          start=b == 0, stop=b == TB - 1)
                        mm.then_inc(s_o.sem, 1)
                for h in range(HEADS):
                    pe.wait_ge(s_on.sem, s_on.until(l, h + 1))
                    for b in range(TB):
                        mm = t.transpose(pair(h)[:, b * P:(b + 1) * P], yn[:, h, b, :], ident[:, :])
                    mm.then_inc(s_ot.sem, 1)

                pe.wait_ge(s_yl.sem, s_yl.until(l, KT))
                for n in range(KT):
                    if n >= 4:
                        pe.wait_ge(s_res.sem, s_res.until(l, n - 3))
                    feature_tile(l, P_OUT + 2 * n, n % 4)

                norm(l, 1)

                def down_half(chunk, h, p, i=None):
                    for q in range(CH):
                        pe.wait_ge(s_split.sem, s_split.until(l, p + q + 1 if i is None else p + q + 1 + i * STEP))
                    for n in range(4):
                        m = 4 * h + n
                        if m < 4:
                            if i is None:
                                pe.wait_ge(s_dn.sem, s_dn.until(l, (NCH - 1) * KT - 4 + m + 1))
                            else:
                                pe.wait_ge(s_m3.sem, s_m3.until(l, 2 * CH * (i + 1) + n + 1))
                        else:
                            pe.wait_ge(s_dn.sem, s_dn.until(l, chunk * KT + m - 4 + 1))
                        for q in range(CH):
                            r = (p + q) % RING
                            mm = k_tile(halves(psum_down(m)), whi[r][:, n * P:(n + 1) * P],
                                        wlo[r][:, n * P:(n + 1) * P], mhi[:, q, :], mlo[:, q, :], q == 0, q == CH - 1)
                            if n == 3:
                                mm.then_inc(s_panel.sem, 1)
                        if n < 3:
                            mm.then_inc(s_dr.sem, 1)

                for n in range(2 * CH):
                    feature_tile(l, P_UP0 + 2 * n, (n + 2) % 4, ready=(s_hl, KT) if n == 0 else None)
                with nc.tensor.Fori(0, NCH - 1) as i:
                    for n in range(2 * CH):
                        pe.wait_ge(s_m3.sem, s_m3.until(l, 2 * CH * i + n + 1))
                        pe.wait_ge(s_dn.sem, s_dn.until(l, KT * i - 4 + n + 1))
                        feature_tile(l, P_BODY + 2 * n, (n + 2) % 4, i)
                    pe.wait_ge(s_ml.sem, s_ml.until(l, CH * (i + 1)))
                    for h in range(2):
                        down_half(i, h, P_BODY + UPN + h * CH, i)
                pe.wait_ge(s_ml.sem, s_ml.until(l, FT))
                for h in range(2):
                    down_half(NCH - 1, h, P_DN + h * CH)

            square_sums(L, 0)
            pe.wait_ge(s_ms.sem, s_ms.until(L, 1))
            for b in range(TB):
                if b >= 4:
                    pe.wait_ge(s_row, b - 3)
                for k in range(KT):
                    mm = t.transpose(pair(b % 4)[:, k * P:(k + 1) * P], xT[:, k, b * P:(b + 1) * P], ident[:, :])
                mm.then_inc(s_fin, 1)


_INS = ["x", "positions", "norm_mix_g", "w_in", "lam_q1", "lam_k1", "lam_q2", "lam_k2", "subln_g", "sc_conv_w",
        "ssd_conv_w", "ssd_conv_b", "ssd_dt_bias", "ssd_a_log", "ssd_d", "ssd_norm_g", "w_out",
        "norm_ffn_g", "w_up", "ffn_conv_w", "ffn_conv_b", "w_down", "final_norm_g"]


def kernel(**inputs):
    import numpy as np
    import concourse.bacc as bacc
    from concourse.bass_utils import run_bass_kernel_spmd

    nc = bacc.Bacc("TRN2", target_bir_lowering=False, num_devices=1)
    arrays, args = {}, []
    for name in _INS:
        a = np.ascontiguousarray(inputs[name])
        arrays[f"in_{name}"] = a
        args.append(nc.dram_tensor(f"in_{name}", a.shape, mybir.dt.from_np(a.dtype), kind="ExternalInput").ap())
    out = nc.dram_tensor("out", inputs["x"].shape, F32, kind="ExternalOutput").ap()
    build(nc, *args, out)
    r = run_bass_kernel_spmd(nc, [arrays], core_ids=[0])
    return r.results[0]["out"]
```

```python
import math
from contextlib import ExitStack

import numpy as np

import concourse.bass as bass
from concourse import mybir

F32 = mybir.dt.float32
F32R = mybir.dt.float32r
I32 = mybir.dt.int32
ALU = mybir.AluOpType
ACT = mybir.ActivationFunctionType
AX_X = mybir.AxisListType.X

P = 128
HALF = 512
EPS = 1e-5
ROPE_THETA = 500000.0
RING = 6
RAW = 3
LOOKAHEAD = 4
TWO_PI_PARTS = (6.28125, 1.93500518798828125e-3, 3.01991598196e-7)
PI_BELOW = 3.1415925
ROUND = 12582912.0


def build(nc, x, positions, norm_mix_g, w_in, lam_q1, lam_k1, lam_q2, lam_k2, subln_g, sc_conv_w,
          ssd_conv_w, ssd_conv_b, ssd_dt_bias, ssd_a_log, ssd_d, ssd_norm_g, w_out,
          norm_ffn_g, w_up, ffn_conv_w, ffn_conv_b, w_down, final_norm_g, out):
    _, S, D = x.shape
    L = w_in.shape[0]
    KT = D // P
    TB = S // P
    DQK = lam_q1.shape[1]
    DV = subln_g.shape[1]
    HEADS = 4
    ROT = DQK // 4
    R2 = ROT // 2
    HC = 2 * HEADS
    SCW = sc_conv_w.shape[2]
    SCT = SCW // P
    SSDW = ssd_norm_g.shape[1]
    XT = SSDW // P
    XBCT = ssd_conv_w.shape[2] // P
    NH = ssd_d.shape[1]
    FF = w_down.shape[1]
    FT = FF // P
    CH = 2
    NCH = FT // CH
    assert (S, D, DQK, DV, KT, TB, SCT, XT, XBCT, NH) == (1024, 1024, 64, 128, 8, 8, 2, 2, 6, 4)
    assert FT % CH == 0

    COL_Q, COL_K, COL_V, COL_SC = 0, HC * DQK, 2 * HC * DQK, 2 * HC * DQK + HEADS * DV
    COL_Z = COL_SC + 3 * SCW
    COL_XBC = COL_Z + SSDW
    COL_DT = COL_XBC + XBCT * P
    F_TILES = ([("xbc", t, COL_XBC + t * P) for t in range(XBCT)] + [("z", t, COL_Z + t * P) for t in range(XT)]
               + [(kind, t, COL_SC + n * SCW + t * P) for t in range(SCT) for kind, n in (("c", 1), ("h", 2), ("b", 0))])
    GROUPS = [("v", COL_V), ("q", COL_Q), ("k", COL_K)]
    MIXED = XBCT + XT
    SLOTS = [10, 6, 6, 6, 5, 5, 5, 5]
    assert len(SLOTS) == TB and sum(SLOTS) == (len(F_TILES) - MIXED) * KT
    P_DT = 0
    P_F = 4
    P_G = P_F + 2 * len(F_TILES)
    P_OUT = P_G + KT * len(GROUPS)
    P_UP0 = P_OUT + 2 * KT
    UPN = 4 * CH
    DNN = 2 * CH
    P_BODY = P_UP0 + UPN
    P_DN = P_BODY + (NCH - 1) * (UPN + DNN)
    PANELS = P_DN + DNN
    assert PANELS % RING == 0 and PANELS % RAW == 0 and (UPN + DNN) % RING == 0

    C_FW = [k * 2 * FT for k in range(3)]
    C_FB = 6 * FT
    C_G1 = 8 * FT
    C_G2 = C_G1 + KT
    C_XW = C_G2 + KT
    C_XB = C_XW + 3 * XBCT
    C_SW = C_XB + XBCT
    C_NG = C_SW + 3 * SCT
    C_SUB = C_NG + XT
    C_LAM = C_SUB + 1
    C_A = C_LAM + 1
    C_DTB = C_A + 2 * NH
    C_D = C_DTB + 2 * NH
    NPRM = C_D + XT
    INV_FREQ = [float(np.float32(ROPE_THETA) ** np.float32(-2.0 * j / ROT)) for j in range(R2)]
    LAM_INIT = [0.8 - 0.6 * math.exp(-0.3 * l) for l in range(L)]

    with ExitStack() as ctx:
        def sb(name, shape, dt=F32):
            return ctx.enter_context(nc.sbuf_tensor(name, shape, dt))

        def sem(name):
            return ctx.enter_context(nc.semaphore(name))

        xT = sb("xT", [P, KT, S])
        base_h = (nc.sbuf_base + 63) // 64 * 64
        slab_h = sb("slab_h", [P, base_h - nc.sbuf_base + 2 * KT * S * 4], mybir.dt.uint8)
        raw = [sb(f"raw{i}", [P, HALF]) for i in range(RAW)]
        whi = [sb(f"whi{i}", [P, HALF], F32R) for i in range(RING)]
        wlo = [sb(f"wlo{i}", [P, HALF], F32R) for i in range(RING)]
        ident = sb("ident", [P, P])
        identr = sb("identr", [P, P], F32R)
        ones = sb("ones", [P, P])
        upto = sb("upto", [P, P])
        downto = sb("downto", [P, P])
        capf = sb("capf", [P, P])
        capb = sb("capb", [P, P])
        prm = sb("prm", [P, L, NPRM])
        pc = sb("pc", [P, NPRM])
        cosT = sb("cosT", [P, TB, R2])
        sinT = sb("sinT", [P, TB, R2])
        small = sb("small", [P, 64])
        minus_half = sb("minus_half", [P, 32])
        rstd = sb("rstd", [P, 32])
        nmax = sb("nmax", [P, 2, 2])
        lsum = sb("lsum", [P, 2, 2])
        rlsum = sb("rlsum", [P, 4, 2])
        mix = sb("mix", [P, 2])
        ssq = sb("ssq", [P, HEADS * TB])

        base_a = (nc.sbuf_base + 63) // 64 * 64
        KB = 1024

        def region(base, limit):
            def at(name, offset, shape, dt=F32):
                n = 4
                for s in shape[1:]:
                    n *= s
                assert offset + n <= limit, name
                return nc.alloc_sbuf_tensor_at(name, shape, dt, offset=base + offset)
            return at

        h_at = region(base_h, 2 * KT * S * 4)
        a_at = region(base_a, 74 * KB)
        slab_a = sb("slab_a", [P, base_a - nc.sbuf_base + 74 * KB], mybir.dt.uint8)

        ahi = h_at("ahi", 0, [P, KT, S], F32R)
        alo = h_at("alo", 32 * KB, [P, KT, S], F32R)
        xin = h_at("xin", 0, [P, TB, D])
        kst = h_at("kst", 32 * KB, [P, HC, S], F32R)
        E = h_at("E", 0, [P, 2, 2, S])
        WT = [h_at(f"WT{i}", (20 + 4 * i) * KB, [P, TB, P]) for i in range(2)]
        q_tok = a_at("q_tok", 0, [P, TB, HEADS * DV])
        v_tok = a_at("v_tok", 16 * KB, [P, TB, HEADS * DV])
        o_tok = q_tok
        yc = a_at("yc", 48 * KB, [P, SCT, S])
        ys = a_at("ys", 56 * KB, [P, XT, S])
        ksp = [a_at(f"ksp{i}", (64 + 4 * i) * KB, [P, HC, 2, DQK], F32R) for i in range(2)]
        k_tok = a_at("k_tok", 32 * KB, [P, TB, HC * DQK])
        qsp = [a_at(f"qsp{i}", (32 + 2 * i) * KB, [P, 2, 2, 2, DQK], F32R) for i in range(2)]
        qT = [a_at(f"qT{i}", (36 + 2 * i) * KB, [P, 2, 2, P], F32R) for i in range(2)]
        W = [a_at(f"W{i}", (40 + 4 * i) * KB, [P, S]) for i in range(2)]
        yn = h_at("yn", 0, [P, HEADS, TB, P])
        xbc = a_at("xbc", 0, [P, XBCT, S])
        st = a_at("st", 24 * KB, [P, TB, XT, 2, P])
        cv = [a_at(f"cv{i}", (40 + 4 * i) * KB, [P, S]) for i in range(2)]
        seg = a_at("seg", 40 * KB, [P, 2, NH, P])
        erow = a_at("erow", 44 * KB, [P, 2, NH, P])
        xb_tok = [a_at(f"xb_tok{i}", (64 + 2 * i) * KB, [P, 4 * P]) for i in range(2)]
        xw = [a_at(f"xw{i}", (68 + 2 * i) * KB, [P, 2, NH, DQK]) for i in range(2)]
        dtT = a_at("dtT", 24 * KB, [8, S])
        rot = a_at("rot", 72 * KB, [P, 4, HC, R2])
        osq = a_at("osq", 64 * KB, [P, P])
        DW = TB * 2 * NH
        dtb_ = [a_at(f"dt{i}", 72 * KB + i * 4 * DW, [P, TB, 2 * NH]) for i in range(8)]
        DT_EXP, DT, DT_W, DT_DEC, DT_A, DT_CUM = (dtb_[i] for i in (2, 7, 0, 1, 4, 5))
        sqs = a_at("sqs", 40 * KB, [P, XT, S])
        acc = a_at("acc", 64 * KB, [P, S])
        sq = a_at("sq", 68 * KB, [P, S])
        ht = [a_at(f"ht{i}", (52 + 8 * i) * KB, [P, S]) for i in range(2)]
        mhi = a_at("mhi", 0, [P, CH, S], F32R)
        mlo = a_at("mlo", 8 * KB, [P, CH, S], F32R)
        tg = [a_at(f"tg{i}", (32 + 4 * i) * KB, [P, S]) for i in range(2)]
        tu = [a_at(f"tu{i}", (40 + 4 * i) * KB, [P, S]) for i in range(2)]
        stage = [[a_at(f"stage{l}{i}", (3 * l + i) * 512, [P, P]) for i in range(3)] for l in range(L)]
        lamv = a_at("lamv", 4 * KB, [P, 4, L, DQK])
        lamp = a_at("lamp", 8 * KB, [P, 2, L, DQK])
        lams = a_at("lams", 10 * KB, [P, 2, L])
        pos_i = a_at("pos_i", 11 * KB, [TB, P], I32)
        pos_f = a_at("pos_f", 11 * KB + 512, [TB, P])
        pos_c = a_at("pos_c", 12 * KB, [P, TB])
        ang = [a_at(f"ang{i}", 13 * KB + 256 * i, [P, TB, R2]) for i in range(3)]
        fg_row = a_at("fg_row", 16 * KB, [P, D])
        o_row = [a_at(f"o_row{i}", (20 + 4 * i) * KB, [P, D]) for i in range(2)]

        ps = ctx.enter_context(nc.psum_tensor("ps", [P, 8, HALF], F32))

        def pair(u):
            k = u % 4
            return ps[:, 2 * k:2 * k + 2, :].rearrange("p b n -> p (b n)")

        def pair(k):
            return ps[:, 2 * k:2 * k + 2, :].rearrange("p b n -> p (b n)")

        def half(k, h):
            return ps[:, 2 * k + h, :]

        class Count:

            def __init__(self, name, n, credit=0):
                self.sem, self.n, self.credit = ctx.enter_context(nc.semaphore(name)), n, credit

            def until(self, l, k):
                return l * self.n + k + self.credit

        s_raw = [sem(f"raw_loaded{i}") for i in range(RAW)]
        s_split = Count("panels_split", PANELS, RAW)
        s_hi = Count("panels_hi", PANELS)
        s_panel = Count("panels_used", PANELS, RING)

        s_setup = sem("setup_loaded")
        s_xin = sem("x_loaded")
        s_fg = sem("final_gain_loaded")
        s_const = sem("constants_made")
        s_pset = sem("setup_pe")
        s_aset = sem("setup_act")
        s_dset = sem("setup_dve")
        s_xt0 = sem("x_feature_major_pe")
        s_xt1 = sem("x_feature_major_stored")
        s_fin = sem("final_transposed")
        s_row = sem("final_row_ready")
        s_dlink = sem("setup_dve_steps")
        s_out = [sem(f"rows_stored{i}") for i in range(2)]

        s_sq = Count("squares_written", 2 * KT)
        s_acc = Count("squares_added", 2 * KT)
        s_nsum = Count("square_sums_ready", 2)
        s_ms = Count("mean_squares_ready", 2)
        s_rs = Count("rstd_ready", 2)
        s_dg = Count("rstd_diagonals_ready", 2)
        s_nb = Count("rstd_broadcast_ready", 2)
        s_ht = Count("normed_ready", 2 * KT)
        s_hh = Count("normed_hi_ready", 2 * KT)
        s_hl = Count("normed_lo_ready", 2 * KT)
        s_pc = Count("layer_parameters_ready", 1)

        s_c1 = Count("conv_centre_done", XBCT)
        s_c2 = Count("conv_left_done", XBCT)
        s_c3 = Count("conv_done", XBCT)
        s_xs = Count("xbc_ready", XBCT)
        s_z = Count("z_gate_ready", XT)
        s_sa = Count("short_conv_c_stored", SCT)
        s_sc = Count("short_conv_steps", 5 * SCT)
        s_dtp = Count("dt_feature_major_stored", 1)
        s_dtt = Count("dt_transposed", 1)

        STEP_A = 17
        DV_STEPS = STEP_A + 3
        s_dv = Count("dt_steps", DV_STEPS)
        s_da = Count("dt_exps", 3)
        s_cum = Count("cumulated", 1)
        s_t1 = Count("chunk_transposed", TB)
        s_tok = Count("chunk_position_major", TB)
        s_xw = Count("weighted_x_ready", TB)
        s_stp = Count("states_made", TB)
        s_st = Count("states_stored", TB)
        s_chain = Count("states_chained", 2 * (TB - 2))
        s_rows = Count("decay_rows_made", TB)
        s_gx = Count("gram_made", TB)
        s_seg = Count("segments_ready", TB)
        s_es = Count("segments_exped", TB)
        s_er = Count("rows_exped", TB)
        s_xt = Count("x_position_major", TB)
        s_cs = Count("scaled_c_ready", TB)
        s_mf = Count("decay_forward_done", TB)
        s_mb = Count("decay_both_done", TB)
        s_m = Count("ssd_matrix_ready", TB)
        s_y = Count("ssd_product_ready", TB)
        s_yd = Count("ssd_skip_added", TB)
        s_yz = Count("ssd_gated", TB)
        s_ysq = Count("ssd_squares_ready", 1)
        s_ysum = Count("ssd_square_sums_ready", 1)
        s_yms = Count("ssd_mean_squares_ready", 1)
        s_yrs = Count("ssd_rstd_ready", 1)
        s_ydg = Count("ssd_diagonals_ready", 1)
        s_ynb = Count("ssd_rstd_broadcast_ready", XT)
        s_yn = Count("ssd_output_ready", XT)

        s_g = Count("group_bank_ready", (TB - 1) * len(GROUPS))
        s_ge = Count("group_rows_stored", TB * len(GROUPS))
        s_ra = Count("rotary_products", 2 * TB)
        s_rb = Count("rotary_written", 2 * TB)
        s_kh = Count("k_hi_ready", TB)
        s_kl = Count("k_lo_ready", TB)
        s_kt = Count("k_transposed", TB)
        s_ks = Count("k_stack_ready", TB)

        ITS = HEADS * TB
        s_qh = Count("q_hi_split", ITS)
        s_ql = Count("q_lo_split", ITS)
        s_qt = Count("q_transposed", ITS, 2)
        s_qs = Count("q_stack_ready", ITS, 1)
        s_s = Count("scores_ready", 2 * ITS, 4)
        s_mx = Count("maxima_ready", 2 * ITS)
        s_e = Count("exps_ready", 2 * ITS, 2)
        s_rl = Count("sum_reciprocals_ready", ITS)
        s_cc = Count("mix_factor_ready", ITS)
        s_w = Count("weights_mixed", ITS, 2)
        s_wt = Count("weights_transposed", ITS, 2)
        s_we = Count("weights_key_major", ITS, 1)
        s_o = Count("head_product_ready", ITS, 2)
        s_oe = Count("head_output_stored", ITS, 1)
        s_os = Count("head_squares_summed", ITS, 4)
        s_oms = Count("head_mean_squares_ready", 1)
        s_ors = Count("head_rstd_ready", 1)
        s_on = Count("heads_normed", HEADS)
        s_ot = Count("heads_transposed", HEADS)
        s_yh = Count("outputs_hi_ready", KT)
        s_yl = Count("outputs_lo_ready", KT)

        s_res = Count("residual_added", KT)
        s_m1 = Count("mlp_centre_done", 2 * FT)
        s_m2 = Count("mlp_left_done", 2 * FT)
        s_m3 = Count("mlp_conv_done", 2 * FT)
        s_sg = Count("mlp_gate_ready", FT)
        s_mm = Count("mlp_product_ready", FT)
        s_mh = Count("mlp_hi_ready", FT)
        s_ml = Count("mlp_lo_ready", FT)
        s_dr = Count("down_tile_ready", NCH * (KT - 2))
        s_dn = Count("down_tile_added", NCH * KT, KT)

        STEP = UPN + DNN

        FIRST, LAST = -4, 3

        def pipeline(engine, period):
            for p in range(FIRST, LAST):
                period(0, p)
            with engine.Fori(0, HEADS - 1) as hd:
                for j in range(TB):
                    period(hd, j + LAST)
            for j in range(TB):
                period(HEADS - 1, j + LAST)

        def exists(hd, j):
            return not isinstance(hd, int) or 0 <= hd * TB + j < ITS

        def hi_of(act, l, p, i=None, width=HALF):
            at = p if i is None else p + i * STEP
            loads = p // RAW + 1 if i is None else p // RAW + 1 + i * (STEP // RAW)
            act.wait_ge(s_raw[p % RAW], (l * (PANELS // RAW) + loads) * 16)
            act.wait_ge(s_panel.sem, s_panel.until(l, at - RING + 1))
            nc.scalar.activation(whi[p % RING][:, 0:width], raw[p % RAW][:, 0:width], ACT.Copy).then_inc(s_hi.sem, 1)

        def lo_of(dve, l, p, i=None, width=HALF):
            at = p if i is None else p + i * STEP
            dve.wait_ge(s_hi.sem, s_hi.until(l, at + 1))
            nc.vector.tensor_tensor(wlo[p % RING][:, 0:width], raw[p % RAW][:, 0:width],
                                    whi[p % RING][:, 0:width].bitcast(F32), ALU.subtract).then_inc(s_split.sem, 1)

        def ahead(part_of, eng, l, p, i=None):
            q = p + LOOKAHEAD
            if q < PANELS:
                part_of(eng, l, q, i)
            else:
                part_of(eng, l + 1, q - PANELS, None, width=16)

        def psum_down(n):
            return (n + 2) % 4

        def f_pair(n):
            return n if n < 2 else 2 + n % 2

        def slot_panels(c):
            first = sum(SLOTS[:c])
            return [P_F + 2 * MIXED + u // 4 for u in range(first, first + SLOTS[c]) if u % 4 == 0]

        def slot_tiles(c):
            first = sum(SLOTS[:c])
            return [MIXED + u // KT for u in range(first, first + SLOTS[c]) if u % KT == KT - 1]

        block = ctx.enter_context(nc.Block())

        @block.sync
        def _(sp):
            n_setup = 0

            def setup(dst, src):
                sp.dma_start(dst, src).then_inc(s_setup, 16)

            sp.dma_start(xin[:, :, :], x[0].rearrange("(t p) d -> p t d", p=P)).then_inc(s_xin, 16)
            for l in range(L):
                a, b, c = stage[l]
                taps = [ffn_conv_w[l, k].rearrange("(t p) -> t p", p=P) for k in range(3)]
                setup(a[0:2 * FT, :], taps[0])
                setup(a[2 * FT:4 * FT, :], taps[1])
                setup(b[0:2 * FT, :], taps[2])
                setup(b[2 * FT:4 * FT, :], ffn_conv_b[l].rearrange("(t p) -> t p", p=P))
                r = 0
                for src in (norm_mix_g[l], norm_ffn_g[l], ssd_conv_w[l].rearrange("k c -> (k c)"), ssd_conv_b[l],
                            sc_conv_w[l].rearrange("k c -> (k c)"), ssd_norm_g[l], subln_g[l]):
                    rows = src.rearrange("(t p) -> t p", p=P)
                    setup(c[r:r + rows.shape[0], :], rows)
                    r += rows.shape[0]
                assert r == C_LAM - C_G1
                for n, v in enumerate((lam_q1, lam_k1, lam_q2, lam_k2)):
                    setup(lamv[:, n, l, :], v[l].partition_broadcast(P))
                setup(prm[:, l, C_A:C_A + 2 * NH], ssd_a_log[l].rearrange("d h -> (d h)").partition_broadcast(P))
                setup(prm[:, l, C_DTB:C_DTB + 2 * NH], ssd_dt_bias[l].rearrange("d h -> (d h)").partition_broadcast(P))
                for h in range(NH):
                    g, hf = h // 2, h % 2
                    setup(prm[64 * hf:64 * hf + 64, l, C_D + g:C_D + g + 1], ssd_d[l, h:h + 1].partition_broadcast(64))
            setup(pos_i[:, :], positions[0].rearrange("(t p) -> t p", p=P))

            w_in_t = w_in.rearrange("l (k p) n -> l p k n", p=P)
            w_out_t = w_out.rearrange("l (k p) n -> l p k n", p=P)
            w_up_t = w_up.rearrange("l (k p) n -> l p k n", p=P)

            def load(l, dst, src, p, i=None, also=False):
                sp.wait_ge(s_split.sem, s_split.until(l, (p if i is None else p + i * STEP) - RAW + 1 + also))
                sp.dma_start(dst, src).then_inc(s_raw[p % RAW], 16)

            def one(ap, l):
                return ap[bass.ds(l, 1)].rearrange("l p k n -> (l p) k n")

            def dt_slot(p):
                return raw[p % RAW][:, 0:16].rearrange("p (k n) -> p k n", n=8)

            def tiles_slot(p):
                return raw[p % RAW][:, :].rearrange("p (k c) -> p k c", c=P)

            def load_up(l, q, p, chunk, i=None):
                cols = bass.ds(chunk * (CH * P) + (q // 4) * P + ((q % 4) // 2) * FF, P)
                load(l, tiles_slot(p), one(w_up_t[:, :, 4 * (q % 2):4 * (q % 2) + 4, cols], l), p, i)

            def load_dn(l, q, p, chunk, i=None):
                src = w_down[bass.ds(l, 1), bass.ds(chunk * (CH * P) + (q % CH) * P, P),
                             (q // CH) * HALF:(q // CH + 1) * HALF].rearrange("l p n -> (l p) n")
                load(l, raw[p % RAW][:, :], src, p, i)

            with nc.sync.Fori(0, L) as l:
                for p in range(P_F):
                    load(l, dt_slot(p), one(w_in_t[:, :, 2 * p:2 * p + 2, COL_DT:COL_DT + 8], l), p)
                for n, (_, _, col) in enumerate(F_TILES):
                    for h in range(2):
                        p = P_F + 2 * n + h
                        load(l, tiles_slot(p), one(w_in_t[:, :, 4 * h:4 * h + 4, col:col + P], l), p)
                for n, (_, col) in enumerate(GROUPS):
                    for k in range(KT):
                        p = P_G + KT * n + k
                        dst = raw[p % RAW][:, :].rearrange("p (k n) -> p k n", k=1)
                        src = one(w_in_t[:, :, k:k + 1, col:col + HALF], l)
                        if col == k == 0:
                            sp.dma_start(dst, src).then_inc(s_raw[p % RAW], 16)
                            continue
                        load(l, dst, src, p, also=GROUPS[(n + 1) % len(GROUPS)][1] == 0 and k == KT - 1)
                for n in range(KT):
                    for h in range(2):
                        p = P_OUT + 2 * n + h
                        load(l, tiles_slot(p), one(w_out_t[:, :, 4 * h:4 * h + 4, n * P:(n + 1) * P], l), p)
                for q in range(UPN):
                    load_up(l, q, P_UP0 + q, 0)
                with nc.sync.Fori(0, NCH - 1) as i:
                    for q in range(UPN):
                        load_up(l, q, P_BODY + q, i + 1, i)
                    for q in range(DNN):
                        load_dn(l, q, P_BODY + UPN + q, i, i)
                for q in range(DNN):
                    load_dn(l, q, P_DN + q, NCH - 1)
            for p in range(LOOKAHEAD):
                sp.wait_ge(s_split.sem, s_split.until(L, p - RAW + 1))
                sp.dma_start(dt_slot(p), w_in_t[0, :, 2 * p:2 * p + 2, COL_DT:COL_DT + 8]).then_inc(s_raw[p % RAW], 16)
            sp.dma_start(fg_row[:, :], final_norm_g.partition_broadcast(P)).then_inc(s_fg, 16)
            for b in range(TB):
                sp.wait_ge(s_row, b + 1)
                sp.dma_start(out[0, b * P:(b + 1) * P, :], o_row[b % 2][:, :]).then_inc(s_out[b % 2], 16)
            for i in range(2):
                sp.wait_ge(s_out[i], 16 * (TB // 2))

        N_SETUP = 16 * (L * (4 + 7 + 4 + 2 + NH) + 1)

        @block.gpsimd
        def _(pool):
            g = nc.gpsimd
            g.memset(ident[:, :], 0.0).then_inc(s_const, 1)
            g.memset(ones[:, :], 1.0).then_inc(s_const, 1)
            g.memset(capf[:, :], 0.0).then_inc(s_const, 1)
            g.memset(capb[:, :], 0.0).then_inc(s_const, 1)
            g.memset(minus_half[:, :], -0.5).then_inc(s_const, 1)
            pool.wait_ge(s_const, 5)
            g.affine_select(out=ident[:, :], in_=ident[:, :], compare_op=ALU.not_equal, fill=1.0, base=0,
                            pattern=[[-1, P]], channel_multiplier=1).then_inc(s_const, 1)
            for dst, src, fill, sign in ((upto, ones, 0.0, 1), (downto, ones, 0.0, -1),
                                         (capf, capf, -1e30, 1), (capb, capb, -1e30, -1)):
                g.affine_select(out=dst[:, :], in_=src[:, :], compare_op=ALU.is_ge, fill=fill, base=0,
                                pattern=[[sign, P]], channel_multiplier=-sign).then_inc(s_const, 1)

            def power(c_in, c_out, l, k, n):
                pool.wait_ge(c_in.sem, c_in.until(l, k))
                g.tensor_tensor(rstd[:, 0:n], small[:, 0:n], minus_half[:, 0:n], ALU.pow).then_inc(c_out.sem, 1)

            def rotary(l, n, rows, b):
                v = rows[:, b, :].rearrange("p (h d) -> p h d", d=DQK)
                t1, t2 = v[:, :, 0:R2], v[:, :, R2:ROT]
                c = cosT[:, b:b + 1, :].broadcast_to([P, HC, R2])
                s = sinT[:, b:b + 1, :].broadcast_to([P, HC, R2])
                if n or b:
                    pool.wait_ge(s_rb.sem, s_rb.until(l, TB * n + b))
                pool.wait_ge(s_ge.sem, s_ge.until(l, TB * (n + 1) + b + 1))
                g.tensor_tensor(rot[:, 0, :, :], t1, c, ALU.mult)
                g.tensor_tensor(rot[:, 1, :, :], t2, s, ALU.mult)
                g.tensor_tensor(rot[:, 2, :, :], t2, c, ALU.mult)
                g.tensor_tensor(rot[:, 3, :, :], t1, s, ALU.mult).then_inc(s_ra.sem, 1)
                pool.wait_ge(s_ra.sem, s_ra.until(l, TB * n + b + 1))
                g.tensor_tensor(t1, rot[:, 0, :, :], rot[:, 1, :, :], ALU.subtract)
                g.tensor_tensor(t2, rot[:, 2, :, :], rot[:, 3, :, :], ALU.add).then_inc(s_rb.sem, 1)

            pool.wait_ge(s_aset, 3)
            with nc.gpsimd.Fori(0, L) as l:
                power(s_ms, s_rs, l, 1, TB)
                power(s_yms, s_yrs, l, 1, XT * TB)
                for n, rows in enumerate((q_tok, k_tok)):
                    for b in range(TB):
                        rotary(l, n, rows, b)

                def q_lo(hd, j):
                    src = q_tok[:, j % TB, bass.ds(hd * DV + j // TB * DV, DV)].rearrange("p (c d) -> p c d", d=DQK)
                    pool.wait_ge(s_qh.sem, s_qh.until(l, hd * TB + j + 1))
                    g.tensor_tensor(qsp[j % 2][:, :, 1, :, :], src.unsqueeze(2).broadcast_to([P, 2, 2, DQK]),
                                    qsp[j % 2][:, :, 0, :, :].bitcast(F32), ALU.subtract).then_inc(s_ql.sem, 1)

                def pool_period(hd, p):
                    if exists(hd, p + 4):
                        q_lo(hd, p + 4)

                pipeline(nc.gpsimd, pool_period)
                power(s_oms, s_ors, l, 1, ITS)
                power(s_ms, s_rs, l, 2, TB)
            power(s_ms, s_rs, L, 1, TB)

        @block.scalar
        def _(act):
            a = nc.scalar

            def square_tile(l, k):
                if isinstance(k, int) and k % KT >= 2:
                    act.wait_ge(s_acc.sem, s_acc.until(l, k - 1))
                a.activation((sq, ht[0])[k % 2][:, :], xT[:, k % KT, :], ACT.Square).then_inc(s_sq.sem, 1)

            def normed_hi(l, n):
                for k in range(KT):
                    act.wait_ge(s_ht.sem, s_ht.until(l, n * KT + k + 1))
                    a.activation(ahi[:, k, :], ht[k % 2][:, :], ACT.Copy).then_inc(s_hh.sem, 1)

            def col(c):
                return pc[:, c:c + 1]

            act.sem_inc(s_qs.sem, s_qs.credit)
            act.sem_inc(s_e.sem, s_e.credit)
            act.sem_inc(s_we.sem, s_we.credit)
            act.sem_inc(s_oe.sem, s_oe.credit)
            act.sem_inc(s_os.sem, s_os.credit)
            act.wait_ge(s_setup, N_SETUP)
            for l in range(L):
                a_log = prm[:, l, C_A:C_A + 2 * NH]
                last = a.activation(a_log, a_log, ACT.Exp)
            last.then_inc(s_aset, 1)
            act.wait_ge(s_dset, 1)
            a.activation(lams[:, :, :], lams[:, :, :], ACT.Exp).then_inc(s_aset, 1)
            act.wait_ge(s_dset, 3)
            a.activation(sinT[:, :, :], ang[0][:, :, :], ACT.Sin)
            a.activation(cosT[:, :, :], ang[1][:, :, :], ACT.Sin).then_inc(s_aset, 1)
            for k in range(KT):
                act.wait_ge(s_xt0, k + 1)
                a.activation(xT[:, k, :], pair(k % 4), ACT.Copy).then_inc(s_xt1, 1)
                act.wait_ge(s_xt1, k + 1)
                square_tile(0, k)
            for p in range(LOOKAHEAD):
                hi_of(act, 0, p, width=16)

            with nc.scalar.Fori(0, L) as l:
                normed_hi(l, 0)
                for p in range(P_F):
                    ahead(hi_of, act, l, p)
                act.wait_ge(s_panel.sem, s_panel.until(l, P_F))
                a.activation(dtT[:, :], pair(2)[0:8, :], ACT.Copy).then_inc(s_dtp.sem, 1)

                def silu_xbc(t):
                    act.wait_ge(s_c3.sem, s_c3.until(l, t + 1))
                    a.activation(xbc[:, t, :], cv[t % 2][:, :], ACT.Silu).then_inc(s_xs.sem, 1)

                for n in range(XBCT):
                    p = P_F + 2 * n
                    ahead(hi_of, act, l, p)
                    ahead(hi_of, act, l, p + 1)
                    if n == 2:
                        act.wait_ge(s_dv.sem, s_dv.until(l, 3))
                        a.activation(DT_EXP[:, :, :], DT_EXP[:, :, :], ACT.Exp, scale=-1.0).then_inc(s_da.sem, 1)
                    if n == 5:
                        act.wait_ge(s_dv.sem, s_dv.until(l, DV_STEPS - 1))
                        a.activation(DT_W[:, :, :], DT_W[:, :, :], ACT.Exp).then_inc(s_da.sem, 1)
                        a.activation(DT_DEC[:, :, :], ps[:, 3, DW:2 * DW].rearrange("p (t h) -> p t h", h=2 * NH),
                                     ACT.Exp).then_inc(s_da.sem, 1)
                    act.wait_ge(s_panel.sem, s_panel.until(l, p + 2))
                    if n >= 2:
                        act.wait_ge(s_xs.sem, s_xs.until(l, n - 1))
                    a.activation(cv[n % 2][:, :], pair(f_pair(n)), ACT.Identity, bias=col(C_XB + n),
                                 scale=col(C_XW + XBCT + n)).then_inc(s_c1.sem, 1)
                    if n:
                        silu_xbc(n - 1)
                silu_xbc(XBCT - 1)

                def store_tokens(c):
                    act.wait_ge(s_t1.sem, s_t1.until(l, c + 1))
                    if c >= 2:
                        act.wait_ge(s_stp.sem, s_stp.until(l, c - 1))
                        act.wait_ge(s_xw.sem, s_xw.until(l, c - 1))
                    a.activation(xb_tok[c % 2][:, :], ps[:, c % 2, :], ACT.Copy).then_inc(s_tok.sem, 1)

                def store_states(c):
                    act.wait_ge(s_stp.sem, s_stp.until(l, c + 1))
                    a.activation(st[:, c, :, :, :].rearrange("p g d n -> p (g d n)"), ps[:, 2 + c % 2, :],
                                 ACT.Copy).then_inc(s_st.sem, 1)

                store_tokens(0)
                store_tokens(1)
                for h in range(2 * XT):
                    ahead(hi_of, act, l, P_F + 2 * XBCT + h)
                    for c in (2 * h, 2 * h + 1):
                        store_states(c)
                        if c + 2 < TB:
                            store_tokens(c + 2)
                    if h % 2:
                        act.wait_ge(s_panel.sem, s_panel.until(l, P_F + 2 * XBCT + h + 1))
                        a.activation(ys[:, h // 2, :], pair(f_pair(XBCT + h // 2)), ACT.Silu).then_inc(s_z.sem, 1)

                for c in range(TB):
                    if c:
                        act.wait_ge(s_y.sem, s_y.until(l, c))
                    act.wait_ge(s_rows.sem, s_rows.until(l, c + 1))
                    a.activation(erow[:, :, :, :].rearrange("p d h l -> p (d h l)"), pair(0),
                                 ACT.Exp).then_inc(s_er.sem, 1)
                    act.wait_ge(s_gx.sem, s_gx.until(l, c + 1))
                    a.activation(xb_tok[c % 2][:, 0:SSDW], ps[:, 2, SSDW:2 * SSDW], ACT.Copy).then_inc(s_xt.sem, 1)
                    act.wait_ge(s_seg.sem, s_seg.until(l, c + 1))
                    a.activation(seg[:, :, :, :], seg[:, :, :, :], ACT.Exp).then_inc(s_es.sem, 1)
                    for p in slot_panels(c):
                        ahead(hi_of, act, l, p)
                    for n in slot_tiles(c):
                        kind, t, _ = F_TILES[n]
                        if kind == "c":
                            act.wait_ge(s_panel.sem, s_panel.until(l, P_F + 2 * n + 2))
                            a.activation(yc[:, t, :], pair(f_pair(n)), ACT.Copy).then_inc(s_sa.sem, 1)

                for n, (kind, _) in enumerate(GROUPS):
                    for k in range(KT):
                        ahead(hi_of, act, l, P_G + KT * n + k)
                        if n == k == 0:
                            act.wait_ge(s_yz.sem, s_yz.until(l, TB))
                            a.activation(sqs[:, :, :], ys[:, :, :], ACT.Square).then_inc(s_ysq.sem, 1)
                    for b in range(TB):
                        if b < TB - 1:
                            act.wait_ge(s_g.sem, s_g.until(l, (TB - 1) * n + b + 1))
                        else:
                            act.wait_ge(s_panel.sem, s_panel.until(l, P_G + KT * (n + 1)))
                        dst = {"v": v_tok, "q": q_tok, "k": k_tok}[kind]
                        a.activation(dst[:, b, :], ps[:, b, :], ACT.Copy,
                                     scale=DQK ** -0.5 if kind == "q" else 1.0).then_inc(s_ge.sem, 1)

                def store_stack(b):
                    act.wait_ge(s_kt.sem, s_kt.until(l, b + 1))
                    a.activation(kst[:, :, b * P:(b + 1) * P], pair(b % 4).rearrange("p (h n) -> p h n", n=P),
                                 ACT.Copy).then_inc(s_ks.sem, 1)

                for b in range(TB + 1):
                    if b < TB:
                        act.wait_ge(s_rb.sem, s_rb.until(l, TB + b + 1))
                        if b >= 2:
                            act.wait_ge(s_kt.sem, s_kt.until(l, b - 1))
                        a.activation(ksp[b % 2][:, :, 0, :], k_tok[:, b, :].rearrange("p (h d) -> p h d", d=DQK),
                                     ACT.Copy).then_inc(s_kh.sem, 1)
                    if b:
                        store_stack(b - 1)

                def q_stack(hd, j):
                    it = hd * TB + j
                    act.wait_ge(s_qt.sem, s_qt.until(l, it + 1))
                    act.wait_ge(s_s.sem, s_s.until(l, 2 * it - 2))
                    a.activation(qT[j % 2][:, :, :, :].rearrange("p c s q -> p (c s q)"), ps[:, 6, :],
                                 ACT.Copy).then_inc(s_qs.sem, 1)

                def head_output(hd, j):
                    it = hd * TB + j
                    act.wait_ge(s_o.sem, s_o.until(l, it + 1))
                    act.wait_ge(s_rl.sem, s_rl.until(l, it + 1))
                    r0 = rlsum[:, j % 4, 0:1]
                    a.activation(o_tok[:, j % TB, bass.ds(hd * DV + j // TB * DV, DV)], ps[:, 7, 0:DV], ACT.Copy,
                                 scale=r0).then_inc(s_oe.sem, 1)
                    a.activation(osq[:, :], ps[:, 7, 0:DV], ACT.Square, scale=r0,
                                 accum_out=ssq[:, bass.ds(it, 1)]).then_inc(s_os.sem, 1)

                def exps(hd, j):
                    it = hd * TB + j
                    act.wait_ge(s_w.sem, s_w.until(l, it - 1))
                    for c in range(2):
                        act.wait_ge(s_mx.sem, s_mx.until(l, 2 * it + c + 1))
                        a.activation(E[:, j % 2, c, :], pair(c), ACT.Exp, bias=nmax[:, j % 2, c:c + 1],
                                     accum_out=lsum[:, j % 2, c:c + 1]).then_inc(s_e.sem, 1)

                def store_weights(hd, j):
                    it = hd * TB + j
                    act.wait_ge(s_wt.sem, s_wt.until(l, it + 1))
                    act.wait_ge(s_o.sem, s_o.until(l, it - 1))
                    a.activation(WT[j % 2][:, :, :].rearrange("p b q -> p (b q)"), pair(2),
                                 ACT.Copy).then_inc(s_we.sem, 1)

                def act_period(hd, p):
                    if exists(hd, p + 2):
                        q_stack(hd, p + 2)
                    if exists(hd, p - 3):
                        head_output(hd, p - 3)
                    if exists(hd, p + 1):
                        exps(hd, p + 1)
                    if exists(hd, p - 1):
                        store_weights(hd, p - 1)

                pipeline(nc.scalar, act_period)

                for t, src in enumerate((yc[:, 0, :], yc[:, 1, :], ys[:, 0, :], ys[:, 1, :])):
                    if t == 0:
                        act.wait_ge(s_on.sem, s_on.until(l, 1))
                    a.activation(ahi[:, HEADS + t, :], src, ACT.Copy).then_inc(s_yh.sem, 1)
                for h in range(HEADS):
                    act.wait_ge(s_ot.sem, s_ot.until(l, h + 1))
                    if h == 0:
                        act.wait_ge(s_ot.sem, s_ot.until(l, HEADS))
                    a.activation(ahi[:, h, :], pair(h), ACT.Identity, bias=0.0, scale=col(C_SUB)).then_inc(s_yh.sem, 1)

                for n in range(KT):
                    ahead(hi_of, act, l, P_OUT + 2 * n)
                    ahead(hi_of, act, l, P_OUT + 2 * n + 1)
                    act.wait_ge(s_res.sem, s_res.until(l, n + 1))
                    square_tile(l, KT + n)

                normed_hi(l, 1)

                def centre(n, tile, j, up):
                    c = up * FT + j
                    if isinstance(c, int):
                        b, w = col(C_FB + c), col(C_FW[1] + c)
                    else:
                        b, w = pc[:, bass.ds(C_FB + c, 1)], pc[:, bass.ds(C_FW[1] + c, 1)]
                    a.activation(tile[:, :], pair((n + 2) % 4), ACT.Identity, bias=b, scale=w).then_inc(s_m1.sem, 1)

                def gate(k, j):
                    act.wait_ge(s_m3.sem, s_m3.until(l, 2 * k + 2))
                    a.activation(tg[j][:, :], tg[j][:, :], ACT.Silu).then_inc(s_sg.sem, 1)

                def product_hi(k, slot, j):
                    act.wait_ge(s_mm.sem, s_mm.until(l, k + 1))
                    a.activation(mhi[:, slot, :], tg[j][:, :], ACT.Copy).then_inc(s_mh.sem, 1)

                def up_chunk(chunk, p0, i=None):
                    for n in range(2 * CH):
                        j, up = n // 2, n % 2
                        ahead(hi_of, act, l, p0 + 2 * n, i)
                        ahead(hi_of, act, l, p0 + 2 * n + 1, i)
                        at = p0 + 2 * n + 2 if i is None else p0 + 2 * n + 2 + i * STEP
                        act.wait_ge(s_panel.sem, s_panel.until(l, at))
                        if i is not None and up == 0:
                            act.wait_ge(s_ml.sem, s_ml.until(l, (chunk - 1) * CH + j + 1))
                        centre(n, (tg, tu)[up][j], chunk * CH + j, up)
                        if n == 2:
                            gate(chunk * CH, 0)

                def products(chunk, slot):
                    gate(chunk * CH + 1, 1)
                    product_hi(chunk * CH, slot, 0)
                    product_hi(chunk * CH + 1, slot + 1, 1)

                up_chunk(0, P_UP0)
                products(0, 0)
                with nc.scalar.Fori(0, NCH - 1) as i:
                    up_chunk(i + 1, P_BODY, i)
                    for q in range(DNN):
                        ahead(hi_of, act, l, P_BODY + UPN + q, i)
                        if q == 0:
                            gate((i + 1) * CH + 1, 1)
                    act.wait_ge(s_panel.sem, s_panel.until(l, P_BODY + UPN + DNN + i * STEP))
                    product_hi((i + 1) * CH, 0, 0)
                    product_hi((i + 1) * CH + 1, 1, 1)
                for q in range(DNN):
                    ahead(hi_of, act, l, P_DN + q)
                for n in range(KT):
                    act.wait_ge(s_dn.sem, s_dn.until(l, (NCH - 1) * KT + n + 1))
                    square_tile(l + 1, n)

        @block.vector
        def _(dve):
            v = nc.vector
            links = [0]

            def link(ins, value=None):
                links[0] += 1
                ins.then_inc(s_dlink, 1)
                dve.wait_ge(s_dlink, links[0])

            def col(c):
                return pc[:, c:c + 1]

            def add_squares(l, k):
                src = (sq, ht[0])[k % 2]
                dve.wait_ge(s_sq.sem, s_sq.until(l, k + 1))
                if k % KT == 0:
                    v.tensor_copy(acc[:, :], src[:, :]).then_inc(s_acc.sem, 1)
                else:
                    dve.wait_ge(s_acc.sem, s_acc.until(l, k))
                    v.tensor_tensor(acc[:, :], acc[:, :], src[:, :], ALU.add).then_inc(s_acc.sem, 1)

            def mean_squares(l, n):
                dve.wait_ge(s_nsum.sem, s_nsum.until(l, n + 1))
                v.tensor_scalar(small[:, 0:TB], ps[:, 0, 0:TB], 1.0 / D, EPS, ALU.mult, ALU.add).then_inc(s_ms.sem, 1)

            def diagonals(l, n, c_rs, c_dg, dst, count):
                dve.wait_ge(c_rs.sem, c_rs.until(l, n + 1))
                for b in range(count):
                    last = v.tensor_scalar(dst(b), ident[:, :], rstd[:, b:b + 1], None, ALU.mult)
                last.then_inc(c_dg.sem, 1)

            def norm(l, n, gain):
                mean_squares(l, n)
                diagonals(l, n, s_rs, s_dg, lambda b: sq[:, b * P:(b + 1) * P], TB)
                dve.wait_ge(s_nb.sem, s_nb.until(l, n + 1))

                def lo(k):
                    dve.wait_ge(s_hh.sem, s_hh.until(l, n * KT + k + 1))
                    v.tensor_tensor(alo[:, k, :], ht[k % 2][:, :], ahi[:, k, :].bitcast(F32),
                                    ALU.subtract).then_inc(s_hl.sem, 1)

                for k in range(KT):
                    if k >= 2:
                        dve.wait_ge(s_hl.sem, s_hl.until(l, n * KT + k - 1))
                    v.scalar_tensor_tensor(out=ht[k % 2][:, :], in0=xT[:, k, :], scalar=col(gain + k), in1=pair(1),
                                           op0=ALU.mult, op1=ALU.mult).then_inc(s_ht.sem, 1)
                    if k:
                        lo(k - 1)
                lo(KT - 1)

            def taps(l, dst, src, w0, w2, c_mid, c_end, k):
                v.scalar_tensor_tensor(out=dst[:, 1:S], in0=src[:, 0:S - 1], scalar=w0, in1=dst[:, 1:S],
                                       op0=ALU.mult, op1=ALU.add).then_inc(c_mid.sem, 1)
                dve.wait_ge(c_mid.sem, c_mid.until(l, k))
                v.scalar_tensor_tensor(out=dst[:, 0:S - 1], in0=src[:, 1:S], scalar=w2, in1=dst[:, 0:S - 1],
                                       op0=ALU.mult, op1=ALU.add).then_inc(c_end.sem, 1)

            dve.sem_inc(s_split.sem, s_split.credit)
            dve.sem_inc(s_w.sem, s_w.credit)
            dve.sem_inc(s_dn.sem, s_dn.credit)
            dve.wait_ge(s_const, 10)
            link(v.tensor_copy(identr[:, :], ident[:, :]))
            dve.wait_ge(s_setup, N_SETUP)
            link(v.tensor_copy(pos_f[:, :], pos_i[:, :]))
            v.tensor_tensor(lamp[:, :, :, :], lamv[:, 0:4:2, :, :], lamv[:, 1:4:2, :, :], ALU.mult).then_inc(s_dlink, 1)
            links[0] += 1
            dve.wait_ge(s_dlink, links[0])
            v.tensor_reduce(lams[:, :, :], lamp[:, :, :, :], AX_X, ALU.add).then_inc(s_dset, 1)
            dve.wait_ge(s_pset, 2 * 3 + 1)
            for l in range(L):
                at = 0
                for i, n in enumerate((4 * FT, 4 * FT, C_LAM - C_G1)):
                    link(v.tensor_copy(prm[:, l, at:at + n], ps[:, 3 * l + i, 0:n]))
                    at += n
                sub = prm[:, l, C_SUB:C_SUB + 1]
                link(v.tensor_scalar(sub, sub, 1.0 - LAM_INIT[l], None, ALU.mult))
            dve.wait_ge(s_aset, 1)
            for l in range(L):
                a_row = prm[:, l, C_A:C_A + 2 * NH]
                link(v.tensor_scalar(a_row, a_row, -1.0, None, ALU.mult))
            dve.wait_ge(s_aset, 2)
            for l in range(L):
                m = prm[:, l, C_LAM:C_LAM + 1]
                link(v.tensor_tensor(m, lams[:, 1, l:l + 1], lams[:, 0, l:l + 1], ALU.subtract))
                link(v.tensor_scalar(m, m, -LAM_INIT[l], None, ALU.add))
            link(v.tensor_copy(pos_c[:, :], ps[:, 6, 0:TB]))
            for j in range(R2):
                link(v.tensor_scalar(ang[0][:, :, j], pos_c[:, :], INV_FREQ[j], None, ALU.mult))
            link(v.tensor_scalar(ang[1][:, :, :], ang[0][:, :, :], 1.0 / (2 * math.pi), ROUND, ALU.mult, ALU.add))
            link(v.tensor_scalar(ang[1][:, :, :], ang[1][:, :, :], -ROUND, None, ALU.add))
            for part in TWO_PI_PARTS:
                link(v.scalar_tensor_tensor(out=ang[0][:, :, :], in0=ang[1][:, :, :], scalar=-part,
                                            in1=ang[0][:, :, :], op0=ALU.mult, op1=ALU.add))
            link(v.tensor_scalar(ang[0][:, :, :], ang[0][:, :, :], PI_BELOW, -PI_BELOW, ALU.min, ALU.max))
            link(v.scalar_tensor_tensor(out=ang[2][:, :, :], in0=ang[0][:, :, :], scalar=-1.0, in1=ang[0][:, :, :],
                                        op0=ALU.mult, op1=ALU.max))
            v.tensor_scalar(ang[1][:, :, :], ang[2][:, :, :], -1.0, math.pi / 2, ALU.mult,
                            ALU.add).then_inc(s_dset, 2)
            for k in range(KT):
                add_squares(0, k)
            for p in range(LOOKAHEAD):
                lo_of(dve, 0, p, width=16)

            with nc.vector.Fori(0, L) as l:
                v.tensor_copy(pc[:, :], prm[:, bass.ds(l, 1), :].rearrange("p a n -> p (a n)")).then_inc(s_pc.sem, 1)
                dve.wait_ge(s_pc.sem, s_pc.until(l, 1))
                norm(l, 0, C_G1)
                for p in range(P_F):
                    ahead(lo_of, dve, l, p)

                def dstep(ins):
                    steps[0] += 1
                    ins.then_inc(s_dv.sem, 1)
                    dve.wait_ge(s_dv.sem, s_dv.until(l, steps[0]))

                steps = [0]

                def by_block(c):
                    return pc[:, c:c + 2 * NH].unsqueeze(1).broadcast_to([P, TB, 2 * NH])

                d = [t[:, :, :] for t in dtb_]
                for n in range(XBCT):
                    p = P_F + 2 * n
                    ahead(lo_of, dve, l, p)
                    ahead(lo_of, dve, l, p + 1)
                    if n == 5:
                        dve.wait_ge(s_da.sem, s_da.until(l, 2))
                        dstep(v.tensor_tensor(DT_W[:, :, :], DT_W[:, :, :], d[7], ALU.mult))
                        assert steps[0] == DV_STEPS
                    dve.wait_ge(s_c1.sem, s_c1.until(l, n + 1))
                    taps(l, cv[n % 2], pair(f_pair(n)), col(C_XW + n), col(C_XW + 2 * XBCT + n), s_c2, s_c3, n + 1)
                    if n == 0:
                        dve.wait_ge(s_dtt.sem, s_dtt.until(l, 1))
                        dstep(v.tensor_tensor(dtb_[0][:, :, :], ps[:, 6, 0:DW].rearrange("p (t h) -> p t h", h=2 * NH),
                                              by_block(C_DTB), ALU.add))
                    if n == 1:
                        dstep(v.tensor_scalar(d[1], d[0], 0.0, None, ALU.max))
                        dstep(v.scalar_tensor_tensor(out=d[2], in0=d[0], scalar=-1.0, in1=d[0], op0=ALU.mult,
                                                     op1=ALU.max))
                    if n == 2:
                        dve.wait_ge(s_da.sem, s_da.until(l, 1))
                        dstep(v.tensor_scalar(d[3], d[2], 2.0, None, ALU.add))
                        dstep(v.reciprocal(d[4], d[3]))
                        dstep(v.tensor_tensor(d[5], d[2], d[4], ALU.mult))
                        dstep(v.tensor_tensor(d[6], d[5], d[5], ALU.mult))
                        dstep(v.tensor_scalar(d[3], d[6], 1.0 / 15, None, ALU.mult))
                        for m in (13, 11, 9, 7, 5, 3):
                            dstep(v.scalar_tensor_tensor(out=d[3], in0=d[3], scalar=1.0 / m, in1=d[6], op0=ALU.add,
                                                         op1=ALU.mult))
                        dstep(v.scalar_tensor_tensor(out=d[4], in0=d[3], scalar=1.0, in1=d[5], op0=ALU.add,
                                                     op1=ALU.mult))
                        dstep(v.scalar_tensor_tensor(out=d[7], in0=d[4], scalar=2.0, in1=d[1], op0=ALU.mult,
                                                     op1=ALU.add))
                        dstep(v.tensor_tensor(DT_A[:, :, :], d[7], by_block(C_A), ALU.mult))
                        assert steps[0] == STEP_A
                    if n == 4:
                        dve.wait_ge(s_cum.sem, s_cum.until(l, 1))
                        q4 = DW // 2
                        v.tensor_copy(DT_CUM[:, :, 0:NH], ps[:, 3, 0:q4].rearrange("p (t h) -> p t h", h=NH))
                        dstep(v.tensor_copy(DT_CUM[:, :, NH:2 * NH],
                                            ps[:, 3, q4:DW].rearrange("p (t h) -> p t h", h=NH)))
                        total = ps[:, 3, DW:2 * DW].rearrange("p (t h) -> p t h", h=2 * NH)
                        dstep(v.tensor_tensor(DT_W[:, :, :], total, DT_CUM[:, :, :], ALU.subtract))

                for c in range(TB):
                    dve.wait_ge(s_tok.sem, s_tok.until(l, c + 1))
                    if c >= 2:
                        dve.wait_ge(s_stp.sem, s_stp.until(l, c - 1))
                    x4 = xb_tok[c % 2][:, 0:SSDW].rearrange("p (h d) -> p h d", h=NH)
                    for dr in range(2):
                        w4 = DT_W[:, c, dr * NH:(dr + 1) * NH].unsqueeze(2).broadcast_to([P, NH, DQK])
                        last = v.tensor_tensor(xw[c % 2][:, dr, :, :], x4, w4, ALU.mult)
                    last.then_inc(s_xw.sem, 1)
                    if c % 2:
                        ahead(lo_of, dve, l, P_F + 2 * XBCT + c // 2)

                def chain_states():
                    dve.wait_ge(s_st.sem, s_st.until(l, TB))
                    dve.wait_ge(s_da.sem, s_da.until(l, 3))
                    for n in range(1, TB - 1):
                        for dr in range(2):
                            c, prev = (n, n - 1) if dr == 0 else (TB - 1 - n, TB - n)
                            if n > 1:
                                dve.wait_ge(s_chain.sem, s_chain.until(l, 2 * (n - 1) - 1 + dr))
                            for h in range(NH):
                                g, hf = h // 2, h % 2
                                cols = slice(hf * DQK, (hf + 1) * DQK)
                                last = v.scalar_tensor_tensor(
                                    out=st[:, c, g, dr, cols], in0=st[:, prev, g, dr, cols],
                                    scalar=DT_DEC[:, c, dr * NH + h:dr * NH + h + 1], in1=st[:, c, g, dr, cols],
                                    op0=ALU.mult, op1=ALU.add)
                            last.then_inc(s_chain.sem, 1)

                def short_conv(n):
                    kind, t, _ = F_TILES[n]
                    h_tile = pair(f_pair(n))
                    if kind == "h":
                        dve.wait_ge(s_sa.sem, s_sa.until(l, t + 1))
                        dve.wait_ge(s_panel.sem, s_panel.until(l, P_F + 2 * n + 2))
                        v.tensor_tensor(h_tile, h_tile, yc[:, t, :], ALU.mult).then_inc(s_sc.sem, 1)
                        dve.wait_ge(s_sc.sem, s_sc.until(l, 5 * t + 1))
                        v.tensor_scalar(yc[:, t, :], h_tile, col(C_SW + SCT + t), None, ALU.mult).then_inc(s_sc.sem, 1)
                        for w, (dst, src) in ((t, (slice(1, S), slice(0, S - 1))),
                                              (2 * SCT + t, (slice(0, S - 1), slice(1, S)))):
                            k = 5 * t + (2 if w == t else 3)
                            dve.wait_ge(s_sc.sem, s_sc.until(l, k))
                            v.scalar_tensor_tensor(out=yc[:, t, dst], in0=h_tile[:, src], scalar=col(C_SW + w),
                                                   in1=yc[:, t, dst], op0=ALU.mult, op1=ALU.add).then_inc(s_sc.sem, 1)
                    elif kind == "b":
                        dve.wait_ge(s_panel.sem, s_panel.until(l, P_F + 2 * n + 2))
                        dve.wait_ge(s_sc.sem, s_sc.until(l, 5 * t + 4))
                        v.tensor_tensor(yc[:, t, :], pair(f_pair(n)), yc[:, t, :], ALU.mult).then_inc(s_sc.sem, 1)

                def skip_and_gate(c):
                    cols = slice(c * P, (c + 1) * P)
                    dve.wait_ge(s_y.sem, s_y.until(l, c + 1))
                    for g in range(XT):
                        last = v.scalar_tensor_tensor(out=xbc[:, g, cols], in0=xbc[:, g, cols], scalar=col(C_D + g),
                                                      in1=ps[:, 3, g * P:(g + 1) * P],
                                                      op0=ALU.mult, op1=ALU.add)
                    last.then_inc(s_yd.sem, 1)
                    dve.wait_ge(s_yd.sem, s_yd.until(l, c + 1))
                    v.tensor_tensor(ys[:, :, cols], xbc[:, 0:XT, cols], ys[:, :, cols], ALU.mult).then_inc(s_yz.sem, 1)

                dve.wait_ge(s_z.sem, s_z.until(l, XT))
                for c in range(TB):
                    dve.wait_ge(s_er.sem, s_er.until(l, c + 1))
                    if c:
                        dve.wait_ge(s_y.sem, s_y.until(l, c))
                    rows = pair(0).rearrange("p (d h l) -> p d h l", d=2, h=NH)
                    for dr, cap in ((0, capf), (1, capb)):
                        for h in range(NH):
                            last = v.scalar_tensor_tensor(out=seg[:, dr, h, :], in0=rows[:, dr, h, :],
                                                          scalar=DT_CUM[:, c, dr * NH + h:dr * NH + h + 1],
                                                          in1=cap[:, :], op0=ALU.subtract, op1=ALU.min)
                    last.then_inc(s_seg.sem, 1)
                    for g in range(XT):
                        cT = xbc[:, 4 + g:5 + g, c * P:(c + 1) * P].unsqueeze(1).broadcast_to([P, 2, 2, P])
                        e4 = erow[:, :, 2 * g:2 * g + 2, :]
                        last = v.tensor_tensor(e4, e4, cT, ALU.mult)
                    last.then_inc(s_cs.sem, 1)
                    if c:
                        skip_and_gate(c - 1)
                    else:
                        chain_states()
                    dve.wait_ge(s_es.sem, s_es.until(l, c + 1))
                    for h in range(NH):
                        last = v.tensor_scalar(seg[:, 0, h, :], seg[:, 0, h, :], DT[:, c, h:h + 1], None, ALU.mult)
                    last.then_inc(s_mf.sem, 1)
                    dve.wait_ge(s_mf.sem, s_mf.until(l, c + 1))
                    for h in range(NH):
                        last = v.scalar_tensor_tensor(out=seg[:, 0, h, :], in0=seg[:, 1, h, :],
                                                      scalar=DT[:, c, NH + h:NH + h + 1], in1=seg[:, 0, h, :],
                                                      op0=ALU.mult, op1=ALU.add)
                    last.then_inc(s_mb.sem, 1)
                    dve.wait_ge(s_mb.sem, s_mb.until(l, c + 1))
                    dve.wait_ge(s_xt.sem, s_xt.until(l, c + 1))
                    for g in range(XT):
                        gram = ps[:, 2, g * P:(g + 1) * P].unsqueeze(1).broadcast_to([P, 2, P])
                        m = seg[:, 0, 2 * g:2 * g + 2, :]
                        last = v.tensor_tensor(m, gram, m, ALU.mult)
                    last.then_inc(s_m.sem, 1)
                    for p in slot_panels(c):
                        ahead(lo_of, dve, l, p)
                    for n in slot_tiles(c):
                        short_conv(n)
                skip_and_gate(TB - 1)

                for p in range(P_G, P_OUT):
                    ahead(lo_of, dve, l, p)
                    if p == P_G + KT:
                        dve.wait_ge(s_ysum.sem, s_ysum.until(l, 1))
                        v.tensor_scalar(small[:, 0:XT * TB], ps[:, 7, 0:XT * TB], 1.0 / P, EPS, ALU.mult,
                                        ALU.add).then_inc(s_yms.sem, 1)
                        diagonals(l, 0, s_yrs, s_ydg, lambda b: sqs[:, b // TB, (b % TB) * P:(b % TB + 1) * P], XT * TB)
                    if p == P_G + 2 * KT:
                        for g in range(XT):
                            dve.wait_ge(s_ynb.sem, s_ynb.until(l, g + 1))
                            v.scalar_tensor_tensor(out=ys[:, g, :], in0=ys[:, g, :], scalar=col(C_NG + g),
                                                   in1=pair(2 + g), op0=ALU.mult, op1=ALU.mult).then_inc(s_yn.sem, 1)
                for b in range(TB):
                    dve.wait_ge(s_kh.sem, s_kh.until(l, b + 1))
                    rows = k_tok[:, b, :].rearrange("p (h d) -> p h d", d=DQK)
                    v.tensor_tensor(ksp[b % 2][:, :, 1, :], rows, ksp[b % 2][:, :, 0, :].bitcast(F32),
                                    ALU.subtract).then_inc(s_kl.sem, 1)

                def q_hi(hd, j):
                    it = hd * TB + j
                    dve.wait_ge(s_qt.sem, s_qt.until(l, it - 1))
                    src = q_tok[:, j % TB, bass.ds(hd * DV + j // TB * DV, DV)].rearrange("p (c d) -> p c d", d=DQK)
                    v.tensor_copy(qsp[j % 2][:, :, 0, :, :], src.unsqueeze(2).broadcast_to([P, 2, 2, DQK])
                                  ).then_inc(s_qh.sem, 1)

                def maxima(hd, j):
                    for c in range(2):
                        dve.wait_ge(s_s.sem, s_s.until(l, 2 * (hd * TB + j) + c + 1))
                        v.tensor_reduce(nmax[:, j % 2, c:c + 1], pair(c), AX_X, ALU.max,
                                        negate=True).then_inc(s_mx.sem, 1)

                def mix_weights(hd, j):
                    it = hd * TB + j
                    dve.wait_ge(s_e.sem, s_e.until(l, 2 * it + 2))
                    dve.wait_ge(s_os.sem, s_os.until(l, it - 3))
                    v.reciprocal(rlsum[:, j % 4, :], lsum[:, j % 2, :]).then_inc(s_rl.sem, 1)
                    dve.wait_ge(s_rl.sem, s_rl.until(l, it + 1))
                    v.scalar_tensor_tensor(out=mix[:, j % 2:j % 2 + 1], in0=lsum[:, j % 2, 0:1],
                                           scalar=rlsum[:, j % 4, 1:2], in1=col(C_LAM), op0=ALU.mult,
                                           op1=ALU.mult).then_inc(s_cc.sem, 1)
                    dve.wait_ge(s_cc.sem, s_cc.until(l, it + 1))
                    dve.wait_ge(s_wt.sem, s_wt.until(l, it - 1))
                    v.scalar_tensor_tensor(out=W[j % 2][:, :], in0=E[:, j % 2, 1, :],
                                           scalar=mix[:, j % 2:j % 2 + 1], in1=E[:, j % 2, 0, :],
                                           op0=ALU.mult, op1=ALU.add).then_inc(s_w.sem, 1)

                def dve_period(hd, p):
                    if exists(hd, p + 4):
                        q_hi(hd, p + 4)
                    if exists(hd, p + 1):
                        maxima(hd, p + 1)
                    if exists(hd, p):
                        mix_weights(hd, p)

                pipeline(nc.vector, dve_period)

                dve.wait_ge(s_os.sem, s_os.until(l, ITS))
                v.tensor_scalar(small[:, 0:ITS], ssq[:, :], 1.0 / DV, EPS, ALU.mult, ALU.add).then_inc(s_oms.sem, 1)
                dve.wait_ge(s_ors.sem, s_ors.until(l, 1))
                for h in range(HEADS):
                    for b in range(TB):
                        last = v.tensor_scalar(yn[:, h, b, :], o_tok[:, b, h * DV:(h + 1) * DV],
                                               rstd[:, h * TB + b:h * TB + b + 1], None, ALU.mult)
                    last.then_inc(s_on.sem, 1)
                for t, src in enumerate((yc[:, 0, :], yc[:, 1, :], ys[:, 0, :], ys[:, 1, :])):
                    dve.wait_ge(s_yh.sem, s_yh.until(l, t + 1))
                    v.tensor_tensor(alo[:, HEADS + t, :], src, ahi[:, HEADS + t, :].bitcast(F32),
                                    ALU.subtract).then_inc(s_yl.sem, 1)
                for h in range(HEADS):
                    dve.wait_ge(s_yh.sem, s_yh.until(l, HEADS + h + 1))
                    v.scalar_tensor_tensor(out=alo[:, h, :], in0=pair(h), scalar=col(C_SUB),
                                           in1=ahi[:, h, :].bitcast(F32), op0=ALU.mult,
                                           op1=ALU.subtract).then_inc(s_yl.sem, 1)

                for n in range(KT):
                    ahead(lo_of, dve, l, P_OUT + 2 * n)
                    ahead(lo_of, dve, l, P_OUT + 2 * n + 1)
                    dve.wait_ge(s_panel.sem, s_panel.until(l, P_OUT + 2 * n + 2))
                    v.tensor_tensor(xT[:, n, :], pair(n % 4), xT[:, n, :], ALU.add).then_inc(s_res.sem, 1)
                    if n:
                        add_squares(l, KT + n - 1)
                add_squares(l, 2 * KT - 1)

                norm(l, 1, C_G2)

                def conv(n, j, up, k):
                    c = up * FT + j
                    w0, w2 = ((col(C_FW[0] + c), col(C_FW[2] + c)) if isinstance(c, int) else
                              (pc[:, bass.ds(C_FW[0] + c, 1)], pc[:, bass.ds(C_FW[2] + c, 1)]))
                    dve.wait_ge(s_m1.sem, s_m1.until(l, k))
                    taps(l, (tg, tu)[up][n // 2], pair((n + 2) % 4), w0, w2, s_m2, s_m3, k)

                def up_chunk(chunk, p0, i=None):
                    for n in range(2 * CH):
                        ahead(lo_of, dve, l, p0 + 2 * n, i)
                        ahead(lo_of, dve, l, p0 + 2 * n + 1, i)
                        conv(n, chunk * CH + n // 2, n % 2, 2 * CH * chunk + n + 1)

                def product(k, j):
                    dve.wait_ge(s_sg.sem, s_sg.until(l, k + 1))
                    v.tensor_tensor(tg[j][:, :], tg[j][:, :], tu[j][:, :], ALU.mult).then_inc(s_mm.sem, 1)

                def product_lo(k, j):
                    dve.wait_ge(s_mh.sem, s_mh.until(l, k + 1))
                    v.tensor_tensor(mlo[:, j, :], tg[j][:, :], mhi[:, j, :].bitcast(F32),
                                    ALU.subtract).then_inc(s_ml.sem, 1)

                def add_down(chunk, n, p, i=None):
                    if n % 4 == 3:
                        dve.wait_ge(s_panel.sem, s_panel.until(l, p + 1 if i is None else p + 1 + i * STEP))
                    else:
                        dve.wait_ge(s_dr.sem, s_dr.until(l, chunk * (KT - 2) + (n // 4) * 3 + n % 4 + 1))
                    v.tensor_tensor(xT[:, n, :], pair(psum_down(n)), xT[:, n, :], ALU.add).then_inc(s_dn.sem, 1)

                up_chunk(0, P_UP0)
                product(0, 0)
                product(1, 1)
                product_lo(0, 0)
                product_lo(1, 1)
                with nc.vector.Fori(0, NCH - 1) as i:
                    up_chunk(i + 1, P_BODY, i)
                    product((i + 1) * CH, 0)
                    for h in range(2):
                        for q in range(CH):
                            ahead(lo_of, dve, l, P_BODY + UPN + h * CH + q, i)
                        for n in range(4 * h, 4 * h + 4):
                            add_down(i, n, P_BODY + UPN + h * CH + CH - 1, i)
                        if h == 0:
                            product((i + 1) * CH + 1, 1)
                    product_lo((i + 1) * CH, 0)
                    product_lo((i + 1) * CH + 1, 1)
                for h in range(2):
                    for q in range(CH):
                        ahead(lo_of, dve, l, P_DN + h * CH + q)
                    for n in range(4 * h, 4 * h + 4):
                        add_down(NCH - 1, n, P_DN + h * CH + CH - 1)
                        if n:
                            add_squares(l + 1, n - 1)
                add_squares(l + 1, KT - 1)

            mean_squares(L, 0)
            dve.wait_ge(s_rs.sem, s_rs.until(L, 1))
            dve.wait_ge(s_fg, 16)
            for b in range(TB):
                dve.wait_ge(s_fin, b + 1)
                if b >= 2:
                    dve.wait_ge(s_out[b % 2], 16 * (b // 2))
                v.scalar_tensor_tensor(out=o_row[b % 2][:, :], in0=pair(b % 4), scalar=rstd[:, b:b + 1],
                                       in1=fg_row[:, :], op0=ALU.mult, op1=ALU.mult).then_inc(s_row, 1)

        @block.tensor
        def _(pe):
            t = nc.tensor

            def k_tile(outs, w_hi, w_lo, xhi, xlo, first, last):
                for h in range(2):
                    t.matmul(outs[h], w_hi, xhi[:, h * HALF:(h + 1) * HALF], start=first, stop=False)
                for h in range(2):
                    t.matmul(outs[h], w_hi, xlo[:, h * HALF:(h + 1) * HALF], start=False, stop=False)
                for h in range(2):
                    mm = t.matmul(outs[h], w_lo, xhi[:, h * HALF:(h + 1) * HALF], start=False, stop=last)
                return mm

            def halves(k, rows=P):
                return [ps[0:rows, 2 * k + h, :] for h in range(2)]

            def k_tile_of(l, p, k, kt, i=None):
                h, j = kt // 4, kt % 4
                n = (p + h) % RING
                if j == 0:
                    at = p + h if i is None else p + h + i * STEP
                    pe.wait_ge(s_split.sem, s_split.until(l, at + 1))
                mm = k_tile(halves(k), whi[n][:, j * P:(j + 1) * P], wlo[n][:, j * P:(j + 1) * P],
                            ahi[:, kt, :], alo[:, kt, :], kt == 0, kt == KT - 1)
                if j == 3:
                    mm.then_inc(s_panel.sem, 1)

            def feature_tile(l, p, k, i=None, ready=None):
                for kt in range(KT):
                    if ready is not None:
                        pe.wait_ge(ready[0].sem, ready[0].until(l, ready[1] + kt + 1))
                    k_tile_of(l, p, k, kt, i)

            def square_sums(l, n):
                pe.wait_ge(s_acc.sem, s_acc.until(l, n * KT + KT))
                for b in range(TB):
                    mm = t.matmul(ps[:, 0, b:b + 1], acc[:, b * P:(b + 1) * P], ones[:, 0:1], start=True, stop=True)
                mm.then_inc(s_nsum.sem, 1)

            def norm(l, n):
                square_sums(l, n)
                pe.wait_ge(s_dg.sem, s_dg.until(l, n + 1))
                for b in range(TB):
                    mm = t.matmul(pair(1)[:, b * P:(b + 1) * P], ones[:, :], sq[:, b * P:(b + 1) * P],
                                  start=True, stop=True)
                mm.then_inc(s_nb.sem, 1)

            pe.sem_inc(s_panel.sem, s_panel.credit)
            pe.sem_inc(s_qt.sem, s_qt.credit)
            pe.sem_inc(s_s.sem, s_s.credit)
            pe.sem_inc(s_wt.sem, s_wt.credit)
            pe.sem_inc(s_o.sem, s_o.credit)
            pe.wait_ge(s_const, 10)
            pe.wait_ge(s_setup, N_SETUP)
            for l in range(L):
                for i, n in enumerate((4 * FT, 4 * FT, C_LAM - C_G1)):
                    t.transpose(ps[:, 3 * l + i, 0:n], stage[l][i][0:n, :], ident[0:n, 0:n]).then_inc(s_pset, 1)
            pe.wait_ge(s_dlink, 2)
            t.transpose(ps[:, 6, 0:TB], pos_f[:, :], ident[0:TB, 0:TB]).then_inc(s_pset, 1)
            pe.wait_ge(s_dset, 3)
            pe.wait_ge(s_xin, 16)
            for k in range(KT):
                if k >= 4:
                    pe.wait_ge(s_xt1, k - 3)
                for b in range(TB):
                    mm = t.transpose(pair(k % 4)[:, b * P:(b + 1) * P], xin[:, b, k * P:(k + 1) * P], ident[:, :])
                mm.then_inc(s_xt0, 1)

            with nc.tensor.Fori(0, L) as l:
                norm(l, 0)

                for p in range(P_F):
                    pe.wait_ge(s_split.sem, s_split.until(l, p + 1))
                    for j in range(2):
                        kt = 2 * p + j
                        pe.wait_ge(s_hl.sem, s_hl.until(l, kt + 1))
                        mm = k_tile(halves(2, 8), whi[p % RING][:, 8 * j:8 * j + 8], wlo[p % RING][:, 8 * j:8 * j + 8],
                                    ahi[:, kt, :], alo[:, kt, :], kt == 0, kt == KT - 1)
                    mm.then_inc(s_panel.sem, 1)

                free = [(s_c3, n + 1) for n in range(XBCT)] + [(s_z, n + 1) for n in range(XT)]
                for i in range(SCT):
                    free += [(s_sa, i + 1), (s_sc, 5 * i + 4), (s_sc, 5 * i + 5)]

                def pair_free(n):
                    if n == 2:
                        pe.wait_ge(s_dtp.sem, s_dtp.until(l, 1))
                    elif n == 3:
                        pe.wait_ge(s_dv.sem, s_dv.until(l, 1))
                    elif n >= 4:
                        reader, count = free[n - 2]
                        pe.wait_ge(reader.sem, reader.until(l, count))

                def mixed(first, last):
                    for u in range(first, last):
                        n, kt = MIXED + u // KT, u % KT
                        if kt == 0:
                            pair_free(n)
                        k_tile_of(l, P_F + 2 * n, f_pair(n), kt)

                a8 = DT_A
                for n in range(XBCT):
                    pair_free(n)
                    feature_tile(l, P_F + 2 * n, f_pair(n))
                    if n == 0:
                        pe.wait_ge(s_dtp.sem, s_dtp.until(l, 1))
                        for b in range(TB):
                            mm = t.matmul(ps[:, 6, b * 8:b * 8 + 8], dtT[:, b * P:(b + 1) * P], ident[0:8, 0:8],
                                          start=True, stop=True)
                        mm.then_inc(s_dtt.sem, 1)
                    if n == 4:
                        pe.wait_ge(s_dv.sem, s_dv.until(l, STEP_A))
                        pe.wait_ge(s_c3.sem, s_c3.until(l, 2))
                        q4 = DW // 2
                        t.matmul(ps[:, 3, 0:q4], upto[:, :], a8[:, :, 0:NH], start=True, stop=True)
                        t.matmul(ps[:, 3, q4:DW], downto[:, :], a8[:, :, NH:2 * NH], start=True, stop=True)
                        t.matmul(ps[:, 3, DW:2 * DW], ones[:, :], a8[:, :, :], start=True, stop=True).then_inc(s_cum.sem, 1)

                pe.wait_ge(s_xs.sem, s_xs.until(l, 4))

                def chunk_tokens(c):
                    if c >= 2:
                        pe.wait_ge(s_tok.sem, s_tok.until(l, c - 1))
                    for n in range(4):
                        mm = t.transpose(ps[:, c % 2, n * P:(n + 1) * P], xbc[:, n, c * P:(c + 1) * P], ident[:, :])
                    mm.then_inc(s_t1.sem, 1)

                def chunk_states(c):
                    pe.wait_ge(s_xw.sem, s_xw.until(l, c + 1))
                    if c == 0:
                        pe.wait_ge(s_da.sem, s_da.until(l, 3))
                    if c >= 2:
                        pe.wait_ge(s_st.sem, s_st.until(l, c - 1))
                    for g in range(XT):
                        mm = t.matmul(ps[:, 2 + c % 2, 2 * g * P:2 * (g + 1) * P],
                                      xb_tok[c % 2][:, SSDW + g * P:SSDW + (g + 1) * P],
                                      xw[c % 2][:, :, 2 * g:2 * g + 2, :], start=True, stop=True)
                    mm.then_inc(s_stp.sem, 1)

                chunk_tokens(0)
                chunk_tokens(1)
                for h in range(2 * XT):
                    n = XBCT + h // 2
                    if h % 2 == 0:
                        pair_free(n)
                    for kt in range(4 * (h % 2), 4 * (h % 2) + 4):
                        k_tile_of(l, P_F + 2 * n, f_pair(n), kt)
                    for c in (2 * h, 2 * h + 1):
                        chunk_states(c)
                        if c + 2 < TB:
                            chunk_tokens(c + 2)

                def decay_rows(c):
                    if c == 0:
                        pe.wait_ge(s_tok.sem, s_tok.until(l, TB))
                    else:
                        pe.wait_ge(s_seg.sem, s_seg.until(l, c))
                        pe.wait_ge(s_er.sem, s_er.until(l, c))
                    for n in range(2 * NH):
                        mm = t.matmul(pair(0)[:, n * P:(n + 1) * P], a8[:, c, n:n + 1].broadcast_to([P, P]),
                                      (upto if n < NH else downto)[:, :], start=True, stop=True)
                    mm.then_inc(s_rows.sem, 1)

                def gram(c):
                    cols = slice(c * P, (c + 1) * P)
                    if c == 0:
                        pe.wait_ge(s_xs.sem, s_xs.until(l, XBCT))
                        pe.wait_ge(s_st.sem, s_st.until(l, TB))
                    else:
                        pe.wait_ge(s_xt.sem, s_xt.until(l, c))
                        pe.wait_ge(s_m.sem, s_m.until(l, c))
                    for g in range(XT):
                        t.matmul(ps[:, 2, g * P:(g + 1) * P], xbc[:, 2 + g, cols], xbc[:, 4 + g, cols],
                                 start=True, stop=True)
                    for g in range(XT):
                        mm = t.transpose(ps[:, 2, (2 + g) * P:(3 + g) * P], xbc[:, g, cols], ident[:, :])
                    mm.then_inc(s_gx.sem, 1)

                decay_rows(0)
                gram(0)
                for c in range(TB):
                    mixed(sum(SLOTS[:c]), sum(SLOTS[:c + 1]))
                    if c + 1 < TB:
                        decay_rows(c + 1)
                        gram(c + 1)
                    pe.wait_ge(s_m.sem, s_m.until(l, c + 1))
                    pe.wait_ge(s_xt.sem, s_xt.until(l, c + 1))
                    pe.wait_ge(s_cs.sem, s_cs.until(l, c + 1))
                    if c == 0:
                        pe.wait_ge(s_chain.sem, s_chain.until(l, 2 * (TB - 2)))
                    else:
                        pe.wait_ge(s_yd.sem, s_yd.until(l, c))
                    for h in range(NH):
                        g, hf = h // 2, h % 2
                        o = ps[64 * hf:64 * hf + 64, 3, g * P:(g + 1) * P]
                        cols = slice(hf * DQK, (hf + 1) * DQK)
                        parts = [(xb_tok[c % 2][:, h * DQK:(h + 1) * DQK], seg[:, 0, h, :])]
                        if c > 0:
                            parts.append((st[:, c - 1, g, 0, cols], erow[:, 0, h, :]))
                        if c < TB - 1:
                            parts.append((st[:, c + 1, g, 1, cols], erow[:, 1, h, :]))
                        for n, (w, m) in enumerate(parts):
                            mm = t.matmul(o, w, m, start=n == 0, stop=n == len(parts) - 1)
                    mm.then_inc(s_y.sem, 1)

                def ssd_square_sums():
                    pe.wait_ge(s_ysq.sem, s_ysq.until(l, 1))
                    pe.wait_ge(s_ge.sem, s_ge.until(l, TB))
                    for n in range(XT * TB):
                        mm = t.matmul(ps[:, 7, n:n + 1], sqs[:, n // TB, (n % TB) * P:(n % TB + 1) * P],
                                      ones[:, 0:1], start=True, stop=True)
                    mm.then_inc(s_ysum.sem, 1)

                def ssd_broadcast():
                    pe.wait_ge(s_ydg.sem, s_ydg.until(l, 1))
                    pe.wait_ge(s_ge.sem, s_ge.until(l, 2 * TB))
                    for g in range(XT):
                        for b in range(TB):
                            cols = slice(b * P, (b + 1) * P)
                            mm = t.matmul(pair(2 + g)[:, cols], ones[:, :], sqs[:, g, cols], start=True, stop=True)
                        mm.then_inc(s_ynb.sem, 1)

                for n in range(len(GROUPS)):
                    for k in range(KT):
                        p = P_G + KT * n + k
                        pe.wait_ge(s_split.sem, s_split.until(l, p + 1))
                        if n == 1 and k == 0:
                            ssd_square_sums()
                        for b in range(TB):
                            if n == 0 and k == 0 and b == 3:
                                pe.wait_ge(s_yd.sem, s_yd.until(l, TB))
                            if n == 0 and k == 0 and b == 4:
                                pe.wait_ge(s_sc.sem, s_sc.until(l, 5 * SCT - 1))
                            if n == 0 and k == 0 and b == 6:
                                pe.wait_ge(s_sc.sem, s_sc.until(l, 5 * SCT))
                            if n and k == 0:
                                pe.wait_ge(s_ge.sem, s_ge.until(l, TB * (n - 1) + b + 1))
                            if n == 1 and k == 0 and b == 7:
                                pe.wait_ge(s_yms.sem, s_yms.until(l, 1))
                            if n == 2 and k == 0 and b == 4:
                                ssd_broadcast()
                            if n == 2 and k == 0 and b % 2 == 0 and b >= 4:
                                pe.wait_ge(s_yn.sem, s_yn.until(l, b // 2 - 1))
                            xh, xl = ahi[:, k, b * P:(b + 1) * P], alo[:, k, b * P:(b + 1) * P]
                            w_h, w_l = whi[p % RING][:, :], wlo[p % RING][:, :]
                            t.matmul(ps[:, b, :], xh, w_h, start=k == 0, stop=False)
                            t.matmul(ps[:, b, :], xh, w_l, start=False, stop=False)
                            mm = t.matmul(ps[:, b, :], xl, w_h, start=False, stop=k == KT - 1)
                            if k == KT - 1 and b < TB - 1:
                                mm.then_inc(s_g.sem, 1)
                        mm.then_inc(s_panel.sem, 1)
                for b in range(TB):
                    pe.wait_ge(s_kl.sem, s_kl.until(l, b + 1))
                    if b < 4:
                        pe.wait_ge(s_ge.sem, s_ge.until(l, TB * 2 + 2 * b + 2))
                    else:
                        pe.wait_ge(s_ks.sem, s_ks.until(l, b - 3))
                    for h in range(HC):
                        mm = t.transpose(pair(b % 4)[:, h * P:(h + 1) * P].bitcast(F32R),
                                         ksp[b % 2][:, h, :, :].rearrange("p a d -> p (a d)"), identr[:, :])
                    mm.then_inc(s_kt.sem, 1)

                def q_turn(hd, j):
                    it = hd * TB + j
                    if isinstance(hd, int) and it == 0:
                        pe.wait_ge(s_ks.sem, s_ks.until(l, TB))
                    pe.wait_ge(s_ql.sem, s_ql.until(l, it + 1))
                    pe.wait_ge(s_qs.sem, s_qs.until(l, it))
                    for n in range(4):
                        mm = t.transpose(ps[:, 6, n * P:(n + 1) * P].bitcast(F32R),
                                         qsp[j % 2][:, n // 2, n % 2, :, :].rearrange("p a d -> p (a d)"),
                                         identr[:, :])
                    mm.then_inc(s_qt.sem, 1)

                def scores(hd, j):
                    it = hd * TB + j
                    pe.wait_ge(s_qs.sem, s_qs.until(l, it + 1))
                    for c in range(2):
                        pe.wait_ge(s_e.sem, s_e.until(l, 2 * it - 1 + c))
                        for part in range(2):
                            for h in range(2):
                                mm = t.matmul(half(c, h), qT[j % 2][:, c, part, :],
                                              kst[:, bass.ds(hd * 2 + (j // TB * 2 + c), 1), h * HALF:(h + 1) * HALF]
                                              .rearrange("p a n -> p (a n)"), start=part == 0, stop=part == 1)
                        mm.then_inc(s_s.sem, 1)

                def turn_weights(hd, j):
                    it = hd * TB + j
                    pe.wait_ge(s_w.sem, s_w.until(l, it + 1))
                    pe.wait_ge(s_we.sem, s_we.until(l, it))
                    for b in range(TB):
                        mm = t.transpose(pair(2)[:, b * P:(b + 1) * P], W[j % 2][:, b * P:(b + 1) * P], ident[:, :])
                    mm.then_inc(s_wt.sem, 1)

                def weigh_v(hd, j):
                    it = hd * TB + j
                    pe.wait_ge(s_we.sem, s_we.until(l, it + 1))
                    pe.wait_ge(s_os.sem, s_os.until(l, it))
                    for b in range(TB):
                        mm = t.matmul(ps[:, 7, 0:DV], WT[j % 2][:, b, :],
                                      v_tok[:, b, bass.ds(hd * DV + j // TB * DV, DV)],
                                      start=b == 0, stop=b == TB - 1)
                    mm.then_inc(s_o.sem, 1)

                def pe_period(hd, p):
                    if exists(hd, p + 1):
                        scores(hd, p + 1)
                    if exists(hd, p - 1):
                        turn_weights(hd, p - 1)
                    if exists(hd, p - 2):
                        weigh_v(hd, p - 2)
                    if exists(hd, p + 3):
                        q_turn(hd, p + 3)

                pipeline(nc.tensor, pe_period)
                for h in range(HEADS):
                    pe.wait_ge(s_on.sem, s_on.until(l, h + 1))
                    for b in range(TB):
                        mm = t.transpose(pair(h)[:, b * P:(b + 1) * P], yn[:, h, b, :], ident[:, :])
                    mm.then_inc(s_ot.sem, 1)

                pe.wait_ge(s_yl.sem, s_yl.until(l, KT))
                for n in range(KT):
                    if n >= 4:
                        pe.wait_ge(s_res.sem, s_res.until(l, n - 3))
                    feature_tile(l, P_OUT + 2 * n, n % 4)

                norm(l, 1)

                def down_half(chunk, h, p, i=None):
                    for q in range(CH):
                        pe.wait_ge(s_split.sem, s_split.until(l, p + q + 1 if i is None else p + q + 1 + i * STEP))
                    for n in range(4):
                        m = 4 * h + n
                        if m < 4:
                            if i is None:
                                pe.wait_ge(s_dn.sem, s_dn.until(l, (NCH - 1) * KT - 4 + m + 1))
                            else:
                                pe.wait_ge(s_m3.sem, s_m3.until(l, 2 * CH * (i + 1) + n + 1))
                        else:
                            pe.wait_ge(s_dn.sem, s_dn.until(l, chunk * KT + m - 4 + 1))
                        for q in range(CH):
                            r = (p + q) % RING
                            mm = k_tile(halves(psum_down(m)), whi[r][:, n * P:(n + 1) * P],
                                        wlo[r][:, n * P:(n + 1) * P], mhi[:, q, :], mlo[:, q, :], q == 0, q == CH - 1)
                            if n == 3:
                                mm.then_inc(s_panel.sem, 1)
                        if n < 3:
                            mm.then_inc(s_dr.sem, 1)

                for n in range(2 * CH):
                    feature_tile(l, P_UP0 + 2 * n, (n + 2) % 4, ready=(s_hl, KT) if n == 0 else None)
                with nc.tensor.Fori(0, NCH - 1) as i:
                    for n in range(2 * CH):
                        pe.wait_ge(s_m3.sem, s_m3.until(l, 2 * CH * i + n + 1))
                        pe.wait_ge(s_dn.sem, s_dn.until(l, KT * i - 4 + n + 1))
                        feature_tile(l, P_BODY + 2 * n, (n + 2) % 4, i)
                    pe.wait_ge(s_ml.sem, s_ml.until(l, CH * (i + 1)))
                    for h in range(2):
                        down_half(i, h, P_BODY + UPN + h * CH, i)
                pe.wait_ge(s_ml.sem, s_ml.until(l, FT))
                for h in range(2):
                    down_half(NCH - 1, h, P_DN + h * CH)

            square_sums(L, 0)
            pe.wait_ge(s_ms.sem, s_ms.until(L, 1))
            for b in range(TB):
                if b >= 4:
                    pe.wait_ge(s_row, b - 3)
                for k in range(KT):
                    mm = t.transpose(pair(b % 4)[:, k * P:(k + 1) * P], xT[:, k, b * P:(b + 1) * P], ident[:, :])
                mm.then_inc(s_fin, 1)


_INS = ["x", "positions", "norm_mix_g", "w_in", "lam_q1", "lam_k1", "lam_q2", "lam_k2", "subln_g", "sc_conv_w",
        "ssd_conv_w", "ssd_conv_b", "ssd_dt_bias", "ssd_a_log", "ssd_d", "ssd_norm_g", "w_out",
        "norm_ffn_g", "w_up", "ffn_conv_w", "ffn_conv_b", "w_down", "final_norm_g"]


def kernel(**inputs):
    import numpy as np
    import concourse.bacc as bacc
    from concourse.bass_utils import run_bass_kernel_spmd

    nc = bacc.Bacc("TRN2", target_bir_lowering=False, num_devices=1)
    arrays, args = {}, []
    for name in _INS:
        a = np.ascontiguousarray(inputs[name])
        arrays[f"in_{name}"] = a
        args.append(nc.dram_tensor(f"in_{name}", a.shape, mybir.dt.from_np(a.dtype), kind="ExternalInput").ap())
    out = nc.dram_tensor("out", inputs["x"].shape, F32, kind="ExternalOutput").ap()
    build(nc, *args, out)
    r = run_bass_kernel_spmd(nc, [arrays], core_ids=[0])
    return r.results[0]["out"]
```

```python
import math
from contextlib import ExitStack

import numpy as np

import concourse.bass as bass
from concourse import mybir

F32 = mybir.dt.float32
F32R = mybir.dt.float32r
I32 = mybir.dt.int32
ALU = mybir.AluOpType
ACT = mybir.ActivationFunctionType
AX_X = mybir.AxisListType.X

P = 128
HALF = 512
EPS = 1e-5
ROPE_THETA = 500000.0
RING = 6
RAW = 3
ROWS = 4
LOOKAHEAD = 4
TWO_PI_PARTS = (6.28125, 1.93500518798828125e-3, 3.01991598196e-7)
PI_BELOW = 3.1415925
ROUND = 12582912.0


def build(nc, x, positions, norm_mix_g, w_in, lam_q1, lam_k1, lam_q2, lam_k2, subln_g, sc_conv_w,
          ssd_conv_w, ssd_conv_b, ssd_dt_bias, ssd_a_log, ssd_d, ssd_norm_g, w_out,
          norm_ffn_g, w_up, ffn_conv_w, ffn_conv_b, w_down, final_norm_g, out):
    _, S, D = x.shape
    L = w_in.shape[0]
    KT = D // P
    TB = S // P
    DQK = lam_q1.shape[1]
    DV = subln_g.shape[1]
    HEADS = 4
    ROT = DQK // 4
    R2 = ROT // 2
    HC = 2 * HEADS
    SCW = sc_conv_w.shape[2]
    SCT = SCW // P
    SSDW = ssd_norm_g.shape[1]
    XT = SSDW // P
    XBCT = ssd_conv_w.shape[2] // P
    NH = ssd_d.shape[1]
    FF = w_down.shape[1]
    FT = FF // P
    CH = 2
    NCH = FT // CH
    assert (S, D, DQK, DV, KT, TB, SCT, XT, XBCT, NH) == (1024, 1024, 64, 128, 8, 8, 2, 2, 6, 4)
    assert FT % CH == 0

    COL_Q, COL_K, COL_V, COL_SC = 0, HC * DQK, 2 * HC * DQK, 2 * HC * DQK + HEADS * DV
    COL_Z = COL_SC + 3 * SCW
    COL_XBC = COL_Z + SSDW
    COL_DT = COL_XBC + XBCT * P
    F_TILES = ([("xbc", t, COL_XBC + t * P) for t in range(XBCT)] + [("z", t, COL_Z + t * P) for t in range(XT)]
               + [(kind, t, COL_SC + n * SCW + t * P) for t in range(SCT) for kind, n in (("c", 1), ("h", 2))]
               + [("b", t, COL_SC + t * P) for t in range(SCT)])
    GROUPS = [("v", COL_V), ("q", COL_Q), ("k", COL_K)]
    OUT_ORDER = (4, 5, 6, 7, 0, 1, 2, 3)
    MIXED = XBCT + XT
    SLOTS = [11, 6, 6, 5, 5, 5, 5, 5]
    assert len(SLOTS) == TB and sum(SLOTS) == (len(F_TILES) - MIXED) * KT
    DT_PANELS = (0, 1, 3, 4)
    F0_PANELS = (2, 5)
    P_F = 4
    P_G = P_F + 2 * len(F_TILES)
    P_OUT = P_G + KT * len(GROUPS)
    P_UP0 = P_OUT + 2 * KT
    UPN = 4 * CH
    DNN = 2 * CH
    P_BODY = P_UP0 + UPN
    P_DN = P_BODY + (NCH - 1) * (UPN + DNN)
    PANELS = P_DN + DNN
    assert PANELS % RING == 0 and PANELS % RAW == 0 and (UPN + DNN) % RING == 0

    C_FW = [k * 2 * FT for k in range(3)]
    C_FB = 6 * FT
    C_G1 = 8 * FT
    C_G2 = C_G1 + KT
    C_XW = C_G2 + KT
    C_XB = C_XW + 3 * XBCT
    C_SW = C_XB + XBCT
    C_NG = C_SW + 3 * SCT
    C_SUB = C_NG + XT
    C_LAM = C_SUB + 1
    C_A = C_LAM + 1
    C_DTB = C_A + 2 * NH
    C_D = C_DTB + 2 * NH
    C_GN = C_D + XT
    NPRM = C_GN + KT
    INV_FREQ = [float(np.float32(ROPE_THETA) ** np.float32(-2.0 * j / ROT)) for j in range(R2)]
    LAM_INIT = [0.8 - 0.6 * math.exp(-0.3 * l) for l in range(L)]

    with ExitStack() as ctx:
        def sb(name, shape, dt=F32):
            return ctx.enter_context(nc.sbuf_tensor(name, shape, dt))

        def sem(name):
            return ctx.enter_context(nc.semaphore(name))

        xT = sb("xT", [P, KT, S])
        base_h = (nc.sbuf_base + 63) // 64 * 64
        slab_h = sb("slab_h", [P, base_h - nc.sbuf_base + 2 * KT * S * 4], mybir.dt.uint8)
        raw = [sb(f"raw{i}", [P, HALF]) for i in range(RAW)]
        whi = [sb(f"whi{i}", [P, HALF], F32R) for i in range(RING)]
        wlo = [sb(f"wlo{i}", [P, HALF], F32R) for i in range(RING)]
        ident = sb("ident", [P, P])
        identr = sb("identr", [P, P], F32R)
        ones = sb("ones", [P, P])
        upto = sb("upto", [P, P])
        downto = sb("downto", [P, P])
        capf = sb("capf", [P, P])
        capb = sb("capb", [P, P])
        prm = sb("prm", [P, L, NPRM])
        pc = sb("pc", [P, NPRM])
        cosT = sb("cosT", [P, TB, R2])
        sinT = sb("sinT", [P, TB, R2])
        small = sb("small", [P, 32])
        minus_half = sb("minus_half", [P, 32])
        rstd = sb("rstd", [P, 32])
        rs = sb("rs", [P, 2 * TB])
        nmax = sb("nmax", [P, 2, 2])
        lsum = sb("lsum", [P, 2, 2])
        rlsum = sb("rlsum", [P, 4, 2])
        mix = sb("mix", [P, 2])
        ssq = sb("ssq", [P, 4])
        eps_dv = sb("eps_dv", [P, 1])
        eps_f = sb("eps_f", [P, 1])
        sse = sb("sse", [P, 4])
        srs = sb("srs", [P, 4])

        base_a = (nc.sbuf_base + 63) // 64 * 64
        KB = 1024

        def region(base, limit):
            def at(name, offset, shape, dt=F32):
                n = 4
                for s in shape[1:]:
                    n *= s
                assert offset + n <= limit, name
                return nc.alloc_sbuf_tensor_at(name, shape, dt, offset=base + offset)
            return at

        h_at = region(base_h, 2 * KT * S * 4)
        a_at = region(base_a, 74 * KB)
        slab_a = sb("slab_a", [P, base_a - nc.sbuf_base + 74 * KB], mybir.dt.uint8)

        ahi = h_at("ahi", 0, [P, KT, S], F32R)
        alo = h_at("alo", 32 * KB, [P, KT, S], F32R)
        kst = h_at("kst", 32 * KB, [P, HC, S], F32R)
        E = h_at("E", 0, [P, 2, 2, S])
        qsp = [h_at(f"qsp{i}", (24 + 2 * i) * KB, [P, 2, 2, 2, DQK], F32R) for i in range(2)]
        qT = [h_at(f"qT{i}", (28 + 2 * i) * KB, [P, 2, 2, P], F32R) for i in range(2)]
        q_tok = a_at("q_tok", 0, [P, TB, HEADS * DV])
        v_tok = a_at("v_tok", 16 * KB, [P, TB, HEADS * DV])
        o_tok = q_tok
        yc = a_at("yc", 48 * KB, [P, SCT, S])
        ys = a_at("ys", 56 * KB, [P, XT, S])
        ksp = [a_at(f"ksp{i}", (64 + 4 * i) * KB, [P, HC, 2, DQK], F32R) for i in range(2)]
        k_tok = a_at("k_tok", 32 * KB, [P, TB, HC * DQK])
        W = [a_at(f"W{i}", (40 + 4 * i) * KB, [P, S]) for i in range(2)]
        WT = [a_at(f"WT{i}", (64 + 4 * i) * KB, [P, TB, P]) for i in range(2)]
        xbc = a_at("xbc", 0, [P, XBCT, S])
        st = a_at("st", 24 * KB, [P, TB, XT, 2, P])
        cv = [a_at(f"cv{i}", (40 + 4 * i) * KB, [P, S]) for i in range(2)]
        seg = a_at("seg", 40 * KB, [P, 2, NH, P])
        erow = a_at("erow", 44 * KB, [P, 2, NH, P])
        xb_tok = [a_at(f"xb_tok{i}", (64 + 2 * i) * KB, [P, 4 * P]) for i in range(2)]
        xw = [a_at(f"xw{i}", (68 + 2 * i) * KB, [P, 2, NH, DQK]) for i in range(2)]
        dtT = a_at("dtT", 24 * KB, [8, S])
        rot = a_at("rot", 72 * KB, [P, 2, HC, 2, R2])
        osq = a_at("osq", 72 * KB, [P, P])
        DW = TB * 2 * NH
        dtb_ = [a_at(f"dt{i}", 72 * KB + i * 4 * DW, [P, TB, 2 * NH]) for i in range(8)]
        DT_EXP, DT, DT_W, DT_DEC, DT_A, DT_CUM = (dtb_[i] for i in (2, 7, 0, 1, 4, 5))
        sqs = a_at("sqs", 40 * KB, [P, XT, S])
        acc = a_at("acc", 64 * KB, [P, S])
        sq = a_at("sq", 68 * KB, [P, S])
        sq2 = a_at("sq2", 60 * KB, [P, S])
        rs_row = a_at("rs_row", 48 * KB, [P, S])
        rs_row2 = a_at("rs_row2", 68 * KB, [P, S])
        mhi = a_at("mhi", 0, [P, CH, S], F32R)
        mlo = a_at("mlo", 8 * KB, [P, CH, S], F32R)
        tg = [a_at(f"tg{i}", (32 + 4 * i) * KB, [P, S]) for i in range(2)]
        tu = [a_at(f"tu{i}", (40 + 4 * i) * KB, [P, S]) for i in range(2)]
        xin = a_at("xin", 28 * KB, [P, TB, D])
        stage = [a_at(f"stage{i}", i * 512, [P, P]) for i in range(L + 3)]
        lamv = a_at("lamv", 4 * KB, [P, 4, L, DQK])
        lamp = a_at("lamp", 8 * KB, [P, 2, L, DQK])
        lams = a_at("lams", 10 * KB, [P, 2, L])
        d_rows = a_at("d_rows", 10 * KB + 512, [P, L, NH])
        pos_i = a_at("pos_i", 11 * KB, [TB, P], I32)
        pos_f = a_at("pos_f", 11 * KB + 512, [TB, P])
        pos_c = a_at("pos_c", 12 * KB, [P, TB])
        ang = [a_at(f"ang{i}", 13 * KB + 256 * i, [P, TB, R2]) for i in range(3)]
        fms = a_at("fms", 15 * KB, [P, TB])
        fg_row = a_at("fg_row", 16 * KB, [P, D])
        o_row = [a_at(f"o_row{i}", (20 + 4 * i) * KB, [P, D]) for i in range(ROWS)]

        ps = ctx.enter_context(nc.psum_tensor("ps", [P, 8, HALF], F32))

        def pair(k):
            return ps[:, 2 * k:2 * k + 2, :].rearrange("p b n -> p (b n)")

        def half(k, h):
            return ps[:, 2 * k + h, :]

        class Count:

            def __init__(self, name, n, credit=0):
                self.sem, self.n, self.credit = ctx.enter_context(nc.semaphore(name)), n, credit

            def until(self, l, k):
                return l * self.n + k + self.credit

        s_raw = [sem(f"raw_loaded{i}") for i in range(RAW)]
        s_split = Count("panels_split", PANELS, RAW)
        s_hi = Count("panels_hi", PANELS)
        s_panel = Count("panels_used", PANELS, RING)

        s_setup = sem("setup_loaded")
        s_xin = [sem(f"x_loaded{i}") for i in range(4)]
        s_pos = sem("positions_loaded")
        s_fg = sem("final_gain_loaded")
        s_const = sem("constants_made")
        s_pset = sem("setup_pe")
        s_aset = sem("setup_act")
        s_dset = sem("setup_dve")
        s_xt0 = sem("x_feature_major_pe")
        s_xa = sem("x_feature_major_stored_act")
        s_xv = sem("x_feature_major_stored_dve")
        s_posf = sem("positions_float")
        s_post = sem("positions_by_partition")
        s_ang = sem("angles_reduced")
        s_tab = sem("rotary_tables_ready")
        s_gain = sem("gains_ready")
        s_fin = sem("final_transposed")
        s_fsq = sem("final_mean_squares")
        s_feps = sem("final_eps_added")
        s_frs = sem("final_rstd_ready")
        s_row = sem("final_row_ready")
        s_dlink = sem("setup_dve_steps")
        s_out = [sem(f"rows_stored{i}") for i in range(ROWS)]

        s_sq = Count("squares_written", 2 * KT)
        s_acc = Count("squares_added", 2 * KT)
        s_nsum = Count("square_sums_ready", 2)
        s_ms = Count("mean_squares_ready", 2)
        s_rs = Count("rstd_ready", 2)
        s_dg = Count("rstd_diagonals_ready", 2)
        s_nb = Count("rstd_broadcast_ready", 2)
        s_nr = Count("rstd_row_ready", 2)
        s_nr2 = Count("rstd_row_moved", 1)
        s_hh = Count("operand_hi_ready", 2 * KT)
        s_hl = Count("operand_lo_ready", 2 * KT)
        s_pc = Count("layer_parameters_ready", 1)

        s_fs = Count("feature_tile_scaled", XBCT + XT)
        s_c1 = Count("conv_centre_done", XBCT)
        s_c2 = Count("conv_left_done", XBCT)
        s_c3 = Count("conv_done", XBCT)
        s_xs = Count("xbc_ready", XBCT)
        s_z = Count("z_gate_ready", XT)
        s_sa = Count("short_conv_c_stored", SCT)
        s_sc = Count("short_conv_steps", 5 * SCT)
        s_ss = Count("short_conv_scaled", 3 * SCT)
        s_dtp = Count("dt_feature_major_stored", 1)
        s_dtt = Count("dt_transposed", 1)

        STEP_A = 18
        DV_STEPS = STEP_A + 3
        s_dv = Count("dt_steps", DV_STEPS)
        s_da = Count("dt_exps", 3)
        s_cum = Count("cumulated", 1)
        s_t1 = Count("chunk_transposed", TB)
        s_tok = Count("chunk_position_major", TB)
        s_xw = Count("weighted_x_ready", TB)
        s_stp = Count("states_made", TB)
        s_st = Count("states_stored", TB)
        s_chain = Count("states_chained", 2 * (TB - 2))
        s_rows = Count("decay_rows_made", TB)
        s_gx = Count("gram_made", TB)
        s_seg = Count("segments_ready", TB)
        s_es = Count("segments_exped", TB)
        s_er = Count("rows_exped", TB)
        s_xt = Count("x_position_major", TB)
        s_cs = Count("scaled_c_ready", TB)
        s_mf = Count("decay_forward_done", TB)
        s_mb = Count("decay_both_done", TB)
        s_m = Count("ssd_matrix_ready", TB)
        s_y = Count("ssd_product_ready", TB)
        s_yd = Count("ssd_skip_added", TB)
        s_yz = Count("ssd_gated", TB)
        s_ysq = Count("ssd_squares_ready", 1)
        s_ysum = Count("ssd_square_sums_ready", 1)
        s_yms = Count("ssd_mean_squares_ready", 1)
        s_yrs = Count("ssd_rstd_ready", 1)
        s_ydg = Count("ssd_diagonals_ready", 1)
        s_ynb = Count("ssd_rstd_broadcast_ready", XT)
        s_yn = Count("ssd_output_ready", XT)

        s_g = Count("group_bank_ready", (TB - 1) * len(GROUPS))
        s_ge = Count("group_rows_stored", TB * len(GROUPS))
        s_ra = Count("rotary_products", 2 * TB)
        s_rb = Count("rotary_written", 2 * TB)
        s_kh = Count("k_hi_ready", TB)
        s_kl = Count("k_lo_ready", TB)
        s_kt = Count("k_transposed", TB)
        s_ks = Count("k_stack_ready", TB)

        ITS = HEADS * TB
        s_qh = Count("q_hi_split", ITS)
        s_ql = Count("q_lo_split", ITS)
        s_qt = Count("q_transposed", ITS, 2)
        s_qs = Count("q_stack_ready", ITS, 1)
        s_s = Count("scores_ready", 2 * ITS, 4)
        s_mx = Count("maxima_ready", 2 * ITS)
        s_e = Count("exps_ready", 2 * ITS, 2)
        s_rl = Count("sum_reciprocals_ready", ITS)
        s_cc = Count("mix_factor_ready", ITS)
        s_w = Count("weights_mixed", ITS, 2)
        s_wt = Count("weights_transposed", ITS, 2)
        s_we = Count("weights_key_major", ITS, 1)
        s_o = Count("head_product_ready", ITS, 2)
        s_oe = Count("head_output_stored", ITS, 1)
        s_os = Count("head_squares_summed", ITS, 4)
        s_hms = Count("head_block_eps_added", ITS)
        s_hrs = Count("head_block_rstd_ready", ITS)
        s_hn = Count("head_block_normed", ITS)
        s_ot = Count("heads_transposed", HEADS)
        s_yh = Count("outputs_hi_ready", KT)
        s_yl = Count("outputs_lo_ready", KT)

        s_res = Count("residual_added", KT)
        s_mr = Count("mlp_tile_scaled", 2 * FT)
        s_m1 = Count("mlp_centre_done", 2 * FT)
        s_m2 = Count("mlp_left_done", 2 * FT)
        s_m3 = Count("mlp_conv_done", 2 * FT)
        s_sg = Count("mlp_gate_ready", FT)
        s_mm = Count("mlp_product_ready", FT)
        s_mh = Count("mlp_hi_ready", FT)
        s_ml = Count("mlp_lo_ready", FT)
        s_dr = Count("down_tile_ready", NCH * (KT - 2))
        s_dn = Count("down_tile_added", NCH * KT, KT)

        STEP = UPN + DNN

        EARLY = 3
        FIRST, LAST = -4, 3

        def pipeline(engine, period):
            for p in range(FIRST + EARLY, LAST):
                period(0, p)
            with engine.Fori(0, HEADS - 1) as hd:
                for j in range(TB):
                    period(hd, j + LAST)
            for j in range(TB):
                period(HEADS - 1, j + LAST)

        def exists(hd, j):
            return not isinstance(hd, int) or 0 <= hd * TB + j < ITS

        def hi_of(act, l, p, i=None, width=HALF):
            at = p if i is None else p + i * STEP
            loads = p // RAW + 1 if i is None else p // RAW + 1 + i * (STEP // RAW)
            act.wait_ge(s_raw[p % RAW], (l * (PANELS // RAW) + loads) * 16)
            act.wait_ge(s_panel.sem, s_panel.until(l, at - RING + 1))
            nc.scalar.activation(whi[p % RING][:, 0:width], raw[p % RAW][:, 0:width], ACT.Copy).then_inc(s_hi.sem, 1)

        def lo_of(dve, l, p, i=None, width=HALF):
            at = p if i is None else p + i * STEP
            dve.wait_ge(s_hi.sem, s_hi.until(l, at + 1))
            nc.vector.tensor_tensor(wlo[p % RING][:, 0:width], raw[p % RAW][:, 0:width],
                                    whi[p % RING][:, 0:width].bitcast(F32), ALU.subtract).then_inc(s_split.sem, 1)

        def ahead(part_of, eng, l, p, i=None):
            q = p + LOOKAHEAD
            if q < PANELS:
                part_of(eng, l, q, i, width=panel_width(q))
            else:
                part_of(eng, l + 1, q - PANELS, None, width=panel_width(q - PANELS))

        def panel_width(p):
            return 16 if p in DT_PANELS else HALF

        def psum_down(n):
            return (n + 2) % 4

        def f_pair(n):
            return n if n < 2 else 2 + n % 2

        def slot_panels(c):
            first = sum(SLOTS[:c])
            return [P_F + 2 * MIXED + u // 4 for u in range(first, first + SLOTS[c]) if u % 4 == 0]

        def slot_tiles(c):
            first = sum(SLOTS[:c])
            return [MIXED + u // KT for u in range(first, first + SLOTS[c]) if u % KT == KT - 1]

        N_SETUP = 16 * (7 + (2 * L + 1) + 4 + 2 + 1)

        block = ctx.enter_context(nc.Block())

        @block.sync
        def _(sp):
            n_setup = [0]

            def setup(dst, src):
                n_setup[0] += 1
                sp.dma_start(dst, src).then_inc(s_setup, 16)

            sp.dma_start(pos_i[:, :], positions[0].rearrange("(t p) -> t p", p=P)).then_inc(s_pos, 16)
            for i in range(4):
                two = slice(2 * i, 2 * i + 2)
                sp.dma_start(xin[:, two, :], x[0].rearrange("(t p) d -> p t d", p=P)[:, two, :]).then_inc(s_xin[i], 16)
            rows = stage[L + 2]
            r = 0
            for src in (norm_mix_g, norm_ffn_g, ssd_conv_w.rearrange("l k c -> l (k c)"), ssd_conv_b,
                        sc_conv_w.rearrange("l k c -> l (k c)"), ssd_norm_g, subln_g):
                n = L * src.shape[1] // P
                setup(rows[r:r + n, :], src.rearrange("l (t p) -> (l t) p", p=P))
                r += n
            assert r == L * (C_LAM - C_G1)
            for l in range(L):
                setup(stage[l][0:4 * FT, :], ffn_conv_w[l, 0:2].rearrange("k (t p) -> (k t) p", p=P))
                setup(stage[L][2 * FT * l:2 * FT * (l + 1), :], ffn_conv_w[l, 2].rearrange("(t p) -> t p", p=P))
            setup(stage[L + 1][0:2 * FT * L, :], ffn_conv_b.rearrange("l (t p) -> (l t) p", p=P))
            for n, v in enumerate((lam_q1, lam_k1, lam_q2, lam_k2)):
                setup(lamv[:, n, :, :], v.partition_broadcast(P))
            setup(prm[:, :, C_A:C_A + 2 * NH], ssd_a_log.rearrange("l d h -> l (d h)").partition_broadcast(P))
            setup(prm[:, :, C_DTB:C_DTB + 2 * NH], ssd_dt_bias.rearrange("l d h -> l (d h)").partition_broadcast(P))
            setup(d_rows[:, :, :], ssd_d.partition_broadcast(P))
            assert 16 * n_setup[0] == N_SETUP

            w_in_t = w_in.rearrange("l (k p) n -> l p k n", p=P)
            w_out_t = w_out.rearrange("l (k p) n -> l p k n", p=P)
            w_up_t = w_up.rearrange("l (k p) n -> l p k n", p=P)

            def load(l, dst, src, p, i=None, also=False):
                sp.wait_ge(s_split.sem, s_split.until(l, (p if i is None else p + i * STEP) - RAW + 1 + also))
                sp.dma_start(dst, src).then_inc(s_raw[p % RAW], 16)

            def one(ap, l):
                return ap[bass.ds(l, 1)].rearrange("l p k n -> (l p) k n")

            def dt_slot(p):
                return raw[p % RAW][:, 0:16].rearrange("p (k n) -> p k n", n=8)

            def tiles_slot(p):
                return raw[p % RAW][:, :].rearrange("p (k c) -> p k c", c=P)

            def load_up(l, q, p, chunk, i=None):
                cols = bass.ds(chunk * (CH * P) + (q // 4) * P + ((q % 4) // 2) * FF, P)
                load(l, tiles_slot(p), one(w_up_t[:, :, 4 * (q % 2):4 * (q % 2) + 4, cols], l), p, i)

            def load_dn(l, q, p, chunk, i=None):
                src = w_down[bass.ds(l, 1), bass.ds(chunk * (CH * P) + (q % CH) * P, P),
                             (q // CH) * HALF:(q // CH + 1) * HALF].rearrange("l p n -> (l p) n")
                load(l, raw[p % RAW][:, :], src, p, i)

            with nc.sync.Fori(0, L) as l:
                for p in range(P_F + 2):
                    if p in DT_PANELS:
                        k = 2 * DT_PANELS.index(p)
                        load(l, dt_slot(p), one(w_in_t[:, :, k:k + 2, COL_DT:COL_DT + 8], l), p)
                    else:
                        k = 4 * F0_PANELS.index(p)
                        load(l, tiles_slot(p), one(w_in_t[:, :, k:k + 4, COL_XBC:COL_XBC + P], l), p)
                for n, (_, _, col) in enumerate(F_TILES):
                    if n == 0:
                        continue
                    for h in range(2):
                        p = P_F + 2 * n + h
                        load(l, tiles_slot(p), one(w_in_t[:, :, 4 * h:4 * h + 4, col:col + P], l), p)
                for n, (_, col) in enumerate(GROUPS):
                    for k in range(KT):
                        p = P_G + KT * n + k
                        dst = raw[p % RAW][:, :].rearrange("p (k n) -> p k n", k=1)
                        src = one(w_in_t[:, :, k:k + 1, col:col + HALF], l)
                        if col == k == 0:
                            sp.dma_start(dst, src).then_inc(s_raw[p % RAW], 16)
                            continue
                        load(l, dst, src, p, also=GROUPS[(n + 1) % len(GROUPS)][1] == 0 and k == KT - 1)
                for n in range(KT):
                    for h in range(2):
                        p = P_OUT + 2 * n + h
                        src = one(w_out_t[:, :, 4 - 4 * h:8 - 4 * h, n * P:(n + 1) * P], l)
                        if n == 0 and h == 1:
                            sp.dma_start(tiles_slot(p), src).then_inc(s_raw[p % RAW], 16)
                            continue
                        load(l, tiles_slot(p), src, p, also=n == h == 0)
                for q in range(UPN):
                    load_up(l, q, P_UP0 + q, 0)
                with nc.sync.Fori(0, NCH - 1) as i:
                    for q in range(UPN):
                        load_up(l, q, P_BODY + q, i + 1, i)
                    for q in range(DNN):
                        load_dn(l, q, P_BODY + UPN + q, i, i)
                for q in range(DNN):
                    load_dn(l, q, P_DN + q, NCH - 1)
            for p in range(LOOKAHEAD):
                sp.wait_ge(s_split.sem, s_split.until(L, p - RAW + 1))
                src = (w_in_t[0, :, 0:2, COL_DT:COL_DT + 8] if p in DT_PANELS else
                       w_in_t[0, :, 0:4, COL_XBC:COL_XBC + P])
                sp.dma_start((dt_slot if p in DT_PANELS else tiles_slot)(p), src).then_inc(s_raw[p % RAW], 16)
            sp.dma_start(fg_row[:, :], final_norm_g.partition_broadcast(P)).then_inc(s_fg, 16)
            for b in range(TB):
                sp.wait_ge(s_row, b + 1)
                sp.dma_start(out[0, b * P:(b + 1) * P, :], o_row[b % ROWS][:, :]).then_inc(s_out[b % ROWS], 16)
            for i in range(ROWS):
                sp.wait_ge(s_out[i], 16 * (TB // ROWS))

        @block.gpsimd
        def _(pool):
            g = nc.gpsimd
            g.memset(ident[:, :], 0.0).then_inc(s_const, 1)
            g.memset(ones[:, :], 1.0).then_inc(s_const, 1)
            g.memset(capf[:, :], 0.0).then_inc(s_const, 1)
            g.memset(capb[:, :], 0.0).then_inc(s_const, 1)
            g.memset(minus_half[:, :], -0.5).then_inc(s_const, 1)
            g.memset(eps_dv[:, :], EPS * DV).then_inc(s_const, 1)
            g.memset(eps_f[:, :], EPS).then_inc(s_const, 1)
            pool.wait_ge(s_const, 7)
            g.affine_select(out=ident[:, :], in_=ident[:, :], compare_op=ALU.not_equal, fill=1.0, base=0,
                            pattern=[[-1, P]], channel_multiplier=1).then_inc(s_const, 1)
            for dst, src, fill, sign in ((upto, ones, 0.0, 1), (downto, ones, 0.0, -1),
                                         (capf, capf, -1e30, 1), (capb, capb, -1e30, -1)):
                g.affine_select(out=dst[:, :], in_=src[:, :], compare_op=ALU.is_ge, fill=fill, base=0,
                                pattern=[[sign, P]], channel_multiplier=-sign).then_inc(s_const, 1)

            def power(c_in, c_out, l, k, n, dst=None):
                pool.wait_ge(c_in.sem, c_in.until(l, k))
                g.tensor_tensor((rstd if dst is None else dst)[:, 0:n], small[:, 0:n], minus_half[:, 0:n],
                                ALU.pow).then_inc(c_out.sem, 1)

            def rotary(l, n, rows, b):
                v = rows[:, b, :].rearrange("p (h d) -> p h d", d=DQK)
                both = v[:, :, 0:ROT].rearrange("p h (a r) -> p h a r", r=R2)
                c = cosT[:, b, :].unsqueeze(1).unsqueeze(1).broadcast_to([P, HC, 2, R2])
                s = sinT[:, b, :].unsqueeze(1).unsqueeze(1).broadcast_to([P, HC, 2, R2])
                if n or b:
                    pool.wait_ge(s_rb.sem, s_rb.until(l, TB * n + b))
                pool.wait_ge(s_ge.sem, s_ge.until(l, TB * (n + 1) + b + 1))
                g.tensor_tensor(rot[:, 0, :, :, :], both, c, ALU.mult)
                g.tensor_tensor(rot[:, 1, :, :, :], both, s, ALU.mult).then_inc(s_ra.sem, 1)
                pool.wait_ge(s_ra.sem, s_ra.until(l, TB * n + b + 1))
                g.tensor_tensor(v[:, :, 0:R2], rot[:, 0, :, 0, :], rot[:, 1, :, 1, :], ALU.subtract)
                g.tensor_tensor(v[:, :, R2:ROT], rot[:, 0, :, 1, :], rot[:, 1, :, 0, :], ALU.add).then_inc(s_rb.sem, 1)

            pool.wait_ge(s_tab, 1)
            with nc.gpsimd.Fori(0, L) as l:
                power(s_ms, s_rs, l, 1, TB, rs)
                for t in range(SCT):
                    row = rs_row2[:, :]
                    pool.wait_ge(s_nr2.sem, s_nr2.until(l, 1))
                    pool.wait_ge(s_sa.sem, s_sa.until(l, t + 1))
                    g.tensor_tensor(yc[:, t, :], yc[:, t, :], row, ALU.mult).then_inc(s_ss.sem, 1)
                    pool.wait_ge(s_ss.sem, s_ss.until(l, 3 * t + 1))
                    g.tensor_tensor(yc[:, t, :], yc[:, t, :], row, ALU.mult).then_inc(s_ss.sem, 1)
                    pool.wait_ge(s_sc.sem, s_sc.until(l, 4 * t + 4))
                    g.tensor_tensor(yc[:, t, :], yc[:, t, :], row, ALU.mult).then_inc(s_ss.sem, 1)
                power(s_yms, s_yrs, l, 1, XT * TB)
                def q_lo(hd, j):
                    src = q_tok[:, j % TB, bass.ds(hd * DV + j // TB * DV, DV)].rearrange("p (c d) -> p c d", d=DQK)
                    pool.wait_ge(s_qh.sem, s_qh.until(l, hd * TB + j + 1))
                    g.tensor_tensor(qsp[j % 2][:, :, 1, :, :], src.unsqueeze(2).broadcast_to([P, 2, 2, DQK]),
                                    qsp[j % 2][:, :, 0, :, :].bitcast(F32), ALU.subtract).then_inc(s_ql.sem, 1)

                def head_power(hd, j):
                    it, c = hd * TB + j, j % 4
                    pool.wait_ge(s_os.sem, s_os.until(l, it + 1))
                    g.tensor_tensor(sse[:, c:c + 1], ssq[:, c:c + 1], eps_dv[:, :], ALU.add).then_inc(s_hms.sem, 1)
                    pool.wait_ge(s_hms.sem, s_hms.until(l, it + 1))
                    g.tensor_tensor(srs[:, c:c + 1], sse[:, c:c + 1], minus_half[:, 0:1],
                                    ALU.pow).then_inc(s_hrs.sem, 1)

                for b in range(TB):
                    rotary(l, 0, q_tok, b)
                for b in range(TB):
                    rotary(l, 1, k_tok, b)
                    if b >= 5:
                        q_lo(0, b - 5)

                def pool_period(hd, p):
                    if exists(hd, p + 4):
                        q_lo(hd, p + 4)
                    if exists(hd, p - 3):
                        head_power(hd, p - 3)

                pipeline(nc.gpsimd, pool_period)
                power(s_ms, s_rs, l, 2, TB, rs)
            for b in range(TB):
                pool.wait_ge(s_fsq, b + 1)
                g.tensor_tensor(small[:, b:b + 1], fms[:, b:b + 1], eps_f[:, :], ALU.add).then_inc(s_feps, 1)
                pool.wait_ge(s_feps, b + 1)
                g.tensor_tensor(rs[:, b:b + 1], small[:, b:b + 1], minus_half[:, 0:1], ALU.pow).then_inc(s_frs, 1)

        @block.scalar
        def _(act):
            a = nc.scalar

            def square_tile(l, k):
                if k % KT >= 2:
                    act.wait_ge(s_acc.sem, s_acc.until(l, k - 1))
                a.activation((sq, sq2)[k % 2][:, :], xT[:, k % KT, :], ACT.Square).then_inc(s_sq.sem, 1)

            def operand_hi(k, gain):
                a.activation(ahi[:, k, :], xT[:, k, :], ACT.Copy, scale=gain).then_inc(s_hh.sem, 1)

            def store_rs_row(l, n, k):
                act.wait_ge(s_nb.sem, s_nb.until(l, n + 1))
                a.activation(rs_row[:, :], pair(k), ACT.Copy).then_inc(s_nr.sem, 1)

            def col(c):
                return pc[:, c:c + 1]

            act.sem_inc(s_qs.sem, s_qs.credit)
            act.sem_inc(s_e.sem, s_e.credit)
            act.sem_inc(s_we.sem, s_we.credit)
            act.sem_inc(s_oe.sem, s_oe.credit)
            act.sem_inc(s_os.sem, s_os.credit)
            act.wait_ge(s_ang, 1)
            a.activation(sinT[:, :, :], ang[0][:, :, :], ACT.Sin)
            a.activation(cosT[:, :, :], ang[1][:, :, :], ACT.Sin).then_inc(s_tab, 1)
            for b in range(0, TB, 2):
                act.wait_ge(s_xt0, b + 1)
                a.activation(xT[:, :, b * P:(b + 1) * P], pair(1 + b % 3).rearrange("p (k n) -> p k n", n=P),
                             ACT.Copy).then_inc(s_xa, 1)
            act.wait_ge(s_setup, N_SETUP)
            for l in range(L):
                a_log = prm[:, l, C_A:C_A + 2 * NH]
                last = a.activation(a_log, a_log, ACT.Exp)
            last.then_inc(s_aset, 1)
            act.wait_ge(s_dset, 1)
            a.activation(lams[:, :, :], lams[:, :, :], ACT.Exp).then_inc(s_aset, 1)
            for p in range(RAW):
                hi_of(act, 0, p, width=panel_width(p))
            act.wait_ge(s_xa, TB // 2)
            act.wait_ge(s_xv, TB // 2)
            act.wait_ge(s_gain, 1)
            for k in range(KT):
                operand_hi(k, prm[:, 0, C_G1 + k:C_G1 + k + 1])
                if k == 2:
                    for p in range(RAW, LOOKAHEAD):
                        hi_of(act, 0, p, width=panel_width(p))

            with nc.scalar.Fori(0, L) as l:
                for k in range(KT):
                    square_tile(l, k)
                    if k % 2:
                        ahead(hi_of, act, l, k // 2)
                ahead(hi_of, act, l, P_F)
                ahead(hi_of, act, l, P_F + 1)
                act.wait_ge(s_panel.sem, s_panel.until(l, P_F + 1))
                a.activation(dtT[:, :], pair(2)[0:8, :], ACT.Copy).then_inc(s_dtp.sem, 1)

                def silu_xbc(t):
                    act.wait_ge(s_c3.sem, s_c3.until(l, t + 1))
                    a.activation(xbc[:, t, :], cv[t % 2][:, :], ACT.Silu).then_inc(s_xs.sem, 1)

                for n in range(XBCT):
                    p = P_F + 2 * n
                    if n == 0:
                        store_rs_row(l, 0, 3)
                    else:
                        ahead(hi_of, act, l, p)
                        ahead(hi_of, act, l, p + 1)
                    if n == 2:
                        act.wait_ge(s_dv.sem, s_dv.until(l, 4))
                        a.activation(DT_EXP[:, :, :], DT_EXP[:, :, :], ACT.Exp, scale=-1.0).then_inc(s_da.sem, 1)
                    if n == 5:
                        act.wait_ge(s_dv.sem, s_dv.until(l, DV_STEPS - 1))
                        a.activation(DT_W[:, :, :], DT_W[:, :, :], ACT.Exp).then_inc(s_da.sem, 1)
                        a.activation(DT_DEC[:, :, :], ps[:, 3, DW:2 * DW].rearrange("p (t h) -> p t h", h=2 * NH),
                                     ACT.Exp).then_inc(s_da.sem, 1)
                    act.wait_ge(s_fs.sem, s_fs.until(l, n + 1))
                    if n >= 2:
                        act.wait_ge(s_xs.sem, s_xs.until(l, n - 1))
                    a.activation(cv[n % 2][:, :], pair(f_pair(n)), ACT.Identity, bias=col(C_XB + n),
                                 scale=col(C_XW + XBCT + n)).then_inc(s_c1.sem, 1)
                    if n:
                        silu_xbc(n - 1)
                silu_xbc(XBCT - 1)

                def store_tokens(c):
                    act.wait_ge(s_t1.sem, s_t1.until(l, c + 1))
                    if c >= 2:
                        act.wait_ge(s_stp.sem, s_stp.until(l, c - 1))
                        act.wait_ge(s_xw.sem, s_xw.until(l, c - 1))
                    a.activation(xb_tok[c % 2][:, :], ps[:, c % 2, :], ACT.Copy).then_inc(s_tok.sem, 1)

                def store_states(c):
                    act.wait_ge(s_stp.sem, s_stp.until(l, c + 1))
                    a.activation(st[:, c, :, :, :].rearrange("p g d n -> p (g d n)"), ps[:, 2 + c % 2, :],
                                 ACT.Copy).then_inc(s_st.sem, 1)

                store_tokens(0)
                store_tokens(1)
                for h in range(2 * XT):
                    ahead(hi_of, act, l, P_F + 2 * XBCT + h)
                    for c in (2 * h, 2 * h + 1):
                        store_states(c)
                        if c + 2 < TB:
                            store_tokens(c + 2)
                    if h % 2:
                        act.wait_ge(s_fs.sem, s_fs.until(l, XBCT + h // 2 + 1))
                        a.activation(ys[:, h // 2, :], pair(f_pair(XBCT + h // 2)), ACT.Silu).then_inc(s_z.sem, 1)

                a.activation(rs_row2[:, :], rs_row[:, :], ACT.Copy).then_inc(s_nr2.sem, 1)

                for c in range(TB):
                    if c:
                        act.wait_ge(s_y.sem, s_y.until(l, c))
                    act.wait_ge(s_rows.sem, s_rows.until(l, c + 1))
                    a.activation(erow[:, :, :, :].rearrange("p d h l -> p (d h l)"), pair(0),
                                 ACT.Exp).then_inc(s_er.sem, 1)
                    act.wait_ge(s_gx.sem, s_gx.until(l, c + 1))
                    a.activation(xb_tok[c % 2][:, 0:SSDW], ps[:, 2, SSDW:2 * SSDW], ACT.Copy).then_inc(s_xt.sem, 1)
                    act.wait_ge(s_seg.sem, s_seg.until(l, c + 1))
                    a.activation(seg[:, :, :, :], seg[:, :, :, :], ACT.Exp).then_inc(s_es.sem, 1)
                    for p in slot_panels(c):
                        ahead(hi_of, act, l, p)
                    for n in slot_tiles(c):
                        kind, t, _ = F_TILES[n]
                        if kind == "c":
                            act.wait_ge(s_panel.sem, s_panel.until(l, P_F + 2 * n + 2))
                            act.wait_ge(s_nr2.sem, s_nr2.until(l, 1))
                            a.activation(yc[:, t, :], pair(f_pair(n)), ACT.Copy).then_inc(s_sa.sem, 1)

                for n, (kind, _) in enumerate(GROUPS):
                    for k in range(KT):
                        ahead(hi_of, act, l, P_G + KT * n + k)
                        if n == k == 0:
                            act.wait_ge(s_yz.sem, s_yz.until(l, TB))
                            a.activation(sqs[:, :, :], ys[:, :, :], ACT.Square).then_inc(s_ysq.sem, 1)
                    for b in range(TB if kind != "k" else 0):
                        if b < TB - 1:
                            act.wait_ge(s_g.sem, s_g.until(l, (TB - 1) * n + b + 1))
                        else:
                            act.wait_ge(s_panel.sem, s_panel.until(l, P_G + KT * (n + 1)))
                        dst = {"v": v_tok, "q": q_tok}[kind]
                        r = rs[:, TB + b:TB + b + 1] if kind == "q" else rs[:, b:b + 1]
                        a.activation(dst[:, b, :], ps[:, b, :], ACT.Copy, scale=r).then_inc(s_ge.sem, 1)

                def q_stack(hd, j):
                    it = hd * TB + j
                    act.wait_ge(s_qt.sem, s_qt.until(l, it + 1))
                    act.wait_ge(s_s.sem, s_s.until(l, 2 * it - 2))
                    a.activation(qT[j % 2][:, :, :, :].rearrange("p c s q -> p (c s q)"), ps[:, 6, :],
                                 ACT.Copy).then_inc(s_qs.sem, 1)

                def store_stack(b):
                    act.wait_ge(s_kt.sem, s_kt.until(l, b + 1))
                    a.activation(kst[:, :, b * P:(b + 1) * P], pair(b % 3).rearrange("p (h n) -> p h n", n=P),
                                 ACT.Copy).then_inc(s_ks.sem, 1)

                for b in range(TB + 1):
                    if b < TB:
                        act.wait_ge(s_rb.sem, s_rb.until(l, TB + b + 1))
                        if b >= 2:
                            act.wait_ge(s_kt.sem, s_kt.until(l, b - 1))
                        a.activation(ksp[b % 2][:, :, 0, :], k_tok[:, b, :].rearrange("p (h d) -> p h d", d=DQK),
                                     ACT.Copy).then_inc(s_kh.sem, 1)
                    if b:
                        store_stack(b - 1)
                    if b == 6:
                        q_stack(0, 0)

                def head_output(hd, j):
                    it = hd * TB + j
                    act.wait_ge(s_o.sem, s_o.until(l, it + 1))
                    act.wait_ge(s_rl.sem, s_rl.until(l, it + 1))
                    r0 = rlsum[:, j % 4, 0:1]
                    a.activation(o_tok[:, j % TB, bass.ds(hd * DV + j // TB * DV, DV)], ps[:, 7, 0:DV], ACT.Copy,
                                 scale=r0).then_inc(s_oe.sem, 1)
                    a.activation(osq[:, :], ps[:, 7, 0:DV], ACT.Square, scale=r0,
                                 accum_out=ssq[:, j % 4:j % 4 + 1]).then_inc(s_os.sem, 1)

                def exps(hd, j):
                    it = hd * TB + j
                    act.wait_ge(s_w.sem, s_w.until(l, it - 1))
                    for c in range(2):
                        act.wait_ge(s_mx.sem, s_mx.until(l, 2 * it + c + 1))
                        a.activation(E[:, j % 2, c, :], pair(c), ACT.Exp, bias=nmax[:, j % 2, c:c + 1],
                                     accum_out=lsum[:, j % 2, c:c + 1]).then_inc(s_e.sem, 1)

                def store_weights(hd, j):
                    it = hd * TB + j
                    act.wait_ge(s_wt.sem, s_wt.until(l, it + 1))
                    act.wait_ge(s_o.sem, s_o.until(l, it - 1))
                    a.activation(WT[j % 2][:, :, :].rearrange("p b q -> p (b q)"), pair(2),
                                 ACT.Copy).then_inc(s_we.sem, 1)

                y_parts = (yc[:, 0, :], yc[:, 1, :], ys[:, 0, :], ys[:, 1, :])

                def part_hi(kt):
                    a.activation(ahi[:, kt, :], y_parts[kt - HEADS], ACT.Copy).then_inc(s_yh.sem, 1)

                def head_hi(h):
                    act.wait_ge(s_ot.sem, s_ot.until(l, h + 1))
                    act.wait_ge(s_w.sem, s_w.until(l, ITS - 1 + h // 2))
                    a.activation(ahi[:, h, :], pair(h), ACT.Identity, bias=0.0, scale=col(C_SUB)).then_inc(s_yh.sem, 1)

                def act_period(hd, p):
                    if exists(hd, p + 2):
                        q_stack(hd, p + 2)
                    if exists(hd, p - 3):
                        head_output(hd, p - 3)
                    if exists(hd, p + 1):
                        exps(hd, p + 1)
                    if exists(hd, p - 1):
                        store_weights(hd, p - 1)
                    left = ITS + 3 - (hd * TB + p) if isinstance(hd, int) else None
                    if left == 8:
                        part_hi(4)
                    if left == 7:
                        part_hi(5)
                    if left == 4:
                        act.wait_ge(s_s.sem, s_s.until(l, 2 * ITS))
                        part_hi(6)
                        part_hi(7)
                    if left == 3:
                        head_hi(0)
                    if left == 2:
                        head_hi(1)
                        head_hi(2)
                    if left == 1:
                        head_hi(3)

                pipeline(nc.scalar, act_period)

                for n in range(KT):
                    ahead(hi_of, act, l, P_OUT + 2 * n)
                    ahead(hi_of, act, l, P_OUT + 2 * n + 1)
                    if n < KT - 1:
                        act.wait_ge(s_res.sem, s_res.until(l, n + 1))
                        square_tile(l, KT + n)

                act.wait_ge(s_panel.sem, s_panel.until(l, P_UP0))
                for k in range(KT):
                    if k == 2:
                        act.wait_ge(s_res.sem, s_res.until(l, KT))
                        square_tile(l, 2 * KT - 1)
                    operand_hi(k, col(C_G2 + k))

                def centre(n, tile, j, up):
                    c = up * FT + j
                    if isinstance(c, int):
                        b, w = col(C_FB + c), col(C_FW[1] + c)
                    else:
                        b, w = pc[:, bass.ds(C_FB + c, 1)], pc[:, bass.ds(C_FW[1] + c, 1)]
                    a.activation(tile[:, :], pair((n + 2) % 4), ACT.Identity, bias=b, scale=w).then_inc(s_m1.sem, 1)

                def gate(k, j):
                    act.wait_ge(s_m3.sem, s_m3.until(l, 2 * k + 2))
                    a.activation(tg[j][:, :], tg[j][:, :], ACT.Silu).then_inc(s_sg.sem, 1)

                def product_hi(k, slot, j):
                    act.wait_ge(s_mm.sem, s_mm.until(l, k + 1))
                    a.activation(mhi[:, slot, :], tg[j][:, :], ACT.Copy).then_inc(s_mh.sem, 1)

                def up_chunk(chunk, p0, i=None):
                    for n in range(2 * CH):
                        j, up = n // 2, n % 2
                        ahead(hi_of, act, l, p0 + 2 * n, i)
                        ahead(hi_of, act, l, p0 + 2 * n + 1, i)
                        if i is None and n == 0:
                            store_rs_row(l, 1, 1)
                        act.wait_ge(s_mr.sem, s_mr.until(l, 2 * CH * chunk + n + 1))
                        if i is not None and up == 0:
                            act.wait_ge(s_ml.sem, s_ml.until(l, (chunk - 1) * CH + j + 1))
                        centre(n, (tg, tu)[up][j], chunk * CH + j, up)
                        if n == 2:
                            gate(chunk * CH, 0)

                def products(chunk, slot):
                    gate(chunk * CH + 1, 1)
                    product_hi(chunk * CH, slot, 0)
                    product_hi(chunk * CH + 1, slot + 1, 1)

                up_chunk(0, P_UP0)
                products(0, 0)
                with nc.scalar.Fori(0, NCH - 1) as i:
                    up_chunk(i + 1, P_BODY, i)
                    for q in range(DNN):
                        ahead(hi_of, act, l, P_BODY + UPN + q, i)
                        if q == 0:
                            gate((i + 1) * CH + 1, 1)
                    act.wait_ge(s_panel.sem, s_panel.until(l, P_BODY + UPN + DNN + i * STEP))
                    product_hi((i + 1) * CH, 0, 0)
                    product_hi((i + 1) * CH + 1, 1, 1)
                for q in range(DNN):
                    ahead(hi_of, act, l, P_DN + q)
                for n in range(KT):
                    act.wait_ge(s_dn.sem, s_dn.until(l, (NCH - 1) * KT + n + 1))
                    operand_hi(n, col(C_GN + n))
            for b in range(TB):
                act.wait_ge(s_fin, b + 1)
                if b >= 2:
                    act.wait_ge(s_fsq, b - 1)
                a.activation((sq, sq2)[b % 2][:, :], pair(b % 4), ACT.Square, scale=D ** -0.5,
                             accum_out=fms[:, b:b + 1]).then_inc(s_fsq, 1)

        @block.vector
        def _(dve):
            v = nc.vector
            links = [0]

            def link(ins, value=None):
                links[0] += 1
                ins.then_inc(s_dlink, 1)
                dve.wait_ge(s_dlink, links[0])

            def col(c):
                return pc[:, c:c + 1]

            def add_squares(l, k):
                src = (sq, sq2)[k % 2]
                dve.wait_ge(s_sq.sem, s_sq.until(l, k + 1))
                if k % KT == 0:
                    v.tensor_copy(acc[:, :], src[:, :]).then_inc(s_acc.sem, 1)
                else:
                    dve.wait_ge(s_acc.sem, s_acc.until(l, k))
                    v.tensor_tensor(acc[:, :], acc[:, :], src[:, :], ALU.add).then_inc(s_acc.sem, 1)

            def mean_squares(l, n):
                dve.wait_ge(s_nsum.sem, s_nsum.until(l, n + 1))
                v.tensor_scalar(small[:, 0:TB], ps[:, (6, 0)[n], 0:TB], 1.0 / D, EPS, ALU.mult,
                                ALU.add).then_inc(s_ms.sem, 1)

            def diagonals(l, n, c_rs, c_dg, dst, count, factor=rstd):
                dve.wait_ge(c_rs.sem, c_rs.until(l, n + 1))
                for b in range(count):
                    last = v.tensor_scalar(dst(b), ident[:, :], factor[:, b:b + 1], None, ALU.mult)
                last.then_inc(c_dg.sem, 1)

            def norm(l, n):
                mean_squares(l, n)
                dve.wait_ge(s_rs.sem, s_rs.until(l, n + 1))
                v.tensor_scalar(rs[:, TB:2 * TB], rs[:, 0:TB], DQK ** -0.5, None, ALU.mult)
                diagonals(l, n, s_rs, s_dg, lambda b: sq[:, b * P:(b + 1) * P], TB, rs)

            def operand_lo(l, k, gain):
                dve.wait_ge(s_hh.sem, s_hh.until(l, k + 1))
                n = k % KT
                v.scalar_tensor_tensor(out=alo[:, n, :], in0=xT[:, n, :], scalar=gain, in1=ahi[:, n, :].bitcast(F32),
                                       op0=ALU.mult, op1=ALU.subtract).then_inc(s_hl.sem, 1)

            def scale_tile(k, c_out):
                v.tensor_tensor(pair(k), pair(k), rs_row[:, :], ALU.mult).then_inc(c_out.sem, 1)

            def taps(l, dst, src, w0, w2, c_mid, c_end, k):
                v.scalar_tensor_tensor(out=dst[:, 1:S], in0=src[:, 0:S - 1], scalar=w0, in1=dst[:, 1:S],
                                       op0=ALU.mult, op1=ALU.add).then_inc(c_mid.sem, 1)
                dve.wait_ge(c_mid.sem, c_mid.until(l, k))
                v.scalar_tensor_tensor(out=dst[:, 0:S - 1], in0=src[:, 1:S], scalar=w2, in1=dst[:, 0:S - 1],
                                       op0=ALU.mult, op1=ALU.add).then_inc(c_end.sem, 1)

            dve.sem_inc(s_split.sem, s_split.credit)
            dve.sem_inc(s_w.sem, s_w.credit)
            dve.sem_inc(s_dn.sem, s_dn.credit)
            dve.wait_ge(s_const, 12)
            link(v.tensor_copy(identr[:, :], ident[:, :]))
            dve.wait_ge(s_pos, 16)
            v.tensor_copy(pos_f[:, :], pos_i[:, :]).then_inc(s_posf, 1)
            dve.wait_ge(s_post, 1)
            link(v.tensor_copy(pos_c[:, :], ps[:, 1, 0:TB]))
            for j in range(R2):
                last = v.tensor_scalar(ang[0][:, :, j], pos_c[:, :], INV_FREQ[j], None, ALU.mult)
            link(last)
            link(v.tensor_scalar(ang[1][:, :, :], ang[0][:, :, :], 1.0 / (2 * math.pi), ROUND, ALU.mult, ALU.add))
            link(v.tensor_scalar(ang[1][:, :, :], ang[1][:, :, :], -ROUND, None, ALU.add))
            for part in TWO_PI_PARTS:
                link(v.scalar_tensor_tensor(out=ang[0][:, :, :], in0=ang[1][:, :, :], scalar=-part,
                                            in1=ang[0][:, :, :], op0=ALU.mult, op1=ALU.add))
            link(v.tensor_scalar(ang[0][:, :, :], ang[0][:, :, :], PI_BELOW, -PI_BELOW, ALU.min, ALU.max))
            link(v.scalar_tensor_tensor(out=ang[2][:, :, :], in0=ang[0][:, :, :], scalar=-1.0, in1=ang[0][:, :, :],
                                        op0=ALU.mult, op1=ALU.max))
            v.tensor_scalar(ang[1][:, :, :], ang[2][:, :, :], -1.0, math.pi / 2, ALU.mult,
                            ALU.add).then_inc(s_ang, 1)
            for b in range(1, TB, 2):
                dve.wait_ge(s_xt0, b + 1)
                v.tensor_copy(xT[:, :, b * P:(b + 1) * P],
                              pair(1 + b % 3).rearrange("p (k n) -> p k n", n=P)).then_inc(s_xv, 1)
            dve.wait_ge(s_setup, N_SETUP)
            link(v.tensor_tensor(lamp[:, :, :, :], lamv[:, 0:4:2, :, :], lamv[:, 1:4:2, :, :], ALU.mult))
            v.tensor_reduce(lams[:, :, :], lamp[:, :, :, :], AX_X, ALU.add).then_inc(s_dset, 1)
            dve.wait_ge(s_pset, 1)
            at = 0
            for l in range(L):
                v.tensor_copy(prm[:, l, 0:4 * FT], ps[:, 0, at:at + 4 * FT])
                at += 4 * FT
            first = 4 * FT
            for n in (2 * FT, 2 * FT, KT, KT, 3 * XBCT, XBCT, 3 * SCT, XT, 1):
                last = v.tensor_copy(prm[:, :, first:first + n],
                                     ps[:, 0, at:at + L * n].rearrange("p (l n) -> p l n", n=n))
                first += n
                at += L * n
            assert first == C_LAM
            for hf in range(2):
                half_of = slice(64 * hf, 64 * hf + 64)
                last = v.tensor_copy(prm[half_of, :, C_D:C_D + XT], d_rows[half_of, :, hf:NH:2])
            link(last)
            for l in range(L):
                last = v.tensor_copy(prm[:, l, C_GN:C_GN + KT], prm[:, (l + 1) % L, C_G1:C_G1 + KT])
                sub = prm[:, l, C_SUB:C_SUB + 1]
                link(v.tensor_scalar(sub, sub, (1.0 - LAM_INIT[l]) * DV ** 0.5, None, ALU.mult))
            last.then_inc(s_gain, 1)
            dve.wait_ge(s_aset, 1)
            for l in range(L):
                a_row = prm[:, l, C_A:C_A + 2 * NH]
                link(v.tensor_scalar(a_row, a_row, -1.0, None, ALU.mult))
            dve.wait_ge(s_aset, 2)
            for l in range(L):
                m = prm[:, l, C_LAM:C_LAM + 1]
                link(v.tensor_tensor(m, lams[:, 1, l:l + 1], lams[:, 0, l:l + 1], ALU.subtract))
                link(v.tensor_scalar(m, m, -LAM_INIT[l], None, ALU.add))
            for p in range(RAW):
                lo_of(dve, 0, p, width=panel_width(p))
            for k in range(KT):
                operand_lo(0, k, prm[:, 0, C_G1 + k:C_G1 + k + 1])
                if k == 1:
                    for p in range(RAW, LOOKAHEAD):
                        lo_of(dve, 0, p, width=panel_width(p))

            with nc.vector.Fori(0, L) as l:
                dve.wait_ge(s_hl.sem, s_hl.until(l, KT))
                v.tensor_copy(pc[:, :], prm[:, bass.ds(l, 1), :].rearrange("p a n -> p (a n)")).then_inc(s_pc.sem, 1)
                dve.wait_ge(s_pc.sem, s_pc.until(l, 1))
                for k in range(KT):
                    add_squares(l, k)
                    if k % 2:
                        ahead(lo_of, dve, l, k // 2)
                norm(l, 0)
                ahead(lo_of, dve, l, P_F)
                ahead(lo_of, dve, l, P_F + 1)

                def dstep(ins):
                    steps[0] += 1
                    ins.then_inc(s_dv.sem, 1)
                    dve.wait_ge(s_dv.sem, s_dv.until(l, steps[0]))

                steps = [0]

                def by_block(c):
                    return pc[:, c:c + 2 * NH].unsqueeze(1).broadcast_to([P, TB, 2 * NH])

                d = [t[:, :, :] for t in dtb_]
                for n in range(XBCT):
                    p = P_F + 2 * n
                    if n == 0:
                        dve.wait_ge(s_nr.sem, s_nr.until(l, 1))
                    else:
                        ahead(lo_of, dve, l, p)
                        ahead(lo_of, dve, l, p + 1)
                    if n == 5:
                        dve.wait_ge(s_da.sem, s_da.until(l, 2))
                        dstep(v.tensor_tensor(DT_W[:, :, :], DT_W[:, :, :], d[7], ALU.mult))
                        assert steps[0] == DV_STEPS
                    dve.wait_ge(s_panel.sem, s_panel.until(l, p + 2))
                    scale_tile(f_pair(n), s_fs)
                    dve.wait_ge(s_c1.sem, s_c1.until(l, n + 1))
                    taps(l, cv[n % 2], pair(f_pair(n)), col(C_XW + n), col(C_XW + 2 * XBCT + n), s_c2, s_c3, n + 1)
                    if n == 1:
                        dve.wait_ge(s_dtt.sem, s_dtt.until(l, 1))
                        dstep(v.tensor_tensor(dtb_[0][:, :, :], ps[:, 6, 0:DW].rearrange("p (t h) -> p t h", h=2 * NH),
                                              rs[:, 0:TB].unsqueeze(2).broadcast_to([P, TB, 2 * NH]), ALU.mult))
                        dstep(v.tensor_tensor(dtb_[0][:, :, :], dtb_[0][:, :, :], by_block(C_DTB), ALU.add))
                        dstep(v.tensor_scalar(d[1], d[0], 0.0, None, ALU.max))
                        dstep(v.scalar_tensor_tensor(out=d[2], in0=d[0], scalar=-1.0, in1=d[0], op0=ALU.mult,
                                                     op1=ALU.max))
                    if n == 2:
                        dve.wait_ge(s_da.sem, s_da.until(l, 1))
                        dstep(v.tensor_scalar(d[3], d[2], 2.0, None, ALU.add))
                        dstep(v.reciprocal(d[4], d[3]))
                        dstep(v.tensor_tensor(d[5], d[2], d[4], ALU.mult))
                        dstep(v.tensor_tensor(d[6], d[5], d[5], ALU.mult))
                        dstep(v.tensor_scalar(d[3], d[6], 1.0 / 15, None, ALU.mult))
                        for m in (13, 11, 9, 7, 5, 3):
                            dstep(v.scalar_tensor_tensor(out=d[3], in0=d[3], scalar=1.0 / m, in1=d[6], op0=ALU.add,
                                                         op1=ALU.mult))
                        dstep(v.scalar_tensor_tensor(out=d[4], in0=d[3], scalar=1.0, in1=d[5], op0=ALU.add,
                                                     op1=ALU.mult))
                        dstep(v.scalar_tensor_tensor(out=d[7], in0=d[4], scalar=2.0, in1=d[1], op0=ALU.mult,
                                                     op1=ALU.add))
                        dstep(v.tensor_tensor(DT_A[:, :, :], d[7], by_block(C_A), ALU.mult))
                        assert steps[0] == STEP_A
                    if n == 4:
                        dve.wait_ge(s_cum.sem, s_cum.until(l, 1))
                        q4 = DW // 2
                        v.tensor_copy(DT_CUM[:, :, 0:NH], ps[:, 3, 0:q4].rearrange("p (t h) -> p t h", h=NH))
                        dstep(v.tensor_copy(DT_CUM[:, :, NH:2 * NH],
                                            ps[:, 3, q4:DW].rearrange("p (t h) -> p t h", h=NH)))
                        total = ps[:, 3, DW:2 * DW].rearrange("p (t h) -> p t h", h=2 * NH)
                        dstep(v.tensor_tensor(DT_W[:, :, :], total, DT_CUM[:, :, :], ALU.subtract))

                for c in range(TB):
                    dve.wait_ge(s_tok.sem, s_tok.until(l, c + 1))
                    if c >= 2:
                        dve.wait_ge(s_stp.sem, s_stp.until(l, c - 1))
                    x4 = xb_tok[c % 2][:, 0:SSDW].rearrange("p (h d) -> p h d", h=NH)
                    for dr in range(2):
                        w4 = DT_W[:, c, dr * NH:(dr + 1) * NH].unsqueeze(2).broadcast_to([P, NH, DQK])
                        last = v.tensor_tensor(xw[c % 2][:, dr, :, :], x4, w4, ALU.mult)
                    last.then_inc(s_xw.sem, 1)
                    if c % 2:
                        ahead(lo_of, dve, l, P_F + 2 * XBCT + c // 2)
                    if c % 4 == 3:
                        n = XBCT + c // 4
                        dve.wait_ge(s_panel.sem, s_panel.until(l, P_F + 2 * n + 2))
                        scale_tile(f_pair(n), s_fs)

                def chain_states():
                    dve.wait_ge(s_st.sem, s_st.until(l, TB))
                    dve.wait_ge(s_da.sem, s_da.until(l, 3))
                    for n in range(1, TB - 1):
                        for dr in range(2):
                            c, prev = (n, n - 1) if dr == 0 else (TB - 1 - n, TB - n)
                            if n > 1:
                                dve.wait_ge(s_chain.sem, s_chain.until(l, 2 * (n - 1) - 1 + dr))
                            for h in range(NH):
                                g, hf = h // 2, h % 2
                                cols = slice(hf * DQK, (hf + 1) * DQK)
                                last = v.scalar_tensor_tensor(
                                    out=st[:, c, g, dr, cols], in0=st[:, prev, g, dr, cols],
                                    scalar=DT_DEC[:, c, dr * NH + h:dr * NH + h + 1], in1=st[:, c, g, dr, cols],
                                    op0=ALU.mult, op1=ALU.add)
                            last.then_inc(s_chain.sem, 1)

                def short_conv(n):
                    kind, t, _ = F_TILES[n]
                    h_tile = pair(f_pair(n))
                    if kind == "h":
                        dve.wait_ge(s_ss.sem, s_ss.until(l, 3 * t + 2))
                        dve.wait_ge(s_panel.sem, s_panel.until(l, P_F + 2 * n + 2))
                        v.tensor_tensor(h_tile, h_tile, yc[:, t, :], ALU.mult).then_inc(s_sc.sem, 1)
                        dve.wait_ge(s_sc.sem, s_sc.until(l, 4 * t + 1))
                        v.tensor_scalar(yc[:, t, :], h_tile, col(C_SW + SCT + t), None, ALU.mult).then_inc(s_sc.sem, 1)
                        for w, (dst, src) in ((t, (slice(1, S), slice(0, S - 1))),
                                              (2 * SCT + t, (slice(0, S - 1), slice(1, S)))):
                            k = 4 * t + (2 if w == t else 3)
                            dve.wait_ge(s_sc.sem, s_sc.until(l, k))
                            v.scalar_tensor_tensor(out=yc[:, t, dst], in0=h_tile[:, src], scalar=col(C_SW + w),
                                                   in1=yc[:, t, dst], op0=ALU.mult, op1=ALU.add).then_inc(s_sc.sem, 1)
                    elif kind == "b":
                        dve.wait_ge(s_panel.sem, s_panel.until(l, P_F + 2 * n + 2))
                        dve.wait_ge(s_ss.sem, s_ss.until(l, 3 * t + 3))
                        v.tensor_tensor(yc[:, t, :], pair(f_pair(n)), yc[:, t, :], ALU.mult).then_inc(s_sc.sem, 1)

                def skip_and_gate(c):
                    cols = slice(c * P, (c + 1) * P)
                    dve.wait_ge(s_y.sem, s_y.until(l, c + 1))
                    for g in range(XT):
                        last = v.scalar_tensor_tensor(out=xbc[:, g, cols], in0=xbc[:, g, cols], scalar=col(C_D + g),
                                                      in1=ps[:, 3, g * P:(g + 1) * P],
                                                      op0=ALU.mult, op1=ALU.add)
                    last.then_inc(s_yd.sem, 1)
                    dve.wait_ge(s_yd.sem, s_yd.until(l, c + 1))
                    v.tensor_tensor(ys[:, :, cols], xbc[:, 0:XT, cols], ys[:, :, cols], ALU.mult).then_inc(s_yz.sem, 1)

                dve.wait_ge(s_z.sem, s_z.until(l, XT))
                for c in range(TB):
                    dve.wait_ge(s_er.sem, s_er.until(l, c + 1))
                    if c:
                        dve.wait_ge(s_y.sem, s_y.until(l, c))
                    rows = pair(0).rearrange("p (d h l) -> p d h l", d=2, h=NH)
                    for dr, cap in ((0, capf), (1, capb)):
                        for h in range(NH):
                            last = v.scalar_tensor_tensor(out=seg[:, dr, h, :], in0=rows[:, dr, h, :],
                                                          scalar=DT_CUM[:, c, dr * NH + h:dr * NH + h + 1],
                                                          in1=cap[:, :], op0=ALU.subtract, op1=ALU.min)
                    last.then_inc(s_seg.sem, 1)
                    for g in range(XT):
                        cT = xbc[:, 4 + g:5 + g, c * P:(c + 1) * P].unsqueeze(1).broadcast_to([P, 2, 2, P])
                        e4 = erow[:, :, 2 * g:2 * g + 2, :]
                        last = v.tensor_tensor(e4, e4, cT, ALU.mult)
                    last.then_inc(s_cs.sem, 1)
                    if c:
                        skip_and_gate(c - 1)
                    else:
                        chain_states()
                    dve.wait_ge(s_es.sem, s_es.until(l, c + 1))
                    for h in range(NH):
                        last = v.tensor_scalar(seg[:, 0, h, :], seg[:, 0, h, :], DT[:, c, h:h + 1], None, ALU.mult)
                    last.then_inc(s_mf.sem, 1)
                    dve.wait_ge(s_mf.sem, s_mf.until(l, c + 1))
                    for h in range(NH):
                        last = v.scalar_tensor_tensor(out=seg[:, 0, h, :], in0=seg[:, 1, h, :],
                                                      scalar=DT[:, c, NH + h:NH + h + 1], in1=seg[:, 0, h, :],
                                                      op0=ALU.mult, op1=ALU.add)
                    last.then_inc(s_mb.sem, 1)
                    dve.wait_ge(s_mb.sem, s_mb.until(l, c + 1))
                    dve.wait_ge(s_xt.sem, s_xt.until(l, c + 1))
                    for g in range(XT):
                        gram = ps[:, 2, g * P:(g + 1) * P].unsqueeze(1).broadcast_to([P, 2, P])
                        m = seg[:, 0, 2 * g:2 * g + 2, :]
                        last = v.tensor_tensor(m, gram, m, ALU.mult)
                    last.then_inc(s_m.sem, 1)
                    for p in slot_panels(c):
                        ahead(lo_of, dve, l, p)
                    for n in slot_tiles(c):
                        short_conv(n)
                skip_and_gate(TB - 1)

                for p in range(P_G, P_OUT):
                    ahead(lo_of, dve, l, p)
                    if p == P_G + KT:
                        dve.wait_ge(s_ysum.sem, s_ysum.until(l, 1))
                        v.tensor_scalar(small[:, 0:XT * TB], ps[:, 7, 0:XT * TB], 1.0 / P, EPS, ALU.mult,
                                        ALU.add).then_inc(s_yms.sem, 1)
                        diagonals(l, 0, s_yrs, s_ydg, lambda b: sqs[:, b // TB, (b % TB) * P:(b % TB + 1) * P], XT * TB)
                    if p == P_G + 2 * KT:
                        for g in range(XT):
                            dve.wait_ge(s_ynb.sem, s_ynb.until(l, g + 1))
                            v.scalar_tensor_tensor(out=ys[:, g, :], in0=ys[:, g, :], scalar=col(C_NG + g),
                                                   in1=pair(2 + g), op0=ALU.mult, op1=ALU.mult).then_inc(s_yn.sem, 1)
                def store_k(b):
                    if b < TB - 1:
                        dve.wait_ge(s_g.sem, s_g.until(l, (TB - 1) * 2 + b + 1))
                    else:
                        dve.wait_ge(s_panel.sem, s_panel.until(l, P_OUT))
                    v.tensor_scalar(k_tok[:, b, :], ps[:, b, :], rs[:, b:b + 1], None, ALU.mult).then_inc(s_ge.sem, 1)

                def k_lo(b):
                    dve.wait_ge(s_kh.sem, s_kh.until(l, b + 1))
                    rows = k_tok[:, b, :].rearrange("p (h d) -> p h d", d=DQK)
                    v.tensor_tensor(ksp[b % 2][:, :, 1, :], rows, ksp[b % 2][:, :, 0, :].bitcast(F32),
                                    ALU.subtract).then_inc(s_kl.sem, 1)

                def q_hi(hd, j):
                    it = hd * TB + j
                    dve.wait_ge(s_qt.sem, s_qt.until(l, it - 1))
                    src = q_tok[:, j % TB, bass.ds(hd * DV + j // TB * DV, DV)].rearrange("p (c d) -> p c d", d=DQK)
                    v.tensor_copy(qsp[j % 2][:, :, 0, :, :], src.unsqueeze(2).broadcast_to([P, 2, 2, DQK])
                                  ).then_inc(s_qh.sem, 1)

                for b in range(3):
                    store_k(b)
                for b in range(3, TB):
                    store_k(b)
                    k_lo(b - 3)
                q_hi(0, 0)
                q_hi(0, 1)
                for b in range(TB - 3, TB):
                    k_lo(b)
                q_hi(0, 2)

                def maxima(hd, j):
                    for c in range(2):
                        dve.wait_ge(s_s.sem, s_s.until(l, 2 * (hd * TB + j) + c + 1))
                        v.tensor_reduce(nmax[:, j % 2, c:c + 1], pair(c), AX_X, ALU.max,
                                        negate=True).then_inc(s_mx.sem, 1)

                def mix_weights(hd, j):
                    it = hd * TB + j
                    dve.wait_ge(s_e.sem, s_e.until(l, 2 * it + 2))
                    dve.wait_ge(s_os.sem, s_os.until(l, it - 3))
                    v.reciprocal(rlsum[:, j % 4, :], lsum[:, j % 2, :]).then_inc(s_rl.sem, 1)
                    dve.wait_ge(s_rl.sem, s_rl.until(l, it + 1))
                    v.scalar_tensor_tensor(out=mix[:, j % 2:j % 2 + 1], in0=lsum[:, j % 2, 0:1],
                                           scalar=rlsum[:, j % 4, 1:2], in1=col(C_LAM), op0=ALU.mult,
                                           op1=ALU.mult).then_inc(s_cc.sem, 1)
                    dve.wait_ge(s_cc.sem, s_cc.until(l, it + 1))
                    dve.wait_ge(s_wt.sem, s_wt.until(l, it - 1))
                    v.scalar_tensor_tensor(out=W[j % 2][:, :], in0=E[:, j % 2, 1, :],
                                           scalar=mix[:, j % 2:j % 2 + 1], in1=E[:, j % 2, 0, :],
                                           op0=ALU.mult, op1=ALU.add).then_inc(s_w.sem, 1)

                y_parts = (yc[:, 0, :], yc[:, 1, :], ys[:, 0, :], ys[:, 1, :])

                def head_scale(hd, j):
                    dve.wait_ge(s_hrs.sem, s_hrs.until(l, hd * TB + j + 1))
                    o = o_tok[:, j % TB, bass.ds(hd * DV + j // TB * DV, DV)]
                    v.tensor_scalar(o, o, srs[:, j % 4:j % 4 + 1], None, ALU.mult).then_inc(s_hn.sem, 1)

                def part_lo(n):
                    kt = OUT_ORDER[n]
                    dve.wait_ge(s_yh.sem, s_yh.until(l, n + 1))
                    v.tensor_tensor(alo[:, kt, :], y_parts[kt - HEADS], ahi[:, kt, :].bitcast(F32),
                                    ALU.subtract).then_inc(s_yl.sem, 1)

                def head_lo(h):
                    dve.wait_ge(s_yh.sem, s_yh.until(l, HEADS + h + 1))
                    v.scalar_tensor_tensor(out=alo[:, h, :], in0=pair(h), scalar=col(C_SUB),
                                           in1=ahi[:, h, :].bitcast(F32), op0=ALU.mult,
                                           op1=ALU.subtract).then_inc(s_yl.sem, 1)

                def dve_period(hd, p):
                    if exists(hd, p + 4):
                        q_hi(hd, p + 4)
                    if exists(hd, p + 1):
                        maxima(hd, p + 1)
                    if exists(hd, p):
                        mix_weights(hd, p)
                    if exists(hd, p - 3):
                        head_scale(hd, p - 3)
                    left = ITS + 3 - (hd * TB + p) if isinstance(hd, int) else None
                    if left in (7, 6):
                        part_lo(7 - left)
                    if left == 4:
                        part_lo(2)
                        part_lo(3)
                    if left == 3:
                        head_lo(0)
                    if left == 2:
                        head_lo(1)
                        head_lo(2)
                    if left == 1:
                        head_lo(3)

                pipeline(nc.vector, dve_period)

                for n in range(KT):
                    ahead(lo_of, dve, l, P_OUT + 2 * n)
                    ahead(lo_of, dve, l, P_OUT + 2 * n + 1)
                    dve.wait_ge(s_panel.sem, s_panel.until(l, P_OUT + 2 * n + 2))
                    v.tensor_tensor(xT[:, n, :], pair(n % 4), xT[:, n, :], ALU.add).then_inc(s_res.sem, 1)
                    if 0 < n < KT - 1:
                        add_squares(l, KT + n - 1)

                for k in range(KT):
                    if k in (3, 5):
                        add_squares(l, 2 * KT - 2 + k // 4)
                    operand_lo(l, KT + k, col(C_G2 + k))
                norm(l, 1)

                def conv(n, j, up, k):
                    c = up * FT + j
                    w0, w2 = ((col(C_FW[0] + c), col(C_FW[2] + c)) if isinstance(c, int) else
                              (pc[:, bass.ds(C_FW[0] + c, 1)], pc[:, bass.ds(C_FW[2] + c, 1)]))
                    dve.wait_ge(s_mr.sem, s_mr.until(l, k))
                    dve.wait_ge(s_m1.sem, s_m1.until(l, k))
                    taps(l, (tg, tu)[up][n // 2], pair((n + 2) % 4), w0, w2, s_m2, s_m3, k)

                def up_chunk(chunk, p0, i=None):
                    for n in range(2 * CH):
                        ahead(lo_of, dve, l, p0 + 2 * n, i)
                        ahead(lo_of, dve, l, p0 + 2 * n + 1, i)
                        if i is None and n == 0:
                            dve.wait_ge(s_nr.sem, s_nr.until(l, 2))
                        at = p0 + 2 * n + 2 if i is None else p0 + 2 * n + 2 + i * STEP
                        dve.wait_ge(s_panel.sem, s_panel.until(l, at))
                        scale_tile((n + 2) % 4, s_mr)
                        conv(n, chunk * CH + n // 2, n % 2, 2 * CH * chunk + n + 1)

                def product(k, j):
                    dve.wait_ge(s_sg.sem, s_sg.until(l, k + 1))
                    v.tensor_tensor(tg[j][:, :], tg[j][:, :], tu[j][:, :], ALU.mult).then_inc(s_mm.sem, 1)

                def product_lo(k, j):
                    dve.wait_ge(s_mh.sem, s_mh.until(l, k + 1))
                    v.tensor_tensor(mlo[:, j, :], tg[j][:, :], mhi[:, j, :].bitcast(F32),
                                    ALU.subtract).then_inc(s_ml.sem, 1)

                def add_down(chunk, n, p, i=None):
                    if n % 4 == 3:
                        dve.wait_ge(s_panel.sem, s_panel.until(l, p + 1 if i is None else p + 1 + i * STEP))
                    else:
                        dve.wait_ge(s_dr.sem, s_dr.until(l, chunk * (KT - 2) + (n // 4) * 3 + n % 4 + 1))
                    v.tensor_tensor(xT[:, n, :], pair(psum_down(n)), xT[:, n, :], ALU.add).then_inc(s_dn.sem, 1)

                up_chunk(0, P_UP0)
                product(0, 0)
                product(1, 1)
                product_lo(0, 0)
                product_lo(1, 1)
                with nc.vector.Fori(0, NCH - 1) as i:
                    up_chunk(i + 1, P_BODY, i)
                    product((i + 1) * CH, 0)
                    for h in range(2):
                        for q in range(CH):
                            ahead(lo_of, dve, l, P_BODY + UPN + h * CH + q, i)
                        for n in range(4 * h, 4 * h + 4):
                            add_down(i, n, P_BODY + UPN + h * CH + CH - 1, i)
                        if h == 0:
                            product((i + 1) * CH + 1, 1)
                    product_lo((i + 1) * CH, 0)
                    product_lo((i + 1) * CH + 1, 1)
                for h in range(2):
                    for q in range(CH):
                        ahead(lo_of, dve, l, P_DN + h * CH + q)
                    for n in range(4 * h, 4 * h + 4):
                        add_down(NCH - 1, n, P_DN + h * CH + CH - 1)
                        if n:
                            operand_lo(l + 1, n - 1, col(C_GN + n - 1))
                operand_lo(l + 1, KT - 1, col(C_GN + KT - 1))

            dve.wait_ge(s_fg, 16)
            for b in range(TB):
                dve.wait_ge(s_frs, b + 1)
                if b >= ROWS:
                    dve.wait_ge(s_out[b % ROWS], 16 * (b // ROWS))
                v.scalar_tensor_tensor(out=o_row[b % ROWS][:, :], in0=pair(b % 4), scalar=rs[:, b:b + 1],
                                       in1=fg_row[:, :], op0=ALU.mult, op1=ALU.mult).then_inc(s_row, 1)

        @block.tensor
        def _(pe):
            t = nc.tensor

            def k_tile(outs, w_hi, w_lo, xhi, xlo, first, last):
                for h in range(2):
                    t.matmul(outs[h], w_hi, xhi[:, h * HALF:(h + 1) * HALF], start=first, stop=False)
                for h in range(2):
                    t.matmul(outs[h], w_hi, xlo[:, h * HALF:(h + 1) * HALF], start=False, stop=False)
                for h in range(2):
                    mm = t.matmul(outs[h], w_lo, xhi[:, h * HALF:(h + 1) * HALF], start=False, stop=last)
                return mm

            def halves(k, rows=P):
                return [ps[0:rows, 2 * k + h, :] for h in range(2)]

            def k_tile_of(l, p, k, kt, i=None, gap=1):
                h, j = kt // 4, kt % 4
                q = p + gap * h
                n = q % RING
                if j == 0:
                    at = q if i is None else q + i * STEP
                    pe.wait_ge(s_split.sem, s_split.until(l, at + 1))
                mm = k_tile(halves(k), whi[n][:, j * P:(j + 1) * P], wlo[n][:, j * P:(j + 1) * P],
                            ahi[:, kt, :], alo[:, kt, :], kt == 0, kt == KT - 1)
                if j == 3:
                    mm.then_inc(s_panel.sem, 1)

            def feature_tile(l, p, k, i=None, ready=None, between=()):
                for kt in range(KT):
                    if ready is not None:
                        pe.wait_ge(ready[0].sem, ready[0].until(l, ready[1] + kt + 1))
                    for at, work in between:
                        if at == kt:
                            work()
                    k_tile_of(l, p, k, kt, i)

            def square_sums(l, n):
                pe.wait_ge(s_acc.sem, s_acc.until(l, n * KT + KT))
                for b in range(TB):
                    mm = t.matmul(ps[:, (6, 0)[n], b:b + 1], acc[:, b * P:(b + 1) * P], ones[:, 0:1],
                                  start=True, stop=True)
                mm.then_inc(s_nsum.sem, 1)

            def rs_broadcast(l, n):
                pe.wait_ge(s_dg.sem, s_dg.until(l, n + 1))
                for b in range(TB):
                    mm = t.matmul(pair((3, 1)[n])[:, b * P:(b + 1) * P], ones[:, :], sq[:, b * P:(b + 1) * P],
                                  start=True, stop=True)
                mm.then_inc(s_nb.sem, 1)

            pe.sem_inc(s_panel.sem, s_panel.credit)
            pe.sem_inc(s_qt.sem, s_qt.credit)
            pe.sem_inc(s_s.sem, s_s.credit)
            pe.sem_inc(s_wt.sem, s_wt.credit)
            pe.sem_inc(s_o.sem, s_o.credit)
            pe.wait_ge(s_const, 12)
            pe.wait_ge(s_posf, 1)
            t.transpose(ps[:, 1, 0:TB], pos_f[:, :], ident[0:TB, 0:TB]).then_inc(s_post, 1)
            for b in range(TB):
                if b % 2 == 0:
                    pe.wait_ge(s_xin[b // 2], 16)
                if b >= 3:
                    pe.wait_ge((s_xa, s_xv)[(b - 3) % 2], (b - 3) // 2 + 1)
                for k in range(KT):
                    mm = t.transpose(pair(1 + b % 3)[:, k * P:(k + 1) * P], xin[:, b, k * P:(k + 1) * P], ident[:, :])
                mm.then_inc(s_xt0, 1)
            pe.wait_ge(s_setup, N_SETUP)
            at = 0
            for tile, n in zip(stage, [4 * FT] * L + [2 * FT * L] * 2 + [L * (C_LAM - C_G1)]):
                mm = t.transpose(ps[:, 0, at:at + n], tile[0:n, :], ident[0:n, 0:n])
                at += n
            mm.then_inc(s_pset, 1)

            with nc.tensor.Fori(0, L) as l:
                pe.wait_ge(s_dn.sem, s_dn.until(l, -1))
                for kt in range(KT):
                    pe.wait_ge(s_hl.sem, s_hl.until(l, kt + 1))
                    p, j = DT_PANELS[kt // 2], kt % 2
                    if kt == KT - 1:
                        square_sums(l, 0)
                    if j == 0:
                        pe.wait_ge(s_split.sem, s_split.until(l, p + 1))
                    mm = k_tile(halves(2, 8), whi[p % RING][:, 8 * j:8 * j + 8], wlo[p % RING][:, 8 * j:8 * j + 8],
                                ahi[:, kt, :], alo[:, kt, :], kt == 0, kt == KT - 1)
                    if j:
                        mm.then_inc(s_panel.sem, 1)
                    k_tile_of(l, F0_PANELS[0], f_pair(0), kt, gap=F0_PANELS[1] - F0_PANELS[0])

                free = [(s_c3, n + 1) for n in range(XBCT)] + [(s_z, n + 1) for n in range(XT)]
                for i in range(SCT):
                    free += [(s_sa, i + 1), (s_sc, 4 * i + 4)]
                free += [(s_sc, 4 * SCT + i + 1) for i in range(SCT)]

                def pair_free(n):
                    if n == 2:
                        pe.wait_ge(s_dtp.sem, s_dtp.until(l, 1))
                    elif n == 3:
                        pe.wait_ge(s_dv.sem, s_dv.until(l, 1))
                    elif n >= 4:
                        reader, count = free[n - 2]
                        pe.wait_ge(reader.sem, reader.until(l, count))

                def mixed(first, last):
                    for u in range(first, last):
                        n, kt = MIXED + u // KT, u % KT
                        if kt == 0:
                            pair_free(n)
                        k_tile_of(l, P_F + 2 * n, f_pair(n), kt)

                a8 = DT_A
                for n in range(XBCT):
                    if n:
                        pair_free(n)
                        feature_tile(l, P_F + 2 * n, f_pair(n),
                                     between=[(2, lambda: rs_broadcast(l, 0))] if n == 1 else ())
                    if n == 1:
                        pe.wait_ge(s_dtp.sem, s_dtp.until(l, 1))
                        pe.wait_ge(s_nr.sem, s_nr.until(l, 1))
                        for b in range(TB):
                            mm = t.matmul(ps[:, 6, b * 8:b * 8 + 8], dtT[:, b * P:(b + 1) * P], ident[0:8, 0:8],
                                          start=True, stop=True)
                        mm.then_inc(s_dtt.sem, 1)
                    if n == 4:
                        pe.wait_ge(s_dv.sem, s_dv.until(l, STEP_A))
                        pe.wait_ge(s_c3.sem, s_c3.until(l, 2))
                        q4 = DW // 2
                        t.matmul(ps[:, 3, 0:q4], upto[:, :], a8[:, :, 0:NH], start=True, stop=True)
                        t.matmul(ps[:, 3, q4:DW], downto[:, :], a8[:, :, NH:2 * NH], start=True, stop=True)
                        t.matmul(ps[:, 3, DW:2 * DW], ones[:, :], a8[:, :, :], start=True, stop=True).then_inc(s_cum.sem, 1)

                pe.wait_ge(s_xs.sem, s_xs.until(l, 4))

                def chunk_tokens(c):
                    if c >= 2:
                        pe.wait_ge(s_tok.sem, s_tok.until(l, c - 1))
                    for n in range(4):
                        mm = t.transpose(ps[:, c % 2, n * P:(n + 1) * P], xbc[:, n, c * P:(c + 1) * P], ident[:, :])
                    mm.then_inc(s_t1.sem, 1)

                def chunk_states(c):
                    pe.wait_ge(s_xw.sem, s_xw.until(l, c + 1))
                    if c == 0:
                        pe.wait_ge(s_da.sem, s_da.until(l, 3))
                    if c >= 2:
                        pe.wait_ge(s_st.sem, s_st.until(l, c - 1))
                    for g in range(XT):
                        mm = t.matmul(ps[:, 2 + c % 2, 2 * g * P:2 * (g + 1) * P],
                                      xb_tok[c % 2][:, SSDW + g * P:SSDW + (g + 1) * P],
                                      xw[c % 2][:, :, 2 * g:2 * g + 2, :], start=True, stop=True)
                    mm.then_inc(s_stp.sem, 1)

                chunk_tokens(0)
                chunk_tokens(1)
                for h in range(2 * XT):
                    n = XBCT + h // 2
                    if h % 2 == 0:
                        pair_free(n)
                    for kt in range(4 * (h % 2), 4 * (h % 2) + 4):
                        k_tile_of(l, P_F + 2 * n, f_pair(n), kt)
                    for c in (2 * h, 2 * h + 1):
                        chunk_states(c)
                        if c + 2 < TB:
                            chunk_tokens(c + 2)

                def decay_rows(c):
                    if c == 0:
                        pe.wait_ge(s_tok.sem, s_tok.until(l, TB))
                    else:
                        pe.wait_ge(s_seg.sem, s_seg.until(l, c))
                        pe.wait_ge(s_er.sem, s_er.until(l, c))
                    for n in range(2 * NH):
                        mm = t.matmul(pair(0)[:, n * P:(n + 1) * P], a8[:, c, n:n + 1].broadcast_to([P, P]),
                                      (upto if n < NH else downto)[:, :], start=True, stop=True)
                    mm.then_inc(s_rows.sem, 1)

                def gram(c):
                    cols = slice(c * P, (c + 1) * P)
                    if c == 0:
                        pe.wait_ge(s_xs.sem, s_xs.until(l, XBCT))
                        pe.wait_ge(s_st.sem, s_st.until(l, TB))
                    else:
                        pe.wait_ge(s_xt.sem, s_xt.until(l, c))
                        pe.wait_ge(s_m.sem, s_m.until(l, c))
                    for g in range(XT):
                        t.matmul(ps[:, 2, g * P:(g + 1) * P], xbc[:, 2 + g, cols], xbc[:, 4 + g, cols],
                                 start=True, stop=True)
                    for g in range(XT):
                        mm = t.transpose(ps[:, 2, (2 + g) * P:(3 + g) * P], xbc[:, g, cols], ident[:, :])
                    mm.then_inc(s_gx.sem, 1)

                decay_rows(0)
                gram(0)
                for c in range(TB):
                    mixed(sum(SLOTS[:c]), sum(SLOTS[:c + 1]))
                    if c + 1 < TB:
                        decay_rows(c + 1)
                        gram(c + 1)
                    pe.wait_ge(s_m.sem, s_m.until(l, c + 1))
                    pe.wait_ge(s_xt.sem, s_xt.until(l, c + 1))
                    pe.wait_ge(s_cs.sem, s_cs.until(l, c + 1))
                    if c == 0:
                        pe.wait_ge(s_chain.sem, s_chain.until(l, 2 * (TB - 2)))
                    else:
                        pe.wait_ge(s_yd.sem, s_yd.until(l, c))
                    for h in range(NH):
                        g, hf = h // 2, h % 2
                        o = ps[64 * hf:64 * hf + 64, 3, g * P:(g + 1) * P]
                        cols = slice(hf * DQK, (hf + 1) * DQK)
                        parts = [(xb_tok[c % 2][:, h * DQK:(h + 1) * DQK], seg[:, 0, h, :])]
                        if c > 0:
                            parts.append((st[:, c - 1, g, 0, cols], erow[:, 0, h, :]))
                        if c < TB - 1:
                            parts.append((st[:, c + 1, g, 1, cols], erow[:, 1, h, :]))
                        for n, (w, m) in enumerate(parts):
                            mm = t.matmul(o, w, m, start=n == 0, stop=n == len(parts) - 1)
                    mm.then_inc(s_y.sem, 1)

                def ssd_square_sums():
                    pe.wait_ge(s_ysq.sem, s_ysq.until(l, 1))
                    pe.wait_ge(s_ge.sem, s_ge.until(l, TB))
                    for n in range(XT * TB):
                        mm = t.matmul(ps[:, 7, n:n + 1], sqs[:, n // TB, (n % TB) * P:(n % TB + 1) * P],
                                      ones[:, 0:1], start=True, stop=True)
                    mm.then_inc(s_ysum.sem, 1)

                def ssd_broadcast():
                    pe.wait_ge(s_ydg.sem, s_ydg.until(l, 1))
                    pe.wait_ge(s_ge.sem, s_ge.until(l, 2 * TB))
                    for g in range(XT):
                        for b in range(TB):
                            cols = slice(b * P, (b + 1) * P)
                            mm = t.matmul(pair(2 + g)[:, cols], ones[:, :], sqs[:, g, cols], start=True, stop=True)
                        mm.then_inc(s_ynb.sem, 1)

                for n in range(len(GROUPS)):
                    for k in range(KT):
                        p = P_G + KT * n + k
                        pe.wait_ge(s_split.sem, s_split.until(l, p + 1))
                        if n == 1 and k == 0:
                            ssd_square_sums()
                        for b in range(TB):
                            if n == 0 and k == 0 and b == 3:
                                pe.wait_ge(s_yd.sem, s_yd.until(l, TB))
                            if n == 0 and k == 0 and b == 4:
                                pe.wait_ge(s_sc.sem, s_sc.until(l, 5 * SCT - 1))
                            if n == 0 and k == 0 and b == 6:
                                pe.wait_ge(s_sc.sem, s_sc.until(l, 5 * SCT))
                            if n and k == 0:
                                pe.wait_ge(s_ge.sem, s_ge.until(l, TB * (n - 1) + b + 1))
                            if n == 1 and k == 0 and b == 7:
                                pe.wait_ge(s_yms.sem, s_yms.until(l, 1))
                            if n == 2 and k == 0 and b == 4:
                                ssd_broadcast()
                            if n == 2 and k == 0 and b % 2 == 0 and b >= 4:
                                pe.wait_ge(s_yn.sem, s_yn.until(l, b // 2 - 1))
                            xh, xl = ahi[:, k, b * P:(b + 1) * P], alo[:, k, b * P:(b + 1) * P]
                            w_h, w_l = whi[p % RING][:, :], wlo[p % RING][:, :]
                            t.matmul(ps[:, b, :], xh, w_h, start=k == 0, stop=False)
                            t.matmul(ps[:, b, :], xh, w_l, start=False, stop=False)
                            mm = t.matmul(ps[:, b, :], xl, w_h, start=False, stop=k == KT - 1)
                            if k == KT - 1 and b < TB - 1:
                                mm.then_inc(s_g.sem, 1)
                        mm.then_inc(s_panel.sem, 1)
                def q_turn(hd, j):
                    it = hd * TB + j
                    if isinstance(hd, int) and it == 0:
                        pe.wait_ge(s_ge.sem, s_ge.until(l, TB * 2 + 7))
                    pe.wait_ge(s_ql.sem, s_ql.until(l, it + 1))
                    pe.wait_ge(s_qs.sem, s_qs.until(l, it))
                    for n in range(4):
                        mm = t.transpose(ps[:, 6, n * P:(n + 1) * P].bitcast(F32R),
                                         qsp[j % 2][:, n // 2, n % 2, :, :].rearrange("p a d -> p (a d)"),
                                         identr[:, :])
                    mm.then_inc(s_qt.sem, 1)

                for b in range(TB):
                    pe.wait_ge(s_kl.sem, s_kl.until(l, b + 1))
                    if b < 3:
                        pe.wait_ge(s_ge.sem, s_ge.until(l, TB * 2 + 2 * b + 2))
                    else:
                        pe.wait_ge(s_ks.sem, s_ks.until(l, b - 2))
                    for h in range(HC):
                        mm = t.transpose(pair(b % 3)[:, h * P:(h + 1) * P].bitcast(F32R),
                                         ksp[b % 2][:, h, :, :].rearrange("p a d -> p (a d)"), identr[:, :])
                    mm.then_inc(s_kt.sem, 1)
                    if b == 4:
                        q_turn(0, 0)
                q_turn(0, 1)

                def scores(hd, j):
                    it = hd * TB + j
                    if isinstance(hd, int) and it == 0:
                        pe.wait_ge(s_ks.sem, s_ks.until(l, TB))
                    pe.wait_ge(s_qs.sem, s_qs.until(l, it + 1))
                    for c in range(2):
                        pe.wait_ge(s_e.sem, s_e.until(l, 2 * it - 1 + c))
                        for part in range(2):
                            for h in range(2):
                                mm = t.matmul(half(c, h), qT[j % 2][:, c, part, :],
                                              kst[:, bass.ds(hd * 2 + (j // TB * 2 + c), 1), h * HALF:(h + 1) * HALF]
                                              .rearrange("p a n -> p (a n)"), start=part == 0, stop=part == 1)
                        mm.then_inc(s_s.sem, 1)

                def turn_weights(hd, j):
                    it = hd * TB + j
                    pe.wait_ge(s_w.sem, s_w.until(l, it + 1))
                    pe.wait_ge(s_we.sem, s_we.until(l, it))
                    for b in range(TB):
                        mm = t.transpose(pair(2)[:, b * P:(b + 1) * P], W[j % 2][:, b * P:(b + 1) * P], ident[:, :])
                    mm.then_inc(s_wt.sem, 1)

                def weigh_v(hd, j):
                    it = hd * TB + j
                    pe.wait_ge(s_we.sem, s_we.until(l, it + 1))
                    pe.wait_ge(s_os.sem, s_os.until(l, it))
                    for b in range(TB):
                        mm = t.matmul(ps[:, 7, 0:DV], WT[j % 2][:, b, :],
                                      v_tok[:, b, bass.ds(hd * DV + j // TB * DV, DV)],
                                      start=b == 0, stop=b == TB - 1)
                    mm.then_inc(s_o.sem, 1)

                def pe_period(hd, p):
                    if exists(hd, p + 1):
                        scores(hd, p + 1)
                    if exists(hd, p - 1):
                        turn_weights(hd, p - 1)
                    if exists(hd, p - 2):
                        weigh_v(hd, p - 2)
                    if exists(hd, p + 3):
                        q_turn(hd, p + 3)

                def turn_head(h):
                    pe.wait_ge(s_hn.sem, s_hn.until(l, (h + 1) * TB))
                    if h < 2:
                        pe.wait_ge(s_e.sem, s_e.until(l, 2 * ITS - 1 + h))
                    else:
                        pe.wait_ge(s_we.sem, s_we.until(l, ITS))
                    for b in range(TB):
                        mm = t.transpose(pair(h)[:, b * P:(b + 1) * P], o_tok[:, b, h * DV:(h + 1) * DV], ident[:, :])
                    mm.then_inc(s_ot.sem, 1)

                def tail_period(hd, p):
                    pe_period(hd, p)
                    left = ITS + 3 - (hd * TB + p) if isinstance(hd, int) else None
                    if left in (4, 3, 2):
                        turn_head(4 - left)

                pipeline(nc.tensor, tail_period)

                for n in range(KT):
                    if n == 0:
                        pe.wait_ge(s_yl.sem, s_yl.until(l, HEADS + 1))
                    if n >= 4:
                        pe.wait_ge(s_res.sem, s_res.until(l, n - 3))
                    for m, kt in enumerate(OUT_ORDER):
                        p = P_OUT + 2 * n + m // 4
                        if m % 4 == 0:
                            pe.wait_ge(s_split.sem, s_split.until(l, p + 1))
                        if n == 0 and m == 4:
                            turn_head(3)
                        if n == 0:
                            pe.wait_ge(s_yl.sem, s_yl.until(l, m + 1))
                        j = kt % 4
                        mm = k_tile(halves(n % 4), whi[p % RING][:, j * P:(j + 1) * P], wlo[p % RING][:, j * P:(j + 1) * P],
                                    ahi[:, kt, :], alo[:, kt, :], m == 0, m == KT - 1)
                        if m % 4 == 3:
                            mm.then_inc(s_panel.sem, 1)

                def down_half(chunk, h, p, i=None):
                    for q in range(CH):
                        pe.wait_ge(s_split.sem, s_split.until(l, p + q + 1 if i is None else p + q + 1 + i * STEP))
                    for n in range(4):
                        m = 4 * h + n
                        if m < 4:
                            if i is None:
                                pe.wait_ge(s_dn.sem, s_dn.until(l, (NCH - 1) * KT - 4 + m + 1))
                            else:
                                pe.wait_ge(s_m3.sem, s_m3.until(l, 2 * CH * (i + 1) + n + 1))
                        else:
                            pe.wait_ge(s_dn.sem, s_dn.until(l, chunk * KT + m - 4 + 1))
                        for q in range(CH):
                            r = (p + q) % RING
                            mm = k_tile(halves(psum_down(m)), whi[r][:, n * P:(n + 1) * P],
                                        wlo[r][:, n * P:(n + 1) * P], mhi[:, q, :], mlo[:, q, :], q == 0, q == CH - 1)
                            if n == 3:
                                mm.then_inc(s_panel.sem, 1)
                        if n < 3:
                            mm.then_inc(s_dr.sem, 1)

                for n in range(2 * CH):
                    between = [[(6, lambda: square_sums(l, 1))], [(2, lambda: rs_broadcast(l, 1))]]
                    if n == 3:
                        pe.wait_ge(s_nr.sem, s_nr.until(l, 2))
                    feature_tile(l, P_UP0 + 2 * n, (n + 2) % 4, ready=(s_hl, KT) if n == 0 else None,
                                 between=between[n] if n < 2 else ())
                with nc.tensor.Fori(0, NCH - 1) as i:
                    for n in range(2 * CH):
                        pe.wait_ge(s_m3.sem, s_m3.until(l, 2 * CH * i + n + 1))
                        pe.wait_ge(s_dn.sem, s_dn.until(l, KT * i - 4 + n + 1))
                        feature_tile(l, P_BODY + 2 * n, (n + 2) % 4, i)
                    pe.wait_ge(s_ml.sem, s_ml.until(l, CH * (i + 1)))
                    for h in range(2):
                        down_half(i, h, P_BODY + UPN + h * CH, i)
                pe.wait_ge(s_ml.sem, s_ml.until(l, FT))
                for h in range(2):
                    down_half(NCH - 1, h, P_DN + h * CH)

            pe.wait_ge(s_dn.sem, s_dn.until(L, 0))
            for b in range(TB):
                if b >= 4:
                    pe.wait_ge(s_row, b - 3)
                for k in range(KT):
                    mm = t.transpose(pair(b % 4)[:, k * P:(k + 1) * P], xT[:, k, b * P:(b + 1) * P], ident[:, :])
                mm.then_inc(s_fin, 1)


_INS = ["x", "positions", "norm_mix_g", "w_in", "lam_q1", "lam_k1", "lam_q2", "lam_k2", "subln_g", "sc_conv_w",
        "ssd_conv_w", "ssd_conv_b", "ssd_dt_bias", "ssd_a_log", "ssd_d", "ssd_norm_g", "w_out",
        "norm_ffn_g", "w_up", "ffn_conv_w", "ffn_conv_b", "w_down", "final_norm_g"]


def kernel(**inputs):
    import numpy as np
    import concourse.bacc as bacc
    from concourse.bass_utils import run_bass_kernel_spmd

    nc = bacc.Bacc("TRN2", target_bir_lowering=False, num_devices=1)
    arrays, args = {}, []
    for name in _INS:
        a = np.ascontiguousarray(inputs[name])
        arrays[f"in_{name}"] = a
        args.append(nc.dram_tensor(f"in_{name}", a.shape, mybir.dt.from_np(a.dtype), kind="ExternalInput").ap())
    out = nc.dram_tensor("out", inputs["x"].shape, F32, kind="ExternalOutput").ap()
    build(nc, *args, out)
    r = run_bass_kernel_spmd(nc, [arrays], core_ids=[0])
    return r.results[0]["out"]
```
